# Optimizing a Trainium2 kernel written in Bass

```python
import math
import jax, jax.numpy as jnp
from jax import lax
import numpy as np

D_MODEL = 1024
BATCH = 1
SEQ = 256
DEPTH = 2

N_META = 16
Q_BLOCK = 128
ROPE_THETA = 500000.0
RMS_EPS = 1e-6

MLA_HEADS = 8
MLA_NOPE = 64
MLA_ROPE = 32
MLA_V = 64
MLA_Q_RANK = 384
MLA_KV_RANK = 256

DIFF_HEADS = 4
DIFF_DH = 64
DIFF_ROPE = DIFF_DH // 4

D_FF = -(-(8 * D_MODEL) // (3 * 256)) * 256

COL_Q_LAT = MLA_Q_RANK
COL_KV_LAT = MLA_KV_RANK
COL_K_ROPE = MLA_ROPE
COL_DIFF_Q = DIFF_HEADS * 2 * DIFF_DH
COL_DIFF_K = DIFF_HEADS * 2 * DIFF_DH
COL_DIFF_V = DIFF_HEADS * 2 * DIFF_DH
COL_GATE_A = D_MODEL
COL_GATE_B = D_MODEL
IN_COLS = COL_Q_LAT + COL_KV_LAT + COL_K_ROPE + COL_DIFF_Q + COL_DIFF_K + COL_DIFF_V + COL_GATE_A + COL_GATE_B
SPLIT_POINTS = (
    COL_Q_LAT,
    COL_Q_LAT + COL_KV_LAT,
    COL_Q_LAT + COL_KV_LAT + COL_K_ROPE,
    COL_Q_LAT + COL_KV_LAT + COL_K_ROPE + COL_DIFF_Q,
    COL_Q_LAT + COL_KV_LAT + COL_K_ROPE + COL_DIFF_Q + COL_DIFF_K,
    COL_Q_LAT + COL_KV_LAT + COL_K_ROPE + COL_DIFF_Q + COL_DIFF_K + COL_DIFF_V,
    COL_Q_LAT + COL_KV_LAT + COL_K_ROPE + COL_DIFF_Q + COL_DIFF_K + COL_DIFF_V + COL_GATE_A,
)

kernel_name = "hybrid_mla_diffattn_gated_block"

def rms_norm(x, gain):
    xf = x.astype(jnp.float32)
    y = xf * lax.rsqrt(jnp.mean(xf * xf, axis=-1, keepdims=True) + RMS_EPS)
    return y.astype(x.dtype) * gain.astype(x.dtype)

def rope_tables(length, rot_dim, dtype):
    inv = ROPE_THETA ** (-jnp.arange(0, rot_dim, 2, dtype=jnp.float32) / rot_dim)
    ang = jnp.arange(length, dtype=jnp.float32)[:, None] * inv[None, :]
    return jnp.cos(ang).astype(dtype), jnp.sin(ang).astype(dtype)

def apply_rope(t, cos, sin):
    half = cos.shape[-1]
    c = cos[None, :, None, :]
    s = sin[None, :, None, :]
    t1, t2, rest = t[..., :half], t[..., half:2 * half], t[..., 2 * half:]
    return jnp.concatenate([t1 * c - t2 * s, t2 * c + t1 * s, rest], axis=-1)

def to_query_blocks(t):
    b, l, h, d = t.shape
    return t.reshape(b, l // Q_BLOCK, Q_BLOCK, h, d).transpose(1, 0, 3, 2, 4)

def from_query_blocks(t):
    nb, b, h, qb, d = t.shape
    return t.transpose(1, 0, 3, 2, 4).reshape(b, nb * qb, h * d)

def causal_probs(qb, k, start, scale):
    s = jnp.einsum('bhqd,bhkd->bhqk', qb, k).astype(jnp.float32) * scale
    qpos = start + jnp.arange(qb.shape[2])
    kpos = jnp.arange(k.shape[2])
    mask = kpos[None, :] <= qpos[:, None]
    s = jnp.where(mask[None, None], s, -jnp.inf)
    return jax.nn.softmax(s, axis=-1)

def causal_attention(q, k, v, scale):
    kt = k.transpose(0, 2, 1, 3)
    vt = v.transpose(0, 2, 1, 3)
    qblocks = to_query_blocks(q)
    starts = jnp.arange(qblocks.shape[0]) * Q_BLOCK

    def one_block(args):
        qb, start = args
        p = causal_probs(qb, kt, start, scale)
        return jnp.einsum('bhqk,bhkd->bhqd', p.astype(vt.dtype), vt)

    return from_query_blocks(lax.map(one_block, (qblocks, starts)))

def causal_diff_attention(q1, k1, q2, k2, v, lam, scale):
    k1t = k1.transpose(0, 2, 1, 3)
    k2t = k2.transpose(0, 2, 1, 3)
    vt = v.transpose(0, 2, 1, 3)
    q1b = to_query_blocks(q1)
    q2b = to_query_blocks(q2)
    starts = jnp.arange(q1b.shape[0]) * Q_BLOCK

    def one_block(args):
        qa, qc, start = args
        p = causal_probs(qa, k1t, start, scale) - lam * causal_probs(qc, k2t, start, scale)
        return jnp.einsum('bhqk,bhkd->bhqd', p.astype(vt.dtype), vt)

    out = lax.map(one_block, (q1b, q2b, starts))
    nb, b, h, qb, d = out.shape
    return out.transpose(1, 0, 3, 2, 4).reshape(b, nb * qb, h, d)

def setup_inputs(seed: int = 0) -> dict:
    key = jax.random.key(seed)
    ks = jax.random.split(key, 20)
    f32 = jnp.float32

    def w(k, shape, fan_in):
        return jax.random.normal(k, shape, f32) * (fan_in ** -0.5)

    def gain(k, shape):
        return 1.0 + 0.02 * jax.random.normal(k, shape, f32)

    return {
        "x": jax.random.normal(ks[0], (BATCH, SEQ, D_MODEL), f32),
        "meta_tokens": jax.random.normal(ks[1], (N_META, D_MODEL), f32),
        "norm_mix_pre": gain(ks[2], (DEPTH, D_MODEL)),
        "norm_mix_post": gain(ks[3], (DEPTH, D_MODEL)),
        "norm_ffn_pre": gain(ks[4], (DEPTH, D_MODEL)),
        "norm_ffn_post": gain(ks[5], (DEPTH, D_MODEL)),
        "w_in": w(ks[6], (DEPTH, D_MODEL, IN_COLS), D_MODEL),
        "mla_q_norm": gain(ks[7], (DEPTH, MLA_Q_RANK)),
        "mla_kv_norm": gain(ks[8], (DEPTH, MLA_KV_RANK)),
        "mla_w_uq": w(ks[9], (DEPTH, MLA_Q_RANK, MLA_HEADS * (MLA_NOPE + MLA_ROPE)), MLA_Q_RANK),
        "mla_w_ukv": w(ks[10], (DEPTH, MLA_KV_RANK, MLA_HEADS * (MLA_NOPE + MLA_V)), MLA_KV_RANK),
        "w_o_mla": w(ks[11], (DEPTH, MLA_HEADS * MLA_V, D_MODEL), MLA_HEADS * MLA_V),
        "diff_lambda": 0.1 * jax.random.normal(ks[12], (DEPTH, 4, DIFF_DH), f32),
        "diff_subln": gain(ks[13], (DEPTH, 2 * DIFF_DH)),
        "w_o_diff": w(ks[14], (DEPTH, DIFF_HEADS * 2 * DIFF_DH, D_MODEL), DIFF_HEADS * 2 * DIFF_DH),
        "w_out": w(ks[15], (DEPTH, D_MODEL, D_MODEL), D_MODEL),
        "w_gate_up": w(ks[16], (DEPTH, D_MODEL, 2 * D_FF), D_MODEL),
        "w_down": w(ks[17], (DEPTH, D_FF, D_MODEL), D_FF),
    }

def reference(x, meta_tokens, norm_mix_pre, norm_mix_post, norm_ffn_pre, norm_ffn_post,
              w_in, mla_q_norm, mla_kv_norm, mla_w_uq, mla_w_ukv, w_o_mla,
              diff_lambda, diff_subln, w_o_diff, w_out, w_gate_up, w_down):
    dt = x.dtype
    b, s, d = x.shape
    length = s + N_META
    l_pad = -(-length // Q_BLOCK) * Q_BLOCK
    meta = jnp.broadcast_to(meta_tokens.astype(dt)[None], (b, N_META, d))
    r = jnp.concatenate([meta, x, jnp.zeros((b, l_pad - length, d), dt)], axis=1)

    cos_mla, sin_mla = rope_tables(l_pad, MLA_ROPE, dt)
    cos_dif, sin_dif = rope_tables(l_pad, DIFF_ROPE, dt)
    mla_scale = 1.0 / math.sqrt(MLA_NOPE + MLA_ROPE)
    diff_scale = 1.0 / math.sqrt(DIFF_DH)

    for layer in range(DEPTH):
        h = rms_norm(r, norm_mix_pre[layer])
        proj = h @ w_in[layer].astype(dt)
        (q_lat, kv_lat, k_pe, dq, dk, dv, g_a, g_b) = jnp.split(proj, SPLIT_POINTS, axis=-1)

        c_q = rms_norm(q_lat, mla_q_norm[layer])
        qa = (c_q @ mla_w_uq[layer].astype(dt)).reshape(b, l_pad, MLA_HEADS, MLA_NOPE + MLA_ROPE)
        qa = jnp.concatenate([qa[..., :MLA_NOPE], apply_rope(qa[..., MLA_NOPE:], cos_mla, sin_mla)], axis=-1)
        c_kv = rms_norm(kv_lat, mla_kv_norm[layer])
        kva = (c_kv @ mla_w_ukv[layer].astype(dt)).reshape(b, l_pad, MLA_HEADS, MLA_NOPE + MLA_V)
        k_nope, va = kva[..., :MLA_NOPE], kva[..., MLA_NOPE:]
        k_rope = apply_rope(k_pe[:, :, None, :], cos_mla, sin_mla)
        ka = jnp.concatenate(
            [k_nope, jnp.broadcast_to(k_rope, (b, l_pad, MLA_HEADS, MLA_ROPE))], axis=-1)
        out_a = causal_attention(qa, ka, va, mla_scale) @ w_o_mla[layer].astype(dt)

        qd = apply_rope(dq.reshape(b, l_pad, DIFF_HEADS * 2, DIFF_DH), cos_dif, sin_dif)
        kd = apply_rope(dk.reshape(b, l_pad, DIFF_HEADS * 2, DIFF_DH), cos_dif, sin_dif)
        qd = qd.reshape(b, l_pad, DIFF_HEADS, 2, DIFF_DH)
        kd = kd.reshape(b, l_pad, DIFF_HEADS, 2, DIFF_DH)
        vd = dv.reshape(b, l_pad, DIFF_HEADS, 2 * DIFF_DH)
        lam_init = 0.8 - 0.6 * math.exp(-0.3 * layer)
        lp = diff_lambda[layer].astype(jnp.float32)
        lam = (jnp.exp(jnp.sum(lp[0] * lp[1])) - jnp.exp(jnp.sum(lp[2] * lp[3])) + lam_init)
        od = causal_diff_attention(qd[..., 0, :], kd[..., 0, :], qd[..., 1, :], kd[..., 1, :],
                                   vd, lam, diff_scale)
        od = rms_norm(od, diff_subln[layer]) * (1.0 - lam_init)
        out_b = od.reshape(b, l_pad, DIFF_HEADS * 2 * DIFF_DH) @ w_o_diff[layer].astype(dt)

        mix = (jax.nn.sigmoid(g_a) * out_a + jax.nn.sigmoid(g_b) * out_b) @ w_out[layer].astype(dt)
        r = r + rms_norm(mix, norm_mix_post[layer])

        h = rms_norm(r, norm_ffn_pre[layer])
        gu = h @ w_gate_up[layer].astype(dt)
        ff = (jax.nn.silu(gu[..., :D_FF]) * gu[..., D_FF:]) @ w_down[layer].astype(dt)
        r = r + rms_norm(ff, norm_ffn_post[layer])

    return r[:, N_META:N_META + s, :]


_drawn_inputs = setup_inputs


def setup_inputs(seed=0):
    import zlib

    import numpy as np

    out = dict(_drawn_inputs(seed))
    spreads = {}
    factors = {'norm_ffn_post': 3.379,
     'mla_q_norm': 8.0,
     'mla_kv_norm': 7.302,
     'diff_lambda': 8.0,
     'diff_subln': 7.788}
    for name, (base, spread) in spreads.items():
        noise = np.random.default_rng([zlib.crc32(name.encode()), seed]).standard_normal(out[name].shape)
        drawn = base * np.exp(spread * noise) if base else spread * noise
        out[name] = __import__('jax').numpy.asarray(drawn.astype(out[name].dtype))
    for name, factor in factors.items():
        out[name] = (out[name] * factor).astype(out[name].dtype)
    return out
```

```python
import concourse.bass as bass
from concourse import mybir
from contextlib import ExitStack
import math
import numpy as np

P = 128
D_MODEL, SEQ, DEPTH, N_META = 1024, 256, 2, 16
TOK = SEQ + N_META
MLA_HEADS, NOPE, ROPE, MLA_V = 8, 64, 32, 64
Q_RANK, KV_RANK = 384, 256
DIFF_HEADS, DIFF_DH = 4, 64
DIFF_ROPE = DIFF_DH // 4
D_FF = -(-(8 * D_MODEL) // (3 * 256)) * 256
THETA, EPS = 500000.0, 1e-6
MLA_SCALE = 1.0 / math.sqrt(NOPE + ROPE)
DIFF_SCALE = 1.0 / math.sqrt(DIFF_DH)
LAM_INIT = [0.8 - 0.6 * math.exp(-0.3 * l) for l in range(DEPTH)]
MASKED = -1e30

KC = D_MODEL // P
QC, KVC = Q_RANK // P, KV_RANK // P
FC = D_FF // P
HW = NOPE + ROPE
DOWN_SPLIT = (6, 6, 5, 5)
SLOT = 8 * P
RING, RAW, AHEAD, BANKS = 8, 4, 6, 4
CH = [(0, 16), (16, 144), (144, 272)]
UNITS = DIFF_HEADS + MLA_HEADS
NORMS = 7
PRE_MIX, NQ, NKV, NDIFF, POST_MIX, PRE_FFN, POST_FFN = range(NORMS)
CHUNKS = {PRE_MIX: KC, NQ: QC, NKV: KVC, POST_MIX: KC, PRE_FFN: KC, POST_FFN: KC}

STAGES = [("lat", 6, [1] * 6), ("dq", 4, [1] * 4), ("dk", 4, [1] * 4), ("dv", 4, [1] * 4),
          ("uq", 3, [3, 3, 2]), ("ukv", 2, [4, 4]), ("gate", 16, [1] * 16),
          ("oa", 4, [2] * 4), ("ob", 4, [2] * 4), ("out", 8, [1] * 8),
          ("gu", 2 * FC, [1] * (2 * FC)), ("down", 4 * KC, [0, 0, 0, 1] * KC)]

O_DQ = Q_RANK + KV_RANK + ROPE
O_DK = O_DQ + DIFF_HEADS * 2 * DIFF_DH
O_DV = O_DK + DIFF_HEADS * 2 * DIFF_DH
O_G = O_DV + DIFF_HEADS * 2 * DIFF_DH
G_MIXPRE, G_MIXPOST, G_FFNPRE, G_FFNPOST, G_Q, G_KV, G_SUB = 0, 8, 16, 24, 32, 35, 37
GAINS = 38
C_ID, C_MASK, C_MASKM, C_COSD, C_SIND, C_COSM, C_SINM = 0, 128, 256, 512, 784, 1056, 1328
C_ALL = 1600


class Plan:

    def __init__(self):
        self.slot0, self.tile0 = {}, {}
        self.slot_done, self.tile_done = [], []
        done = 0
        for l in range(DEPTH):
            for name, slots, ends in STAGES:
                self.slot0[l, name], self.tile0[l, name] = len(self.slot_done), len(self.tile_done)
                for e in ends:
                    for _ in range(e):
                        done += 1
                        self.tile_done.append(done)
                    if e == 0:
                        done += 1
                    self.slot_done.append(done)
        self.slots = len(self.slot_done)
        self.sq0, self.add0 = {}, {}
        s = a = 0
        for l in range(DEPTH):
            for k in range(NORMS):
                if k in CHUNKS:
                    self.sq0[l * NORMS + k], self.add0[l * NORMS + k] = s, a
                    s, a = s + CHUNKS[k], a + CHUNKS[k] - 1


def build_trunk(nc: bass.Bass, xT, weights, gains, lam_in, consts, outT):
    f32, f32r, bf16 = mybir.dt.float32, mybir.dt.float32r, mybir.dt.bfloat16
    ALU, ACT, AX = mybir.AluOpType, mybir.ActivationFunctionType, mybir.AxisListType
    plan = Plan()
    ctx = ExitStack()
    with ctx:
        base = -(-nc.sbuf_base // 32) * 32

        def place(at, tensors):
            made = []
            for name, shape, dt in tensors:
                size = int(np.prod(shape[1:])) * (2 if dt == bf16 else 4)
                made.append(nc.alloc_sbuf_tensor_at(name, shape, dt, offset=at))
                at += -(-size // 32) * 32
            return made, at

        (w_raw, w_hi, w_lo, r, hh, hl, y, rstd_h, rstd_p, acc, sq, rc_d, rs_d, rc_q, rs_q,
         cst, identb, maskb, gain, small, lat, tres), at = place(base, [
            ("w_raw", [P, RAW, SLOT], f32), ("w_hi", [P, RING, SLOT], f32r), ("w_lo", [P, RING, SLOT], f32r),
            ("resid", [P, KC, TOK], f32), ("h_hi", [P, KC, TOK], f32r), ("h_lo", [P, KC, TOK], f32r),
            ("y", [P, KC, TOK], f32),
            ("rstd_h", [P, TOK], f32), ("rstd_p", [P, TOK], f32), ("acc", [P, 2, TOK], f32), ("sq", [P, 2, TOK], f32),
            ("rcos_d", [P, TOK], f32), ("rsin_d", [P, TOK], f32), ("rcos_q", [P, TOK], f32),
            ("rsin_q", [P, TOK], f32),
            ("cst", [P, C_ALL - 512 + 128], f32), ("identb", [P, P], bf16), ("maskb", [P, P], bf16),
            ("gain", [P, DEPTH, GAINS], f32), ("small", [P, 96], f32), ("lat", [P, 2, TOK], f32),
            ("tres", [P, TOK], f32)])
        lat_tmp_at = at - 4 * 3 * TOK
        rstd_q, rstd_kv = rstd_p, tres
        att0 = at
        (q_t, dqk, v_tok, gates), at = place(att0, [
            ("q_t", [P, MLA_HEADS, TOK], f32), ("dqk_t", [P, 8, TOK], f32),
            ("v_tok", [P, 3, 1024], f32), ("gates", [P, 16, TOK], f32)])
        gates_last_at = at - 4 * TOK
        k_t = nc.alloc_sbuf_tensor_at("k_t", [P, MLA_HEADS, TOK], f32, offset=base + 4 * (RAW + 2 * RING) * SLOT + 3 * 4 * KC * TOK)
        lat_at = at
        (lat_hi, lat_lo), at = place(lat_at, [("lat_hi", [P, QC + KVC, TOK], f32r), ("lat_lo", [P, QC + KVC, TOK], f32r)])
        (e_t, pt0, pt1, pt2, ptm), _ = place(lat_at, [("e_t", [P, 2, 416], f32), ("pt0", [16, 2, TOK], f32), ("pt1", [P, 2, 256], f32),
                                                      ("pt2", [P, 2, 128], f32), ("ptm", [16, UNITS, 16], f32)])
        assert _ <= at
        v_at = at
        (kv_t, dv_t), at = place(v_at, [("kv_t", [P, MLA_HEADS, TOK], f32), ("dv_t", [P, DIFF_HEADS, TOK], f32)])
        (am_hi, am_lo, od), _ = place(v_at, [("am_hi", [P, 4, TOK], f32r), ("am_lo", [P, 4, TOK], f32r),
                                             ("od", [P, DIFF_HEADS, TOK], f32)])
        assert _ <= at
        (b_t,), at = place(at, [("b_t", [P, 4, TOK], f32)])
        (pm,), _ = place(lat_tmp_at, [("pm", [16, 3, 256], f32)])
        (maskmb,), _ = place(gates_last_at, [("maskmb", [16, 256], bf16)])
        krope = dv_t[:, 0, :]
        dqk_at = att0 + 4 * MLA_HEADS * TOK
        (od_hi, od_lo), _ = place(dqk_at, [("od_hi", [P, 4, TOK], f32r), ("od_lo", [P, 4, TOK], f32r)])
        (ff_hi, ff_lo, gbuf, ubuf, sbuf_, pbuf), _ = place(att0, [
            ("ff_hi", [P, FC, TOK], f32r), ("ff_lo", [P, FC, TOK], f32r), ("gbuf", [P, 2, TOK], f32),
            ("ubuf", [P, 2, TOK], f32), ("sbuf", [P, 2, TOK], f32), ("pbuf", [P, 2, TOK], f32)])
        assert _ <= nc.sbuf_usable_end
        ident = cst[:, 0:P]
        cos_d, sin_d, cos_m, sin_m = (cst[:, P + TOK * i:P + TOK * (i + 1)] for i in range(4))
        stage = y[:, 0:2, 0:256]
        eps = small[:, 0:1]
        ones = small[:, 1:2]
        neglam = small[:, 2:4]
        lam_e = small[:, 4:8]
        std = [small[:, 8 + 12 * i:20 + 12 * i] for i in range(2)]
        rec = [small[:, 32 + 12 * i:44 + 12 * i] for i in range(2)]
        mx = [small[:, 56 + 4 * i:60 + 4 * i] for i in range(2)]
        sm = [small[:, 64 + 4 * i:68 + 4 * i] for i in range(2)]
        mxm = small[0:16, 72:88]
        lamp = small[:, 92:96]
        idle = small[:, 90:91]
        gsub = small[:, 88:90]
        lam_raw = b_t[:, 0:2, 0:256]
        ps = [ctx.enter_context(nc.psum_tensor(f"bank{i}", [P, 512], f32)) for i in range(8)]

        def sem(name):
            return ctx.enter_context(nc.semaphore(name))

        raw_in = [sem(f"raw_in{i}") for i in range(RAW)]
        x_in, cst_in, out_done = sem("x_in"), sem("cst_in"), sem("out_done")
        hi_ready, lo_ready = sem("hi_ready"), sem("lo_ready")
        pe_done, tile_free = sem("pe_done"), sem("tile_free")
        dve_step, act_step = sem("dve_step"), sem("act_step")
        const_ready, lam_ready, lam_exp = sem("const_ready"), sem("lam_ready"), sem("lam_exp")
        sq_ready, sq_added = sem("sq_ready"), sem("sq_added")
        norm_sum, norm_std, norm_rec, norm_bc, norm_ready = (sem(n) for n in ("norm_sum", "norm_std", "norm_rec", "norm_bc", "norm_ready"))
        r_ready, h_hi, h_lo = sem("r_ready"), sem("h_hi_ready"), sem("h_lo_ready")
        lat_ready_hi, lat_ready_lo = sem("lat_hi_ready"), sem("lat_lo_ready")
        rope_in, rope_done, kr_ready, k_copied = sem("rope_in"), sem("rope_done"), sem("kr_ready"), sem("k_copied")
        v_ready, v_copied = sem("v_ready"), sem("v_copied")
        meta_half, meta_scores, meta_shift, meta_exp, meta_probs, meta_pt, meta_copied = (sem(n) for n in ("meta_half", "meta_scores", "meta_shift", "meta_exp", "meta_probs", "meta_pt", "meta_copied"))
        scores_ready, negmax_ready, exp_ready, probs_ready = (sem(n) for n in ("scores_ready", "negmax_ready", "exp_ready", "probs_ready"))
        pt_ready, pt_copied, pv_ready, out_hi, out_copied = (sem(n) for n in ("pt_ready", "pt_copied", "pv_ready", "out_hi", "out_copied"))
        od_squared, od_ready, od_hi_ready, od_lo_ready = sem("od_squared"), sem("od_ready"), sem("od_hi_ready"), sem("od_lo_ready")
        sig_ready, mix_ready, mix_hi, mix_lo = sem("sig_ready"), sem("mix_ready"), sem("mix_hi"), sem("mix_lo")
        silu_done, ff_prod, ff_hi_ready, ff_lo_ready = sem("silu_done"), sem("ff_prod"), sem("ff_hi_ready"), sem("ff_lo_ready")

        block = ctx.enter_context(nc.Block())

        def T0(l):
            return 0 if l < DEPTH - 1 else N_META

        def boundary_from(b):
            return N_META if b >= 2 * DEPTH - 1 else 0

        @block.sync
        def _(sp):
            def load(n, width, i=None, per=0):
                m = n if i is None else n + per * i
                if n >= RAW:
                    sp.wait_ge(lo_ready, m - RAW + 1)
                src = weights[bass.ds(m * P, P), 0:width] if i is not None else weights[m * P:(m + 1) * P, 0:width]
                sp.dma_start(w_raw[:, n % RAW, 0:width], src).then_inc(raw_in[n % RAW], 16)

            sp.dma_start(r[:, :, :], xT.rearrange("p (k t) -> p k t", k=KC)).then_inc(x_in, 16)
            for n in range(RAW):
                load(n, SLOT)
            sp.dma_start(gain[:, :, :], gains.rearrange("p (l g) -> p l g", l=DEPTH)).then_inc(cst_in, 16)
            sp.dma_start(cst[:, 0:P], consts[:, 0:P]).then_inc(cst_in, 16)
            sp.dma_start(stage, consts[:, P:512 + P].rearrange("p (a b) -> p a b", a=2)[:, :, 0:256]).then_inc(cst_in, 16)
            sp.dma_start(cst[:, P:], consts[:, 512:C_ALL]).then_inc(cst_in, 16)
            sp.dma_start(lam_raw, lam_in.rearrange("p (l g) -> p l g", l=DEPTH)).then_inc(cst_in, 16)
            first = RAW
            for l in range(DEPTH):
                d0 = plan.slot0[l, "down"]
                whole = (d0 - first) // RING
                with sp.Fori(0, whole) as i:
                    for j in range(RING):
                        load(first + j, SLOT, i, RING)
                for n in range(first + whole * RING, d0):
                    load(n, SLOT)
                with sp.Fori(0, KC // 2) as i:
                    for j in range(RING):
                        load(d0 + j, DOWN_SPLIT[j % 4] * P, i, RING)
                first = d0 + 4 * KC
            for c in range(KC):
                sp.wait_ge(r_ready, KC * (2 * DEPTH - 1) + c + 1)
                sp.dma_start(outT[:, c * SEQ:(c + 1) * SEQ], r[:, c, N_META:TOK]).then_inc(out_done, 16)
            sp.wait_ge(out_done, 16 * KC)

        @block.scalar
        def _(act):
            def split(n, i=None, per=0):
                if n >= plan.slots:
                    return
                u, v = (0, 0) if i is None else (per * i, 4 * per * i)
                act.wait_ge(raw_in[n % RAW], 16 * (n // RAW + 1) + v)
                if n >= RING:
                    act.wait_ge(pe_done, plan.slot_done[n - RING] + u)
                act.activation(w_hi[:, n % RING, :], w_raw[:, n % RAW, :], ACT.Copy).then_inc(hi_ready, 1)

            def square(K, c, src, t0):
                if c == 0:
                    if K >= 2:
                        act.wait_ge(norm_sum, K - 1)
                    dst = acc[:, K % 2, t0:]
                else:
                    a = plan.add0[K] + c - 1
                    if a >= 2:
                        act.wait_ge(sq_added, a - 1)
                    dst = sq[:, a % 2, t0:]
                act.activation(dst, src, ACT.Square).then_inc(sq_ready, 1)

            def root(K, sums, n, width):
                act.wait_ge(norm_sum, K + 1)
                if K >= 2:
                    act.wait_ge(norm_rec, K - 1)
                act.activation(std[K % 2][:, 0:n], sums, ACT.Sqrt, bias=eps, scale=1.0 / width).then_inc(norm_std, 1)

            def boundary(b, K, g, l):
                t0 = boundary_from(b)
                for c in range(KC):
                    if b == 0:
                        if c == 0:
                            act.wait_ge(x_in, 16)
                            act.wait_ge(cst_in, 16 * 5)
                    else:
                        act.wait_ge(r_ready, KC * (b - 1) + c + 1)
                    act.activation(hh[:, c, t0:], r[:, c, t0:], ACT.Copy, scale=gain[:, l, g + c:g + c + 1]).then_inc(h_hi, 1)
                    square(K, c, r[:, c, t0:], t0)

            act.wait_ge(lam_ready, 1)
            act.activation(lam_e, lamp, ACT.Exp).then_inc(lam_exp, 1)
            act.wait_ge(const_ready, 1)
            boundary(0, 0, G_MIXPRE, 0)
            for n in range(AHEAD):
                split(n)
            for l in range(DEPTH):
                t0 = T0(l)
                K0 = NORMS * l
                S = lambda name: plan.slot0[l, name]
                TL = lambda name: plan.tile0[l, name]
                root(K0 + PRE_MIX, ps[7][:, 0:3], 3, D_MODEL)
                for i in range(6):
                    split(S("lat") + i + AHEAD)
                    if i == 5:
                        continue
                    c0 = t0 if i < QC else 0
                    act.wait_ge(tile_free, TL("lat") + i + 1)
                    if l and i == 0:
                        act.wait_ge(pt_ready, UNITS * l)
                    act.activation(lat_hi[:, i, c0:], lat[:, i % 2, c0:], ACT.Copy,
                                   scale=gain[:, l, G_Q + i:G_Q + i + 1]).then_inc(lat_ready_hi, 1)
                    if i < QC:
                        square(K0 + NQ, i, lat[:, i % 2, c0:], c0)
                    else:
                        square(K0 + NKV, i - QC, lat[:, i % 2, c0:], c0)
                root(K0 + NQ, ps[7][:, 0:3], 3, Q_RANK)
                root(K0 + NKV, ps[6][:, 0:3], 3, KV_RANK)
                act.wait_ge(rope_done, 5 * l + 1)
                act.activation(k_t[64:96, :, :], krope[64:96, None, :].to_broadcast([32, MLA_HEADS, TOK]), ACT.Copy).then_inc(kr_ready, 1)
                for n in range(S("dq"), S("ukv")):
                    split(n + AHEAD)
                for i in range(2):
                    split(S("ukv") + i + AHEAD)
                    for h in range(4 * i, 4 * i + 4):
                        act.wait_ge(tile_free, TL("ukv") + h + 1)
                        act.activation(k_t[0:64, h, :], kv_t[0:64, h, :], ACT.Copy).then_inc(k_copied, 1)

                def v_evac(g):
                    act.wait_ge(v_ready, 3 * l + g + 1)
                    for c, (a, b) in enumerate(CH):
                        n = b - a
                        if g == 0:
                            act.activation(v_tok[0:n, c, 0:512], ps[4 + c][0:n, :], ACT.Copy).then_inc(v_copied, 1)
                        else:
                            act.activation(v_tok[0:n, c, 512 + 256 * (g - 1):768 + 256 * (g - 1)].rearrange("p (a b) -> p a b", a=4),
                                           ps[4 + c][0:n, :].rearrange("p (a b) -> p a b", a=4)[:, :, 64:128], ACT.Copy).then_inc(v_copied, 1)

                def exps(u):
                    U = UNITS * l + u
                    act.wait_ge(negmax_ready, U + 1)
                    maps = [(4, 0, 0), (5, 1, 2)] if u < DIFF_HEADS else [(4 + u % 2, u % 2, 0)]
                    scale = DIFF_SCALE if u < DIFF_HEADS else MLA_SCALE
                    for bank, e, s in maps:
                        for part, (a, b) in enumerate(((0, 144), (144, 416))):
                            last = act.activation(e_t[:, e, a:b], ps[bank][:, a:b], ACT.Exp, bias=mx[u % 2][:, s + part:s + part + 1],
                                                  scale=scale, accum_out=sm[u % 2][:, s + part:s + part + 1])
                    last.then_inc(exp_ready, 1)

                def hi_out(u):
                    if u < DIFF_HEADS:
                        return
                    h = u - DIFF_HEADS
                    o = 64 * (h % 2)
                    act.wait_ge(pv_ready, UNITS * l + u + 1)
                    act.activation(am_hi[o:o + 64, h // 2, t0:], ps[7][o:o + 64, t0:TOK], ACT.Copy).then_inc(out_hi, 1)

                def pt_evac(u):
                    act.wait_ge(pt_ready, UNITS * l + u + 1)
                    b = u % 2
                    if l == 0:
                        if u == 0:
                            act.wait_ge(meta_copied, 1)
                        act.activation(pt0[0:16, b, 0:16], ptm[:, u, :], ACT.Copy)
                    act.activation(pt0[0:16, b, 16:], ps[6][0:16, 0:256], ACT.Copy)
                    act.activation(pt1[:, b, :], ps[6][:, 256:512], ACT.Copy)
                    act.activation(pt2[:, b, :], ps[7][:, 384:512], ACT.Copy).then_inc(pt_copied, 1)

                for i in range(16):
                    u = i - 4
                    if u < 0:
                        split(S("gate") + i + AHEAD)
                        if i < 3:
                            v_evac(i)
                        elif l == 0:
                            act.wait_ge(meta_shift, 1)
                            act.activation(pm[:, 1, 0:128], pm[:, 0, 0:128], ACT.Exp, scale=MLA_SCALE)
                            act.activation(pm[:, 1, 128:256], pm[:, 0, 128:256], ACT.Exp, scale=DIFF_SCALE).then_inc(meta_exp, 1)
                            act.wait_ge(meta_pt, 1)
                            act.activation(ptm[:, :, :], ps[5][0:16, 0:16 * UNITS].rearrange("p (a b) -> p a b", a=UNITS), ACT.Copy).then_inc(meta_copied, 1)
                        continue
                    exps(u)
                    if u >= 1:
                        hi_out(u - 1)
                    split(S("gate") + i + AHEAD)
                    pt_evac(u)
                    if u == 5:
                        act.wait_ge(out_copied, UNITS * l + 4)
                        act.activation(b_t[:, :, t0:], od[:, :, t0:], ACT.Square).then_inc(od_squared, 1)
                hi_out(UNITS - 1)
                K = K0 + NDIFF
                root(K, ps[4][:, 0:12], 12, 2 * DIFF_DH)
                for half in range(2):
                    act.wait_ge(tile_free, TL("gate") + 8 * half + 8)
                    act.activation(gates[:, 8 * half:8 * half + 8, t0:], gates[:, 8 * half:8 * half + 8, t0:], ACT.Sigmoid).then_inc(sig_ready, 1)
                    if half == 0:
                        for d in range(DIFF_HEADS):
                            act.wait_ge(od_ready, DIFF_HEADS * l + d + 1)
                            act.activation(od_hi[:, d, t0:], od[:, d, t0:], ACT.Copy, scale=gsub[:, l:l + 1]).then_inc(od_hi_ready, 1)
                for i in range(4):
                    split(S("oa") + i + AHEAD)

                def mix_split(m):
                    act.wait_ge(mix_ready, KC * l + m + 1)
                    act.activation(hh[:, m, t0:], gates[:, 8 + m, t0:], ACT.Copy).then_inc(mix_hi, 1)

                for i in range(4):
                    split(S("ob") + i + AHEAD)
                    mix_split(2 * i)
                    mix_split(2 * i + 1)
                for m in range(KC):
                    split(S("out") + m + AHEAD)
                    act.wait_ge(tile_free, TL("out") + m + 1)
                    square(K0 + POST_MIX, m, y[:, m, t0:], t0)
                root(K0 + POST_MIX, ps[7][:, 0:3], 3, D_MODEL)
                boundary(2 * l + 1, K0 + PRE_FFN, G_FFNPRE, l)
                root(K0 + PRE_FFN, ps[7][:, 0:3], 3, D_MODEL)

                def pair(j, i=None, first=False):
                    s, t = S("gu") + 2 * j, TL("gu") + 2 * j
                    per = 0 if i is None else RING
                    o = 0 if i is None else per * i
                    p = 0 if i is None else 4 * i
                    J = FC * l + j
                    split(s + AHEAD, i, per)
                    if not first:
                        hi_ff(j - 1, i)
                    act.wait_ge(tile_free, t + 1 + o)
                    if J >= 2:
                        act.wait_ge(ff_prod, J - 1 + p)
                    act.activation(sbuf_[:, j % 2, t0:], gbuf[:, j % 2, t0:], ACT.Silu).then_inc(silu_done, 1)
                    split(s + 1 + AHEAD, i, per)

                def hi_ff(j, i=None):
                    p = 0 if i is None else 4 * i
                    act.wait_ge(ff_prod, FC * l + j + 1 + p)
                    dst = ff_hi[:, j, t0:] if i is None else ff_hi[:, bass.ds(4 * i + j, 1), t0:]
                    src = pbuf[:, j % 2, t0:] if i is None else pbuf[:, j % 2:j % 2 + 1, t0:]
                    act.activation(dst, src, ACT.Copy).then_inc(ff_hi_ready, 1)

                pair(0, first=True)
                with act.Fori(0, 5) as i:
                    for j in range(1, 5):
                        pair(j, i)
                pair(21)
                hi_ff(21)
                TD, SD = TL("down"), S("down")

                def down(m, i=None):
                    per = 0 if i is None else RING
                    for j in range(4):
                        split(SD + 4 * m + j + AHEAD, i, per)
                for m in range(KC):
                    down(m)
                    act.wait_ge(tile_free, TD + m + 1)
                    square(K0 + POST_FFN, m, y[:, m, t0:], t0)
                root(K0 + POST_FFN, ps[7][:, 0:3], 3, D_MODEL)
                if l < DEPTH - 1:
                    boundary(2 * l + 2, K0 + NORMS + PRE_MIX, G_MIXPRE, l + 1)

        @block.gpsimd
        def _(pool):
            def sum_squares(K, t0):
                for c in range(1, CHUNKS[K % NORMS]):
                    a = plan.add0[K] + c - 1
                    pool.wait_ge(sq_ready, plan.sq0[K] + c + 1)
                    if c > 1:
                        pool.wait_ge(sq_added, a)
                    pool.tensor_tensor(acc[:, K % 2, t0:], acc[:, K % 2, t0:], sq[:, a % 2, t0:], ALU.add).then_inc(sq_added, 1)

            def rope_add(l, i, dst, src):
                if i == 0:
                    pool.wait_ge(sq_added, plan.add0[NORMS * l + NKV] + KVC - 1)
                else:
                    pool.wait_ge(rope_done, 5 * l + i)
                pool.wait_ge(rope_in, 5 * l + i + 1)
                pool.tensor_tensor(dst, dst, src, ALU.add).then_inc(rope_done, 1)

            sum_squares(0, 0)
            for l in range(DEPTH):
                t0, K0 = T0(l), NORMS * l
                sum_squares(K0 + NQ, t0)
                sum_squares(K0 + NKV, 0)
                rope_add(l, 0, krope[64:96, :], b_t[64:96, 0, :])
                rope_add(l, 1, dqk[:, 0:4, t0:], b_t[:, 0:4, t0:])
                rope_add(l, 2, dqk[:, 4:8, :], b_t[:, 0:4, :])
                rope_add(l, 3, q_t[64:96, 0:4, t0:], b_t[64:96, 0:4, t0:])
                rope_add(l, 4, q_t[64:96, 4:8, t0:], b_t[64:96, 0:4, t0:])
                pool.wait_ge(rope_done, 5 * (l + 1))
                sum_squares(K0 + POST_MIX, t0)
                sum_squares(K0 + PRE_FFN, t0)

                def product(j, i=None):
                    o = 0 if i is None else RING * i
                    p = 0 if i is None else 4 * i
                    J = FC * l + j
                    pool.wait_ge(silu_done, J + 1 + p)
                    pool.wait_ge(tile_free, plan.tile0[l, "gu"] + 2 * j + 2 + o)
                    if J >= 2:
                        pool.wait_ge(ff_lo_ready, J - 1 + p)
                    pool.tensor_tensor(pbuf[:, j % 2, t0:], sbuf_[:, j % 2, t0:], ubuf[:, j % 2, t0:], ALU.mult).then_inc(ff_prod, 1)

                product(0)
                with pool.Fori(0, 5) as i:
                    for j in range(1, 5):
                        product(j, i)
                product(21)
                sum_squares(K0 + POST_FFN, t0)
                if l < DEPTH - 1:
                    sum_squares(K0 + NORMS + PRE_MIX, 0)

        @block.vector
        def _(dve):
            steps = [0]

            def step(ins):
                steps[0] += 1
                ins.then_inc(dve_step, 1)
                return steps[0]

            def after(v):
                dve.wait_ge(dve_step, v)

            def split(n, i=None, per=0):
                if n >= plan.slots:
                    return
                u = 0 if i is None else per * i
                dve.wait_ge(hi_ready, n + 1 + u)
                dve.tensor_tensor(w_lo[:, n % RING, :], w_raw[:, n % RAW, :], w_hi[:, n % RING, :].bitcast(f32),
                                  ALU.subtract).then_inc(lo_ready, 1)

            def recip(K, n=3):
                dve.wait_ge(norm_std, K + 1)
                if K >= 2:
                    dve.wait_ge(norm_bc, K - 1)
                dve.reciprocal(rec[K % 2][:, 0:n], std[K % 2][:, 0:n]).then_inc(norm_rec, 1)

            def take(K, bank, dst, t0):
                dve.wait_ge(norm_bc, K + 1)
                dve.tensor_copy(dst[:, t0:], ps[bank][:, 64 + t0:64 + TOK]).then_inc(norm_ready, 1)

            def evac(t, dst, factor, rows=slice(0, P), t0=0):
                dve.wait_ge(pe_done, plan.tile_done[t])
                dve.tensor_tensor(dst, ps[t % BANKS][rows, t0:TOK], factor, ALU.mult).then_inc(tile_free, 1)

            def lo_part(b, c, g, l, t0):
                dve.wait_ge(h_hi, KC * b + c + 1)
                dve.scalar_tensor_tensor(out=hl[:, c, t0:], in0=r[:, c, t0:], scalar=gain[:, l, g + c:g + c + 1],
                                         in1=hh[:, c, t0:].bitcast(f32), op0=ALU.mult, op1=ALU.subtract).then_inc(h_lo, 1)

            def residual(b, gp, lp, t0):
                last = b == 2 * DEPTH
                for c in range(KC):
                    if c:
                        dve.wait_ge(r_ready, KC * (b - 1) + c)
                    v = step(dve.scalar_tensor_tensor(out=tres[:, t0:], in0=y[:, c, t0:], scalar=gain[:, lp, gp + c:gp + c + 1],
                                                      in1=rstd_p[:, t0:], op0=ALU.mult, op1=ALU.mult))
                    after(v)
                    dve.tensor_tensor(r[:, c, t0:], r[:, c, t0:], tres[:, t0:], ALU.add).then_inc(r_ready, 1)
                    if not last and c:
                        lo_part(b, c - 1, *nxt(b), t0)
                if not last:
                    lo_part(b, KC - 1, *nxt(b), t0)

            def nxt(b):
                return (G_FFNPRE, b // 2) if b % 2 else (G_MIXPRE, b // 2)

            dve.memset(eps, EPS).then_inc(const_ready, 1)
            dve.memset(ones, 1.0)
            dve.wait_ge(cst_in, 16 * 5)
            dve.tensor_copy(identb[:, :], ident)
            dve.tensor_copy(maskb[:, :], stage[:, 0, 0:P])
            dve.tensor_copy(maskmb[:, 0:128], stage[0:16, 0, 128:256])
            dve.tensor_copy(maskmb[:, 128:256], stage[0:16, 1, 0:128])
            for l in range(DEPTH):
                for j in range(2):
                    o = 128 * j
                    v = step(dve.tensor_tensor(tres[:, 0:64], lam_raw[:, l, o:o + 64], lam_raw[:, l, o + 64:o + 128], ALU.mult))
                    after(v)
                    v = step(dve.reduce_sum(lamp[:, 2 * l + j:2 * l + j + 1], tres[:, 0:64], AX.X))
                    after(v)
            dve.memset(idle, 0.0).then_inc(lam_ready, 1)
            dve.wait_ge(lam_exp, 1)
            for l in range(DEPTH):
                v = step(dve.tensor_tensor(neglam[:, l:l + 1], lam_e[:, 2 * l + 1:2 * l + 2], lam_e[:, 2 * l:2 * l + 1], ALU.subtract))
                after(v)
                step(dve.tensor_scalar(neglam[:, l:l + 1], neglam[:, l:l + 1], LAM_INIT[l], None, ALU.subtract))
                step(dve.tensor_scalar(gsub[:, l:l + 1], gain[:, l, G_SUB:G_SUB + 1], 1.0 - LAM_INIT[l], None, ALU.mult))
            after(steps[0])
            dve.memset(idle, 0.0).then_inc(const_ready, 1)

            for c in range(KC):
                lo_part(0, c, G_MIXPRE, 0, 0)
            for n in range(AHEAD):
                split(n)

            for l in range(DEPTH):
                t0, K0 = T0(l), NORMS * l
                S = lambda name: plan.slot0[l, name]
                TL = lambda name: plan.tile0[l, name]
                recip(K0 + PRE_MIX)
                take(K0 + PRE_MIX, 7, rstd_h, 0)
                dve.wait_ge(norm_ready, K0 + PRE_MIX + 1)
                for dst, tab in ((rc_d, cos_d), (rs_d, sin_d)):
                    v = step(dve.tensor_tensor(dst[:, :], rstd_h[:, :], tab, ALU.mult))
                for dst, tab in ((rc_q, cos_m), (rs_q, sin_m)):
                    v = step(dve.tensor_tensor(dst[64:96, :], rstd_h[64:96, :], tab[64:96, :], ALU.mult))
                after(v)
                for i in range(5):
                    split(S("lat") + i + AHEAD)
                    c0 = t0 if i < QC else 0
                    if i >= 2 or l:
                        K = K0 + NQ if i < QC else K0 + NKV
                        prev = plan.sq0[K0 + NQ] + i - 1 if i >= 2 else plan.sq0[K0 - NORMS + NKV] + 2
                        dve.wait_ge(sq_ready, prev)
                    evac(TL("lat") + i, lat[:, i % 2, c0:], rstd_h[:, c0:], t0=c0)
                    dve.wait_ge(lat_ready_hi, 5 * l + i + 1)
                    dve.scalar_tensor_tensor(out=lat_lo[:, i, c0:], in0=lat[:, i % 2, c0:], scalar=gain[:, l, G_Q + i:G_Q + i + 1],
                                             in1=lat_hi[:, i, c0:].bitcast(f32), op0=ALU.mult, op1=ALU.subtract).then_inc(lat_ready_lo, 1)
                split(S("lat") + 5 + AHEAD)
                t = TL("lat") + 5
                swap_m = [(i + 16) % 32 for i in range(32)]
                swap_d = [(i + 8) % 16 if i < 16 else i for i in range(32)]
                dve.wait_ge(pe_done, plan.tile_done[t])
                v = step(dve.tensor_tensor(b_t[64:96, 0, :], ps[t % BANKS][64:96, 0:TOK], rs_q[64:96, :], ALU.mult))
                evac(t, krope[64:96, :], rc_q[64:96, :], rows=slice(64, 96))
                after(v)
                dve.wait_ge(tile_free, t + 1)
                dve.stream_shuffle(b_t[64:96, 0, :], b_t[64:96, 0, :], swap_m).then_inc(rope_in, 1)
                recip(K0 + NQ)
                recip(K0 + NKV)
                for st, base_c, rope_i in (("dq", 0, 1), ("dk", 4, 2)):
                    c0 = t0 if st == "dq" else 0
                    dve.wait_ge(rope_done, 5 * l + rope_i)
                    for i in range(4):
                        split(S(st) + i + AHEAD)
                        t = TL(st) + i
                        dve.wait_ge(pe_done, plan.tile_done[t])
                        v = step(dve.tensor_tensor(b_t[:, i, c0:], ps[t % BANKS][:, c0:TOK], rs_d[:, c0:], ALU.mult))
                        evac(t, dqk[:, base_c + i, c0:], rc_d[:, c0:], t0=c0)
                        if st == "dq" and i == 1:
                            take(K0 + NQ, 7, rstd_q, t0)
                            take(K0 + NKV, 6, rstd_kv, 0)
                            dve.wait_ge(norm_ready, K0 + NKV + 1)
                            v = step(dve.tensor_tensor(rc_q[0:96, t0:], rstd_q[0:96, t0:], cos_m[0:96, t0:], ALU.mult))
                            v = step(dve.tensor_tensor(rs_q[64:96, t0:], rstd_q[64:96, t0:], sin_m[64:96, t0:], ALU.mult))
                    after(v)
                    dve.wait_ge(tile_free, TL(st) + 4)
                    dve.stream_shuffle(b_t[:, :, c0:], b_t[:, :, c0:], swap_d).then_inc(rope_in, 1)
                dve.wait_ge(kr_ready, l + 1)
                for i in range(4):
                    split(S("dv") + i + AHEAD)
                    evac(TL("dv") + i, dv_t[:, i, :], rstd_h[:, :])
                for h in range(MLA_HEADS):
                    if h % 3 == 0:
                        split(S("uq") + h // 3 + AHEAD)
                    if h % 4 == 0:
                        dve.wait_ge(rope_done, 5 * l + 3 + h // 4)
                    t = TL("uq") + h
                    dve.wait_ge(pe_done, plan.tile_done[t])
                    v = step(dve.tensor_tensor(b_t[64:96, h % 4, t0:], ps[t % BANKS][64:96, t0:TOK], rs_q[64:96, t0:], ALU.mult))
                    evac(t, q_t[0:96, h, t0:], rc_q[0:96, t0:], rows=slice(0, 96), t0=t0)
                    if h % 4 == 3:
                        after(v)
                        dve.wait_ge(tile_free, t + 1)
                        dve.stream_shuffle(b_t[64:96, :, t0:], b_t[64:96, :, t0:], swap_m).then_inc(rope_in, 1)
                for h in range(MLA_HEADS):
                    if h % 4 == 0:
                        split(S("ukv") + h // 4 + AHEAD)
                    evac(TL("ukv") + h, kv_t[:, h, :], rstd_kv[:, :])

                def gate(i):
                    evac(TL("gate") + i, gates[:, i, t0:], rstd_h[:, t0:], t0=t0)

                def unit_maps(u):
                    return [(4, 0, 0), (5, 1, 2)] if u < DIFF_HEADS else [(4 + u % 2, u % 2, 0)]

                def negmax(u):
                    U = UNITS * l + u
                    dve.wait_ge(scores_ready, U + 1)
                    if U >= 2:
                        dve.wait_ge(probs_ready, U - 1)
                    for bank, e, s in unit_maps(u):
                        dve.reduce_max(mx[u % 2][:, s:s + 1], ps[bank][:, 0:144], AX.X)
                        v = step(dve.reduce_max(mx[u % 2][:, s + 1:s + 2], ps[bank][:, 144:416], AX.X))
                    after(v)
                    n = 2 * len(unit_maps(u))
                    dve.tensor_scalar(mx[u % 2][:, 0:n], mx[u % 2][:, 0:n], -(DIFF_SCALE if u < DIFF_HEADS else MLA_SCALE), None,
                                      ALU.mult).then_inc(negmax_ready, 1)

                def probs(u):
                    U = UNITS * l + u
                    dve.wait_ge(exp_ready, U + 1)
                    s = sm[u % 2]
                    n = 2 * len(unit_maps(u))
                    v = step(dve.reciprocal(s[:, 0:n], s[:, 0:n]))
                    after(v)
                    e = unit_maps(u)[0][1]
                    if u < DIFF_HEADS:
                        v = step(dve.tensor_scalar(s[:, 2:4], s[:, 2:4], neglam[:, l:l + 1], None, ALU.mult))
                        step(dve.tensor_scalar(e_t[:, 0, 0:144], e_t[:, 0, 0:144], s[:, 0:1], None, ALU.mult))
                        v = step(dve.tensor_scalar(e_t[:, 0, 144:416], e_t[:, 0, 144:416], s[:, 1:2], None, ALU.mult))
                        after(v)
                        dve.scalar_tensor_tensor(out=e_t[:, 0, 0:144], in0=e_t[:, 1, 0:144], scalar=s[:, 2:3], in1=e_t[:, 0, 0:144],
                                                 op0=ALU.mult, op1=ALU.add)
                        dve.scalar_tensor_tensor(out=e_t[:, 0, 144:416], in0=e_t[:, 1, 144:416], scalar=s[:, 3:4], in1=e_t[:, 0, 144:416],
                                                 op0=ALU.mult, op1=ALU.add).then_inc(probs_ready, 1)
                    else:
                        dve.tensor_scalar(e_t[:, e, 0:144], e_t[:, e, 0:144], s[:, 0:1], None, ALU.mult)
                        dve.tensor_scalar(e_t[:, e, 144:416], e_t[:, e, 144:416], s[:, 1:2], None, ALU.mult).then_inc(probs_ready, 1)

                def out_part(u):
                    if u < DIFF_HEADS:
                        dve.wait_ge(pv_ready, UNITS * l + u + 1)
                        dve.tensor_copy(od[:, u, t0:], ps[7][:, t0:TOK]).then_inc(out_copied, 1)
                    else:
                        h = u - DIFF_HEADS
                        o = 64 * (h % 2)
                        dve.wait_ge(out_hi, MLA_HEADS * l + h + 1)
                        dve.tensor_tensor(am_lo[o:o + 64, h // 2, t0:], ps[7][o:o + 64, t0:TOK], am_hi[o:o + 64, h // 2, t0:].bitcast(f32),
                                          ALU.subtract).then_inc(out_copied, 1)

                for i in range(16):
                    u = i - 4
                    if u < 0:
                        split(S("gate") + i + AHEAD)
                        gate(i)
                        if i == 3 and l == 0:
                            m3 = lambda a: a.rearrange("p (a b) -> p a b", a=16)
                            dve.wait_ge(meta_scores, 1)
                            v = step(dve.reduce_max(mxm, m3(ps[4][0:16, 0:256]), AX.X))
                            after(v)
                            dve.tensor_tensor(m3(pm[:, 0, :]), m3(ps[4][0:16, 0:256]), mxm[:, :, None].to_broadcast([16, 16, 16]),
                                              ALU.subtract).then_inc(meta_shift, 1)
                            dve.wait_ge(meta_exp, 1)
                            v = step(dve.reduce_sum(mxm, m3(pm[:, 1, :]), AX.X))
                            after(v)
                            v = step(dve.reciprocal(mxm, mxm))
                            after(v)
                            v = step(dve.tensor_scalar(mxm[:, 12:16], mxm[:, 12:16], neglam[0:16, 0:1], None, ALU.mult))
                            after(v)
                            v = step(dve.tensor_tensor(m3(pm[:, 2, :]), m3(pm[:, 1, :]), mxm[:, :, None].to_broadcast([16, 16, 16]), ALU.mult))
                            after(v)
                            dve.tensor_tensor(pm[:, 2, 128:192], pm[:, 2, 128:192], pm[:, 2, 192:256], ALU.add).then_inc(meta_probs, 1)
                        continue
                    negmax(u)
                    probs(u)
                    if u >= 1:
                        out_part(u - 1)
                    split(S("gate") + i + AHEAD)
                    gate(i)
                out_part(UNITS - 1)
                K = K0 + NDIFF
                recip(K, 12)
                dve.wait_ge(norm_bc, K + 1)
                dve.wait_ge(out_copied, UNITS * (l + 1))
                for d in range(DIFF_HEADS):
                    ins = dve.tensor_tensor(od[:, d, t0:], ps[4 + d][:, 64 + t0:64 + TOK], od[:, d, t0:], ALU.mult)
                    ins.then_inc(od_ready, 1)
                dve.wait_ge(od_ready, DIFF_HEADS * (l + 1))
                dve.memset(idle, 0.0).then_inc(norm_ready, 1)
                for d in range(DIFF_HEADS):
                    dve.wait_ge(od_hi_ready, DIFF_HEADS * l + d + 1)
                    dve.scalar_tensor_tensor(out=od_lo[:, d, t0:], in0=od[:, d, t0:], scalar=gsub[:, l:l + 1],
                                             in1=od_hi[:, d, t0:].bitcast(f32), op0=ALU.mult, op1=ALU.subtract).then_inc(od_lo_ready, 1)
                dve.wait_ge(sig_ready, 2 * l + 1)
                for m in range(KC):
                    if m % 2 == 0:
                        split(S("oa") + m // 2 + AHEAD)
                    evac(TL("oa") + m, gates[:, m, t0:], gates[:, m, t0:], t0=t0)

                def mix_low(m):
                    dve.wait_ge(mix_hi, KC * l + m + 1)
                    dve.tensor_tensor(hl[:, m, t0:], gates[:, 8 + m, t0:], hh[:, m, t0:].bitcast(f32), ALU.subtract).then_inc(mix_lo, 1)

                dve.wait_ge(sig_ready, 2 * l + 2)
                for m in range(KC):
                    if m % 2 == 0:
                        split(S("ob") + m // 2 + AHEAD)
                    evac(TL("ob") + m, gates[:, 8 + m, t0:], gates[:, 8 + m, t0:], t0=t0)
                    dve.wait_ge(tile_free, TL("ob") + m + 1)
                    dve.tensor_tensor(gates[:, 8 + m, t0:], gates[:, 8 + m, t0:], gates[:, m, t0:], ALU.add).then_inc(mix_ready, 1)
                    if m:
                        mix_low(m - 1)
                mix_low(KC - 1)

                def to_y(t, m):
                    dve.wait_ge(pe_done, plan.tile_done[t])
                    dve.tensor_copy(y[:, m, t0:], ps[t % BANKS][:, t0:TOK]).then_inc(tile_free, 1)

                for m in range(KC):
                    split(S("out") + m + AHEAD)
                    to_y(TL("out") + m, m)
                recip(K0 + POST_MIX)
                take(K0 + POST_MIX, 7, rstd_p, t0)
                dve.wait_ge(norm_ready, K0 + POST_MIX + 1)
                residual(2 * l + 1, G_MIXPOST, l, t0)
                recip(K0 + PRE_FFN)
                take(K0 + PRE_FFN, 7, rstd_h, t0)
                dve.wait_ge(norm_ready, K0 + PRE_FFN + 1)

                def pair(j, i=None, first=False):
                    s, t = S("gu") + 2 * j, TL("gu") + 2 * j
                    o = 0 if i is None else RING * i
                    p = 0 if i is None else 4 * i
                    J = FC * l + j
                    split(s + AHEAD, i, RING)
                    for k, buf in ((0, gbuf), (1, ubuf)):
                        dve.wait_ge(pe_done, plan.tile_done[t + k] + o)
                        if J >= 2:
                            dve.wait_ge(ff_prod if k else silu_done, J - 1 + p)
                        dve.tensor_tensor(buf[:, j % 2, t0:], ps[(t + k) % BANKS][:, t0:TOK], rstd_h[:, t0:], ALU.mult).then_inc(tile_free, 1)
                        if k == 0:
                            split(s + 1 + AHEAD, i, RING)
                    if not first:
                        lo_ff(j - 1, i)

                def lo_ff(j, i=None):
                    p = 0 if i is None else 4 * i
                    dve.wait_ge(ff_hi_ready, FC * l + j + 1 + p)
                    at_j = slice(j, j + 1) if i is None else bass.ds(4 * i + j, 1)
                    dve.tensor_tensor(ff_lo[:, at_j, t0:], pbuf[:, j % 2:j % 2 + 1, t0:], ff_hi[:, at_j, t0:].bitcast(f32),
                                      ALU.subtract).then_inc(ff_lo_ready, 1)

                pair(0, first=True)
                with dve.Fori(0, 5) as i:
                    for j in range(1, 5):
                        pair(j, i)
                pair(21)
                lo_ff(21)
                for m in range(KC):
                    for j in range(4):
                        split(S("down") + 4 * m + j + AHEAD)
                    to_y(TL("down") + m, m)
                recip(K0 + POST_FFN)
                take(K0 + POST_FFN, 7, rstd_p, t0)
                dve.wait_ge(norm_ready, K0 + POST_FFN + 1)
                residual(2 * l + 2, G_FFNPOST, l, t0)

        @block.tensor
        def _(pe):
            def slot_ready(n, i=None):
                pe.wait_ge(lo_ready, n + 1 + (0 if i is None else RING * i))

            def bank_free(t, i=None, per=0):
                if t >= BANKS:
                    pe.wait_ge(tile_free, t - BANKS + 1 + (0 if i is None else per * i))

            def block(t, n, at, width, hi, lo, t0, first, last):
                dst = ps[t % BANKS][0:width, t0:TOK]
                wh, wl = (w[:, n % RING, at:at + width] for w in (w_hi, w_lo))
                pe.matmul(dst, wh, hi, start=first, stop=False)
                pe.matmul(dst, wh, lo, start=False, stop=False)
                return pe.matmul(dst, wl, hi, start=False, stop=last)

            def tile(t, n, at, width, src, t0, wait=None, i=None, per=0):
                bank_free(t, i, per)
                for k, (a, b) in enumerate(src):
                    if wait:
                        pe.wait_ge(wait[0], wait[1] + k + 1)
                    mm = block(t, n, at + k * width, width, a, b, t0, k == 0, k == len(src) - 1)
                mm.then_inc(pe_done, 1)

            def two_tiles(t, n, src, t0, wait):
                slot_ready(n + 1)
                bank_free(t + 1)
                for k, (a, b) in enumerate(src):
                    pe.wait_ge(wait[0], wait[1] + k + 1)
                    for q in range(2):
                        mm = block(t + q, n + q, k * P, P, a, b, t0, k == 0, k == len(src) - 1)
                        if k == len(src) - 1:
                            mm.then_inc(pe_done, 1)

            def sums(K, a, bank, col=0, src=None, count=True):
                src = acc[:, K % 2, :] if src is None else src
                for c, (t_a, t_b) in enumerate(CH):
                    if a > t_a:
                        t_a = a
                    mm = pe.matmul(ps[bank][:, col + c:col + c + 1], src[:, t_a:t_a + P], ones, start=True, stop=True)
                if count:
                    mm.then_inc(norm_sum, 1)

            def norm_sums(K, bank, t0):
                k = K % NORMS
                pe.wait_ge(sq_added, plan.add0[K] + CHUNKS[k] - 1)
                before = K - 1 if k == NKV else K
                if before > 0:
                    pe.wait_ge(norm_ready, before)
                sums(K, t0, bank)

            def spread(K, bank, t0, col=0, dst=None, count=True):
                for c, (a, b) in enumerate(CH):
                    if t0 > a:
                        continue
                    n = b - a
                    mm = pe.matmul(ps[bank][:, 64 + a:64 + b], rec[K % 2][0:n, col + c:col + c + 1].to_broadcast([n, P]),
                                   ident[0:n, 0:n], start=True, stop=True)
                if count:
                    mm.then_inc(norm_bc, 1)

            def norm_spread(K, bank, t0):
                pe.wait_ge(norm_rec, K + 1)
                spread(K, bank, t0)

            pe.wait_ge(const_ready, 2)
            for l in range(DEPTH):
                t0, K0 = T0(l), NORMS * l
                S = lambda name: plan.slot0[l, name]
                TL = lambda name: plan.tile0[l, name]
                full = [(hh[:, k, :], hl[:, k, :]) for k in range(KC)]
                late = [(hh[:, k, t0:], hl[:, k, t0:]) for k in range(KC)]
                two_tiles(TL("lat"), S("lat"), late, t0, (h_lo, KC * 2 * l))
                norm_sums(K0 + PRE_MIX, 7, 0)
                for i in range(2, 6):
                    slot_ready(S("lat") + i)
                    c0 = t0 if i < QC else 0
                    tile(TL("lat") + i, S("lat") + i, 0, P if i < 5 else HW, late if i < QC else full, c0)
                    if i == 2:
                        norm_spread(K0 + PRE_MIX, 7, 0)
                norm_sums(K0 + NQ, 7, t0)
                norm_sums(K0 + NKV, 6, 0)
                for st in ("dq", "dk", "dv"):
                    for i in range(4):
                        slot_ready(S(st) + i)
                        tile(TL(st) + i, S(st) + i, 0, P, late if st == "dq" else full, t0 if st == "dq" else 0)
                        if st == "dq" and i == 0:
                            norm_spread(K0 + NQ, 7, t0)
                            norm_spread(K0 + NKV, 6, 0)
                pe.wait_ge(lat_ready_lo, 5 * (l + 1))
                qsrc = [(lat_hi[:, k, t0:], lat_lo[:, k, t0:]) for k in range(QC)]
                kvsrc = [(lat_hi[:, QC + k, :], lat_lo[:, QC + k, :]) for k in range(KVC)]
                for h in range(MLA_HEADS):
                    if h % 3 == 0:
                        slot_ready(S("uq") + h // 3)
                    tile(TL("uq") + h, S("uq") + h // 3, (h % 3) * QC * HW, HW, qsrc, t0)
                for h in range(MLA_HEADS):
                    if h % 4 == 0:
                        slot_ready(S("ukv") + h // 4)
                    tile(TL("ukv") + h, S("ukv") + h // 4, (h % 4) * KVC * P, P, kvsrc, 0)

                def v_transposes(g):
                    if g == 0:
                        pe.wait_ge(norm_ready, K0 + NKV + 1)
                        pe.wait_ge(tile_free, TL("dv") + 4)
                    else:
                        pe.wait_ge(tile_free, TL("ukv") + 4 * g)
                        pe.wait_ge(v_copied, 9 * l + 3 * g)
                    for c, (a, b) in enumerate(CH):
                        for s in range(4):
                            src = dv_t[:, s, a:a + P] if g == 0 else kv_t[:, 4 * (g - 1) + s, a:a + P]
                            mm = pe.transpose(ps[4 + c][:, s * P:(s + 1) * P], src, ident)
                    mm.then_inc(v_ready, 1)

                def qk(u, a, b):
                    if u < DIFF_HEADS:
                        return [(dqk[o:o + 64, u, a:b], dqk[o:o + 64, 4 + u, :]) for o in (0, 64)]
                    h = u - DIFF_HEADS
                    return [(q_t[0:96, h, a:b], k_t[0:96, h, :])]

                def keys_ready():
                    pe.wait_ge(rope_done, 5 * (l + 1))
                    pe.wait_ge(kr_ready, l + 1)
                    pe.wait_ge(k_copied, MLA_HEADS * (l + 1))

                def scores(u):
                    U = UNITS * l + u
                    if U:
                        pe.wait_ge(exp_ready, U)
                    for m, (q_a, k) in enumerate(qk(u, 16, 144)):
                        q_b = qk(u, 144, 272)[m][0]
                        bank = ps[4 + m] if u < DIFF_HEADS else ps[4 + u % 2]
                        for q, c0, n in ((q_a, 0, 144), (q_b, 144, 272)):
                            pe.matmul(bank[:, c0:c0 + n], q, k[:, 0:n], start=True, stop=False)
                            mm = pe.matmul(bank[:, c0 + n - P:c0 + n], identb[:, :], maskb[:, :], start=False, stop=True)
                    mm.then_inc(scores_ready, 1)

                def transposes(u):
                    U = UNITS * l + u
                    pe.wait_ge(probs_ready, U + 1)
                    if U:
                        pe.wait_ge(out_copied, U)
                    e = e_t[:, 0 if u < DIFF_HEADS else u % 2, :]
                    for col, src in ((0, 0), (128, 144), (256, 16), (384, 160)):
                        pe.transpose(ps[6][:, col:col + P], e[:, src:src + P], ident)
                    pe.transpose(ps[7][:, 384:512], e[:, 288:416], ident).then_inc(pt_ready, 1)

                def pv(u):
                    U = UNITS * l + u
                    pe.wait_ge(pt_copied, U + 1)
                    if u < DIFF_HEADS:
                        o, n, col = 0, P, P * u
                    else:
                        h = u - DIFF_HEADS
                        o, n, col = 64 * (h % 2), 64, 512 + 64 * h
                    b = u % 2
                    pe.matmul(ps[7][o:o + n, t0:TOK], v_tok[0:16, 0, col:col + n], pt0[0:16, b, t0:], start=True, stop=False)
                    pe.matmul(ps[7][o:o + n, 16:TOK], v_tok[:, 1, col:col + n], pt1[:, b, :], start=False, stop=False)
                    pe.matmul(ps[7][o:o + n, 144:TOK], v_tok[:, 2, col:col + n], pt2[:, b, :], start=False, stop=True).then_inc(pv_ready, 1)

                for i in range(16):
                    u = i - 4
                    if u >= 0:
                        if u == 0 and l == 0:
                            pe.wait_ge(meta_copied, 1)
                        if u == 0:
                            pe.wait_ge(v_copied, 9 * (l + 1))
                        scores(u)
                        if u:
                            pv(u - 1)
                    slot_ready(S("gate") + i)
                    tile(TL("gate") + i, S("gate") + i, 0, P, late, t0)
                    if u >= 0:
                        transposes(u)
                    elif i < 3:
                        v_transposes(i)
                    else:
                        keys_ready()
                        if l == 0:
                            pe.wait_ge(v_copied, 9)
                            pe.matmul(ps[4][0:16, 0:256], identb[0:16, 0:16], maskmb[:, :], start=True, stop=False)
                            maps = [(q, k) for u_ in range(4, 12) for q, k in qk(u_, 0, 16)]
                            maps += [qk(u_, 0, 16)[s] for s in range(2) for u_ in range(4)]
                            for m, (q, k) in enumerate(maps):
                                mm = pe.matmul(ps[4][0:16, 16 * m:16 * m + 16], q, k[:, 0:16], start=False, stop=m == 15)
                                if m == 11:
                                    mm.then_inc(meta_half, 1)
                                    pe.wait_ge(meta_half, 1)
                            mm.then_inc(meta_scores, 1)
                            pe.wait_ge(meta_probs, 1)
                            for u_ in range(UNITS):
                                m = 8 + u_ if u_ < DIFF_HEADS else u_ - DIFF_HEADS
                                mm = pe.matmul(ps[5][0:16, 16 * u_:16 * u_ + 16], pm[:, 2, 16 * m:16 * m + 16], ident[0:16, 0:16],
                                               start=True, stop=True)
                            mm.then_inc(meta_pt, 1)
                K = K0 + NDIFF
                pe.wait_ge(od_squared, l + 1)
                for d in range(DIFF_HEADS):
                    sums(K, t0, 4, 3 * d, b_t[:, d, :], d == DIFF_HEADS - 1)
                pv(UNITS - 1)
                pe.wait_ge(norm_rec, K + 1)
                for d in range(DIFF_HEADS):
                    if d == 3:
                        pe.wait_ge(out_copied, UNITS * (l + 1))
                    spread(K, 4 + d, t0, 3 * d, count=d == DIFF_HEADS - 1)
                src = [(am_hi[:, k, t0:], am_lo[:, k, t0:]) for k in range(4)]
                pe.wait_ge(out_copied, UNITS * (l + 1))
                for m in range(KC):
                    if m % 2 == 0:
                        slot_ready(S("oa") + m // 2)
                    tile(TL("oa") + m, S("oa") + m // 2, (m % 2) * 4 * P, P, src, t0)
                src = [(od_hi[:, k, t0:], od_lo[:, k, t0:]) for k in range(4)]
                pe.wait_ge(od_lo_ready, DIFF_HEADS * (l + 1))
                for m in range(KC):
                    if m % 2 == 0:
                        slot_ready(S("ob") + m // 2)
                    tile(TL("ob") + m, S("ob") + m // 2, (m % 2) * 4 * P, P, src, t0)
                for m in range(KC):
                    slot_ready(S("out") + m)
                    tile(TL("out") + m, S("out") + m, 0, P, late, t0, (mix_lo, KC * l) if m == 0 else None)
                norm_sums(K0 + POST_MIX, 7, t0)
                norm_spread(K0 + POST_MIX, 7, t0)
                g0, gt = S("gu"), TL("gu")
                two_tiles(gt, g0, late, t0, (h_lo, KC * (2 * l + 1)))
                norm_sums(K0 + PRE_FFN, 7, t0)
                norm_spread(K0 + PRE_FFN, 7, t0)
                with pe.Fori(0, 5) as i:
                    for j in range(2, 2 + RING):
                        slot_ready(g0 + j, i)
                        tile(gt + j, g0 + j, 0, P, late, t0, i=i, per=RING)
                for j in (42, 43):
                    slot_ready(g0 + j)
                    tile(gt + j, g0 + j, 0, P, late, t0)
                d0, dt = S("down"), TL("down")
                for m in range(KC):
                    t = dt + m
                    bank_free(t)
                    k = 0
                    for j, cnt in enumerate(DOWN_SPLIT):
                        n = d0 + 4 * m + j
                        slot_ready(n)
                        for q in range(cnt):
                            if m == 0:
                                pe.wait_ge(ff_lo_ready, FC * l + k + 1)
                            mm = block(t, n, q * P, P, ff_hi[:, k, t0:], ff_lo[:, k, t0:], t0, k == 0, k == FC - 1)
                            k += 1
                        mm.then_inc(pe_done, 1)
                norm_sums(K0 + POST_FFN, 7, t0)
                norm_spread(K0 + POST_FFN, 7, t0)


def rope_table(rot, rows, period):
    half = rot // 2
    inv = (np.float32(THETA) ** (-np.arange(0, rot, 2, dtype=np.float32) / np.float32(rot))).astype(np.float32)
    ang = (np.arange(TOK, dtype=np.float32)[:, None] * inv[None, :]).astype(np.float32)
    c, s = np.cos(ang).T.astype(np.float32), np.sin(ang).T.astype(np.float32)
    cos, sin = np.ones((P, TOK), np.float32), np.zeros((P, TOK), np.float32)
    for p0 in range(rows, P, period):
        cos[p0:p0 + half], cos[p0 + half:p0 + rot] = c, c
        sin[p0:p0 + half], sin[p0 + half:p0 + rot] = s, -s
    return cos, sin


def constants():
    c = np.zeros((P, C_ALL), np.float32)
    c[:, C_ID:C_ID + P] = np.eye(P)
    c[:, C_MASK:C_MASK + P] = np.where(np.arange(P)[None, :] > np.arange(P)[:, None], MASKED, 0.0)
    m16 = np.where(np.arange(16)[None, :] > np.arange(16)[:, None], MASKED, 0.0)
    for m in range(16):
        c[0:16, C_MASKM + 16 * m:C_MASKM + 16 * m + 16] = m16
    c[:, C_COSD:C_COSD + TOK], c[:, C_SIND:C_SIND + TOK] = rope_table(DIFF_ROPE, 0, DIFF_DH)
    c[:, C_COSM:C_COSM + TOK], c[:, C_SINM:C_SINM + TOK] = rope_table(ROPE, NOPE, P)
    return c


def pack_weights(w_in, w_uq, w_ukv, w_oa, w_ob, w_out, w_gu, w_down):
    plan = Plan()
    packed = np.zeros((plan.slots, P, SLOT), np.float32)

    def blocks(w, k0, k1, c0, width):
        a = w[k0 * P:k1 * P, c0:c0 + width]
        return a.reshape(k1 - k0, P, width).transpose(1, 0, 2).reshape(P, (k1 - k0) * width)

    def put(n, parts):
        at = 0
        for a in parts:
            packed[n, :, at:at + a.shape[1]] = a
            at += a.shape[1]

    for l in range(DEPTH):
        S = lambda name: plan.slot0[l, name]
        for i in range(5):
            put(S("lat") + i, [blocks(w_in[l], 0, KC, i * P, P)])
        put(S("lat") + 5, [blocks(w_in[l], 0, KC, Q_RANK + KV_RANK - NOPE, HW)])
        for st, o in (("dq", O_DQ), ("dk", O_DK), ("dv", O_DV)):
            for i in range(4):
                put(S(st) + i, [blocks(w_in[l], 0, KC, o + i * P, P)])
        for h in range(MLA_HEADS):
            at = (h % 3) * QC * HW
            packed[S("uq") + h // 3, :, at:at + QC * HW] = blocks(w_uq[l], 0, QC, h * HW, HW)
            at = (h % 4) * KVC * P
            packed[S("ukv") + h // 4, :, at:at + KVC * P] = blocks(w_ukv[l], 0, KVC, h * P, P)
        for i in range(16):
            put(S("gate") + i, [blocks(w_in[l], 0, KC, O_G + i * P, P)])
        for i in range(4):
            put(S("oa") + i, [blocks(w_oa[l], 0, 4, (2 * i + q) * P, P) for q in range(2)])
            put(S("ob") + i, [blocks(w_ob[l], 0, 4, (2 * i + q) * P, P) for q in range(2)])
        for m in range(KC):
            put(S("out") + m, [blocks(w_out[l], 0, KC, m * P, P)])
        for j in range(FC):
            put(S("gu") + 2 * j, [blocks(w_gu[l], 0, KC, j * P, P)])
            put(S("gu") + 2 * j + 1, [blocks(w_gu[l], 0, KC, D_FF + j * P, P)])
        for m in range(KC):
            k = 0
            for j, cnt in enumerate(DOWN_SPLIT):
                put(S("down") + 4 * m + j, [blocks(w_down[l], k, k + cnt, m * P, P)])
                k += cnt
    return packed.reshape(plan.slots * P, SLOT)


def kernel(x, meta_tokens, norm_mix_pre, norm_mix_post, norm_ffn_pre, norm_ffn_post, w_in, mla_q_norm,
           mla_kv_norm, mla_w_uq, mla_w_ukv, w_o_mla, diff_lambda, diff_subln, w_o_diff, w_out, w_gate_up, w_down):
    import concourse.bacc as _bacc
    from concourse.bass_utils import run_bass_kernel_spmd as _run

    A = lambda a: np.asarray(a)
    tokens = np.concatenate([A(meta_tokens), A(x)[0]], axis=0)
    x_t = tokens.T.reshape(KC, P, TOK).transpose(1, 0, 2).reshape(P, KC * TOK)
    cols = [A(g).reshape(DEPTH, -1, P) for g in (norm_mix_pre, norm_mix_post, norm_ffn_pre, norm_ffn_post,
                                                 mla_q_norm, mla_kv_norm, diff_subln)]
    gains = np.concatenate(cols, axis=1).transpose(2, 0, 1).reshape(P, DEPTH * GAINS)
    lam = np.broadcast_to(A(diff_lambda).reshape(1, DEPTH * 4 * DIFF_DH), (P, DEPTH * 4 * DIFF_DH))
    packed = pack_weights(A(w_in), A(mla_w_uq), A(mla_w_ukv), A(w_o_mla), A(w_o_diff), A(w_out), A(w_gate_up), A(w_down))
    arrays = {"x_t": x_t, "weights": packed, "gains": gains, "lam": lam, "consts": constants()}
    arrays = {k: np.ascontiguousarray(v) for k, v in arrays.items()}
    f32 = mybir.dt.float32
    nc = _bacc.Bacc("TRN2", target_bir_lowering=False, num_devices=1)
    ins = [nc.dram_tensor(k, v.shape, f32, kind="ExternalInput").ap() for k, v in arrays.items()]
    out = nc.dram_tensor("out_t", (P, KC * SEQ), f32, kind="ExternalOutput").ap()
    build_trunk(nc, *ins, out)
    r = _run(nc, [arrays], core_ids=[0])
    got = r.results[0]["out_t"]
    return got.reshape(P, KC, SEQ).transpose(2, 1, 0).reshape(1, SEQ, D_MODEL)
```

```python
import concourse.bass as bass
from concourse import mybir
from contextlib import ExitStack
import math
import numpy as np

P = 128
D_MODEL, SEQ, DEPTH, N_META = 1024, 256, 2, 16
TOK = SEQ + N_META
MLA_HEADS, NOPE, ROPE, MLA_V = 8, 64, 32, 64
Q_RANK, KV_RANK = 384, 256
DIFF_HEADS, DIFF_DH = 4, 64
DIFF_ROPE = DIFF_DH // 4
D_FF = -(-(8 * D_MODEL) // (3 * 256)) * 256
THETA, EPS = 500000.0, 1e-6
MLA_SCALE = 1.0 / math.sqrt(NOPE + ROPE)
DIFF_SCALE = 1.0 / math.sqrt(DIFF_DH)
LAM_INIT = [0.8 - 0.6 * math.exp(-0.3 * l) for l in range(DEPTH)]
MASKED = -1e30

KC = D_MODEL // P
QC, KVC = Q_RANK // P, KV_RANK // P
FC = D_FF // P
HW = NOPE + ROPE
DOWN_SPLIT = (6, 6, 5, 5)
SLOT = 8 * P
RING, RAW, AHEAD, BANKS = 8, 4, 6, 4
HI_AHEAD = AHEAD + 1
CH = [(0, 16), (16, 144), (144, 272)]
UNITS = DIFF_HEADS + MLA_HEADS
MAPS = 2 * DIFF_HEADS + MLA_HEADS


def first_map(u):
    return 2 * u if u < DIFF_HEADS else u + DIFF_HEADS


NORMS = 7
PRE_MIX, NQ, NKV, NDIFF, POST_MIX, PRE_FFN, POST_FFN = range(NORMS)
CHUNKS = {PRE_MIX: KC, NQ: QC, NKV: KVC, POST_MIX: KC, PRE_FFN: KC, POST_FFN: KC}

ENDS = {"lat": [1] * 6, "dq": [1] * 4, "dk": [1] * 4, "dv": [1] * 4, "uq": [3, 3, 2], "ukv": [4, 4],
        "gate": [1] * 16, "oa": [2] * 4, "ob": [2] * 4, "out": [1] * 8, "gu": [1] * (2 * FC),
        "down": [0, 0, 0, 1] * KC}
TURNS = [("uq", 0), ("dv", 0), ("uq", 1), ("dv", 1), ("uq", 2), ("dv", 2), ("ukv", 0), ("dv", 3), ("ukv", 1)]

O_DQ = Q_RANK + KV_RANK + ROPE
O_DK = O_DQ + DIFF_HEADS * 2 * DIFF_DH
O_DV = O_DK + DIFF_HEADS * 2 * DIFF_DH
O_G = O_DV + DIFF_HEADS * 2 * DIFF_DH
G_MIXPRE, G_MIXPOST, G_FFNPRE, G_FFNPOST, G_Q, G_KV, G_SUB = 0, 8, 16, 24, 32, 35, 37
GAINS = 38
C_ID, C_MASK, C_MASKM, C_COSD, C_SIND, C_COSM, C_SINM = 0, 128, 256, 512, 784, 1056, 1328
C_ALL = 1600


class Plan:

    def __init__(self):
        self.slot, self.tile, self.name_of = {}, {}, []
        self.slot_done, self.tile_done = [], []
        done = 0
        for l in range(DEPTH):
            order = [(n, i) for n in ("lat", "dq", "dk") for i in range(len(ENDS[n]))] + TURNS
            order += [(n, i) for n in ("gate", "oa", "ob", "out", "gu", "down") for i in range(len(ENDS[n]))]
            for name, i in order:
                self.slot[l, name, i] = len(self.slot_done)
                for _ in range(ENDS[name][i]):
                    done += 1
                    self.tile[l, name, sum(self.name_of[t] == (l, name) for t in range(len(self.name_of)))] = len(self.tile_done)
                    self.name_of.append((l, name))
                    self.tile_done.append(done)
                if ENDS[name][i] == 0:
                    done += 1
                self.slot_done.append(done)
        self.slots = len(self.slot_done)
        self.sq0, self.add0, self.sq_place, self.sq_free = {}, {}, {}, {}
        s = a = 0
        users = []
        for l in range(DEPTH):
            for k in range(NORMS):
                if k in CHUNKS:
                    K = l * NORMS + k
                    self.sq0[K], self.add0[K] = s, a
                    for c in range(1, CHUNKS[k]):
                        last = c == CHUNKS[k] - 1
                        a += not last
                        self.sq_place[K, c] = len(users) % 2
                        self.sq_free[K, c] = users[-2] if len(users) >= 2 else None
                        users.append(("sum", K + 1) if last else ("add", a))
                    s += CHUNKS[k]


def build_trunk(nc: bass.Bass, xT, weights, gains, lam_in, consts, outT):
    f32, f32r, bf16 = mybir.dt.float32, mybir.dt.float32r, mybir.dt.bfloat16
    ALU, ACT, AX = mybir.AluOpType, mybir.ActivationFunctionType, mybir.AxisListType
    plan = Plan()
    ctx = ExitStack()
    with ctx:
        base = -(-nc.sbuf_base // 32) * 32

        def place(at, tensors):
            made = []
            for name, shape, dt in tensors:
                size = int(np.prod(shape[1:])) * (2 if dt == bf16 else 4)
                made.append(nc.alloc_sbuf_tensor_at(name, shape, dt, offset=at))
                at += -(-size // 32) * 32
            return made, at

        (w_raw, w_hi, w_lo, r, hh, hl, y, rstd_h, rstd_p, acc, sq, rc_d, rs_d, rc_q, rs_q,
         cst, identb, maskb, gain, small, lat, tres), at = place(base, [
            ("w_raw", [P, RAW, SLOT], f32), ("w_hi", [P, RING, SLOT], f32r), ("w_lo", [P, RING, SLOT], f32r),
            ("resid", [P, KC, TOK], f32), ("h_hi", [P, KC, TOK], f32r), ("h_lo", [P, KC, TOK], f32r),
            ("y", [P, KC, TOK], f32),
            ("rstd_h", [P, TOK], f32), ("rstd_p", [P, TOK], f32), ("acc", [P, 2, TOK], f32), ("sq", [P, 2, TOK], f32),
            ("rcos_d", [P, TOK], f32), ("rsin_d", [P, TOK], f32), ("rcos_q", [P, TOK], f32),
            ("rsin_q", [P, TOK], f32),
            ("cst", [P, C_ALL - 512 + 128], f32), ("identb", [P, P], bf16), ("maskb", [P, P], bf16),
            ("gain", [P, DEPTH, GAINS], f32), ("small", [P, 96], f32), ("lat", [P, 2, TOK], f32),
            ("tres", [P, TOK], f32)])
        lat_tmp_at = at - 4 * 3 * TOK
        rstd_q, rstd_kv = rstd_p, tres
        att0 = at
        (q_t, dqk, v_tok, gates), at = place(att0, [
            ("q_t", [P, MLA_HEADS, TOK], f32), ("dqk_t", [P, 8, TOK], f32),
            ("v_tok", [P, 3, 1024], f32), ("gates", [P, 16, TOK], f32)])
        gates_last_at = at - 4 * TOK
        k_t = nc.alloc_sbuf_tensor_at("k_t", [P, MLA_HEADS, TOK], f32, offset=base + 4 * (RAW + 2 * RING) * SLOT + 3 * 4 * KC * TOK)
        lat_at = at
        (lat_hi, lat_lo), at = place(lat_at, [("lat_hi", [P, QC + KVC, TOK], f32r), ("lat_lo", [P, QC + KVC, TOK], f32r)])
        (e_t, pt0, pt1, pt2, ptm), _ = place(lat_at, [("e_t", [P, 2, 416], f32), ("pt0", [16, 2, TOK], f32), ("pt1", [P, 2, 256], f32),
                                                      ("pt2", [P, 2, 128], f32), ("ptm", [16, UNITS, 16], f32)])
        assert _ <= at
        v_at = at
        (kv_t, dv_t), at = place(v_at, [("kv_t", [P, MLA_HEADS, TOK], f32), ("dv_t", [P, DIFF_HEADS, TOK], f32)])
        (am_hi, am_lo, od), _ = place(v_at, [("am_hi", [P, 4, TOK], f32r), ("am_lo", [P, 4, TOK], f32r),
                                             ("od", [P, DIFF_HEADS, TOK], f32)])
        assert _ <= at
        (b_t,), at = place(at, [("b_t", [P, 4, TOK], f32)])
        (pm,), _ = place(lat_tmp_at, [("pm", [16, 3, 256], f32)])
        (maskmb,), _ = place(gates_last_at, [("maskmb", [16, 256], bf16)])
        krope = dv_t[:, 0, :]
        dqk_at = att0 + 4 * MLA_HEADS * TOK
        (od_hi, od_lo), _ = place(dqk_at, [("od_hi", [P, 4, TOK], f32r), ("od_lo", [P, 4, TOK], f32r)])
        (ff_hi, ff_lo, gbuf, ubuf, sbuf_, pbuf), _ = place(att0, [
            ("ff_hi", [P, FC, TOK], f32r), ("ff_lo", [P, FC, TOK], f32r), ("gbuf", [P, 2, TOK], f32),
            ("ubuf", [P, 2, TOK], f32), ("sbuf", [P, 2, TOK], f32), ("pbuf", [P, 2, TOK], f32)])
        assert _ <= nc.sbuf_usable_end
        ident = cst[:, 0:P]
        cos_d, sin_d, cos_m, sin_m = (cst[:, P + TOK * i:P + TOK * (i + 1)] for i in range(4))
        stage = y[:, 0:2, 0:256]
        eps = small[:, 0:1]
        ones = small[:, 1:2]
        neglam = small[:, 2:4]
        lam_e = small[:, 4:8]
        std = [small[:, 8 + 12 * i:20 + 12 * i] for i in range(2)]
        rec = [small[:, 32 + 12 * i:44 + 12 * i] for i in range(2)]
        mx = [small[:, 56 + 4 * i:60 + 4 * i] for i in range(2)]
        sm = [small[:, 64 + 4 * i:68 + 4 * i] for i in range(2)]
        mxm = small[0:16, 72:88]
        lamp = small[:, 92:96]
        idle = small[:, 90:91]
        idle_act = small[:, 91:92]
        gsub = small[:, 88:90]
        lam_raw = b_t[:, 0:2, 0:256]
        ps = [ctx.enter_context(nc.psum_tensor(f"bank{i}", [P, 512], f32)) for i in range(8)]

        def sem(name):
            return ctx.enter_context(nc.semaphore(name))

        raw_in = [sem(f"raw_in{i}") for i in range(RAW)]
        x_in = [sem(f"x_in{q}") for q in range(4)]
        gain_in, id_in, tables_in, mask_in, out_done = (sem(n) for n in ("gain_in", "id_in", "tables_in", "mask_in", "out_done"))
        hi_ready, lo_ready = sem("hi_ready"), sem("lo_ready")
        pe_done, tile_free = sem("pe_done"), sem("tile_free")
        dve_step, act_step = sem("dve_step"), sem("act_step")
        const_ready, lam_ready, lam_exp = sem("const_ready"), sem("lam_ready"), sem("lam_exp")
        sq_ready, sq_added = sem("sq_ready"), sem("sq_added")
        norm_sum, norm_std, norm_rec, norm_bc, norm_ready = (sem(n) for n in ("norm_sum", "norm_std", "norm_rec", "norm_bc", "norm_ready"))
        r_ready, h_hi, h_lo = sem("r_ready"), sem("h_hi_ready"), sem("h_lo_ready")
        lat_ready_hi, lat_ready_lo = sem("lat_hi_ready"), sem("lat_lo_ready")
        rope_in, rope_done, kr_ready, k_copied = sem("rope_in"), sem("rope_done"), sem("kr_ready"), sem("k_copied")
        v_ready, v_copied = sem("v_ready"), sem("v_copied")
        meta_half, meta_scores, meta_shift, meta_exp, meta_probs, meta_pt, meta_copied = (sem(n) for n in ("meta_half", "meta_scores", "meta_shift", "meta_exp", "meta_probs", "meta_pt", "meta_copied"))
        scores_ready, negmax_ready, exp_ready, probs_ready = (sem(n) for n in ("scores_ready", "negmax_ready", "exp_ready", "probs_ready"))
        pt_ready, pt_copied, pv_ready, out_hi, out_copied = (sem(n) for n in ("pt_ready", "pt_copied", "pv_ready", "out_hi", "out_copied"))
        od_squared, od_ready, od_hi_ready, od_lo_ready = sem("od_squared"), sem("od_ready"), sem("od_hi_ready"), sem("od_lo_ready")
        sig_ready, mix_ready, mix_hi, mix_lo = sem("sig_ready"), sem("mix_ready"), sem("mix_hi"), sem("mix_lo")
        silu_done, ff_prod, ff_hi_ready, ff_lo_ready = sem("silu_done"), sem("ff_prod"), sem("ff_hi_ready"), sem("ff_lo_ready")

        block = ctx.enter_context(nc.Block())

        def T0(l):
            return 0 if l < DEPTH - 1 else N_META

        def boundary_from(b):
            return N_META if b >= 2 * DEPTH - 1 else 0

        @block.sync
        def _(sp):
            def load(n, width, i=None, per=0):
                m = n if i is None else n + per * i
                if n >= RAW:
                    sp.wait_ge(lo_ready, m - RAW + 1)
                src = weights[bass.ds(m * P, P), 0:width] if i is not None else weights[m * P:(m + 1) * P, 0:width]
                sp.dma_start(w_raw[:, n % RAW, 0:width], src).then_inc(raw_in[n % RAW], 16)

            xc = xT.rearrange("p (k t) -> p k t", k=KC)
            sp.dma_start(gain[:, :, :], gains.rearrange("p (l g) -> p l g", l=DEPTH)).then_inc(gain_in, 16)
            sp.dma_start(r[:, 0:2, :], xc[:, 0:2, :]).then_inc(x_in[0], 16)
            load(0, SLOT)
            load(1, SLOT)
            for q in range(1, 4):
                sp.dma_start(r[:, 2 * q:2 * q + 2, :], xc[:, 2 * q:2 * q + 2, :]).then_inc(x_in[q], 16)
            load(2, SLOT)
            sp.dma_start(cst[:, 0:P], consts[:, 0:P]).then_inc(id_in, 16)
            load(3, SLOT)
            load(4, SLOT)
            sp.dma_start(cst[:, P:], consts[:, 512:C_ALL]).then_inc(tables_in, 16)
            load(5, SLOT)
            sp.dma_start(stage, consts[:, P:512 + P].rearrange("p (a b) -> p a b", a=2)[:, :, 0:256]).then_inc(mask_in, 16)
            sp.dma_start(lam_raw, lam_in.rearrange("p (l g) -> p l g", l=DEPTH)).then_inc(mask_in, 16)
            first = 6
            for l in range(DEPTH):
                d0 = plan.slot[l, "down", 0]
                whole = (d0 - first) // RING
                with sp.Fori(0, whole) as i:
                    for j in range(RING):
                        load(first + j, SLOT, i, RING)
                for n in range(first + whole * RING, d0):
                    load(n, SLOT)
                with sp.Fori(0, KC // 2) as i:
                    for j in range(RING):
                        load(d0 + j, DOWN_SPLIT[j % 4] * P, i, RING)
                first = d0 + 4 * KC
            for c in range(KC):
                sp.wait_ge(r_ready, KC * (2 * DEPTH - 1) + c + 1)
                sp.dma_start(outT[:, c * SEQ:(c + 1) * SEQ], r[:, c, N_META:TOK]).then_inc(out_done, 16)
            sp.wait_ge(out_done, 16 * KC)

        @block.scalar
        def _(act):
            def split(n, i=None, per=0):
                if n >= plan.slots:
                    return
                u, v = (0, 0) if i is None else (per * i, 4 * per * i)
                act.wait_ge(raw_in[n % RAW], 16 * (n // RAW + 1) + v)
                if n >= RING:
                    act.wait_ge(pe_done, plan.slot_done[n - RING] + u)
                act.activation(w_hi[:, n % RING, :], w_raw[:, n % RAW, :], ACT.Copy).then_inc(hi_ready, 1)

            def square(K, c, src, t0):
                if c == 0:
                    if K >= 2:
                        act.wait_ge(norm_sum, K - 1)
                    dst = acc[:, K % 2, t0:]
                else:
                    if plan.sq_free[K, c]:
                        how, value = plan.sq_free[K, c]
                        act.wait_ge(sq_added if how == "add" else norm_sum, value)
                    dst = sq[:, plan.sq_place[K, c], t0:]
                act.activation(dst, src, ACT.Square).then_inc(sq_ready, 1)

            def root(K, sums, n, width):
                act.wait_ge(norm_sum, K + 1)
                if K == 0:
                    act.wait_ge(const_ready, 1)
                if K >= 2:
                    act.wait_ge(norm_rec, K - 1)
                act.activation(std[K % 2][:, 0:n], sums, ACT.Sqrt, bias=eps, scale=1.0 / width).then_inc(norm_std, 1)

            def boundary(b, K, g, l):
                t0 = boundary_from(b)
                for c in range(KC):
                    act.wait_ge(r_ready, KC * (b - 1) + c + 1)
                    act.activation(hh[:, c, t0:], r[:, c, t0:], ACT.Copy, scale=gain[:, l, g + c:g + c + 1]).then_inc(h_hi, 1)
                    square(K, c, r[:, c, t0:], t0)

            act.wait_ge(gain_in, 16)
            for c in range(KC):
                if c % 2 == 0:
                    act.wait_ge(x_in[c // 2], 16)
                act.activation(hh[:, c, :], r[:, c, :], ACT.Copy, scale=gain[:, 0, G_MIXPRE + c:G_MIXPRE + c + 1]).then_inc(h_hi, 1)
                if c in (1, 2):
                    split(c - 1)
            split(2)
            for c in range(KC):
                square(0, c, r[:, c, :], 0)
                if c == 3:
                    split(3)
            for n in range(4, HI_AHEAD):
                split(n)
            for l in range(DEPTH):
                t0, K0 = T0(l), NORMS * l
                S = lambda name, i=0: plan.slot[l, name, i]
                TL = lambda name, i=0: plan.tile[l, name, i]
                root(K0 + PRE_MIX, ps[7][:, 0:3], 3, D_MODEL)
                for i in range(6):
                    split(S("lat") + i + HI_AHEAD)
                    if i == 5:
                        continue
                    c0 = t0 if i < QC else 0
                    act.wait_ge(tile_free, TL("lat") + i + 1)
                    if l and i == 0:
                        act.wait_ge(pt_ready, UNITS * l)
                    act.activation(lat_hi[:, i, c0:], lat[:, i % 2, c0:], ACT.Copy,
                                   scale=gain[:, l, G_Q + i:G_Q + i + 1]).then_inc(lat_ready_hi, 1)
                    if i < QC:
                        square(K0 + NQ, i, lat[:, i % 2, c0:], c0)
                    else:
                        square(K0 + NKV, i - QC, lat[:, i % 2, c0:], c0)
                if l == 0:
                    act.wait_ge(lam_ready, 1)
                    act.activation(lam_e, lamp, ACT.Exp).then_inc(lam_exp, 1)
                for i in range(4):
                    split(S("dq") + i + HI_AHEAD)
                root(K0 + NQ, ps[7][:, 0:3], 3, Q_RANK)
                root(K0 + NKV, ps[6][:, 0:3], 3, KV_RANK)
                act.wait_ge(rope_done, 5 * l + 1)
                act.activation(k_t[64:96, :, :], krope[64:96, None, :].to_broadcast([32, MLA_HEADS, TOK]), ACT.Copy).then_inc(kr_ready, 1)
                for n in range(S("dq") + 4, S("dk") + 4):
                    split(n + HI_AHEAD)
                for st, i in TURNS:
                    split(S(st, i) + HI_AHEAD)
                    if st == "ukv":
                        for h in range(4 * i, 4 * i + 4):
                            act.wait_ge(tile_free, TL("ukv", h) + 1)
                            act.activation(k_t[0:64, h, :], kv_t[0:64, h, :], ACT.Copy).then_inc(k_copied, 1)

                def v_evac(g):
                    act.wait_ge(v_ready, 3 * l + g + 1)
                    for c, (a, b) in enumerate(CH):
                        n = b - a
                        if g == 0:
                            act.activation(v_tok[0:n, c, 0:512], ps[4 + c][0:n, :], ACT.Copy).then_inc(v_copied, 1)
                        else:
                            act.activation(v_tok[0:n, c, 512 + 256 * (g - 1):768 + 256 * (g - 1)].rearrange("p (a b) -> p a b", a=4),
                                           ps[4 + c][0:n, :].rearrange("p (a b) -> p a b", a=4)[:, :, 64:128], ACT.Copy).then_inc(v_copied, 1)

                def exps(u):
                    maps = [(4, 0, 0), (5, 1, 2)] if u < DIFF_HEADS else [(4 + u % 2, u % 2, 0)]
                    scale = DIFF_SCALE if u < DIFF_HEADS else MLA_SCALE
                    for m, (bank, e, s) in enumerate(maps):
                        act.wait_ge(negmax_ready, MAPS * l + first_map(u) + m + 1)
                        for part, (a, b) in enumerate(((0, 144), (144, 416))):
                            last = act.activation(e_t[:, e, a:b], ps[bank][:, a:b], ACT.Exp, bias=mx[u % 2][:, s + part:s + part + 1],
                                                  scale=scale, accum_out=sm[u % 2][:, s + part:s + part + 1])
                        last.then_inc(exp_ready, 1)

                def hi_out(u):
                    if u < DIFF_HEADS:
                        return
                    h = u - DIFF_HEADS
                    o = 64 * (h % 2)
                    act.wait_ge(pv_ready, UNITS * l + u + 1)
                    act.activation(am_hi[o:o + 64, h // 2, t0:], ps[7][o:o + 64, t0:TOK], ACT.Copy).then_inc(out_hi, 1)

                def pt_evac(u):
                    act.wait_ge(pt_ready, UNITS * l + u + 1)
                    b = u % 2
                    if l == 0:
                        if u == 0:
                            act.wait_ge(meta_copied, 1)
                        act.activation(pt0[0:16, b, 0:16], ptm[:, u, :], ACT.Copy)
                    act.activation(pt0[0:16, b, 16:], ps[6][0:16, 0:256], ACT.Copy)
                    act.activation(pt1[:, b, :], ps[6][:, 256:512], ACT.Copy)
                    act.activation(pt2[:, b, :], ps[7][:, 384:512], ACT.Copy).then_inc(pt_copied, 1)

                for i in range(16):
                    u = i - 4
                    if u < 0:
                        split(S("gate") + i + HI_AHEAD)
                        if i < 3:
                            v_evac(i)
                        elif l == 0:
                            act.wait_ge(meta_shift, 1)
                            act.activation(pm[:, 1, 0:128], pm[:, 0, 0:128], ACT.Exp, scale=MLA_SCALE)
                            act.activation(pm[:, 1, 128:256], pm[:, 0, 128:256], ACT.Exp, scale=DIFF_SCALE).then_inc(meta_exp, 1)
                            act.wait_ge(meta_pt, 1)
                            act.activation(ptm[:, :, :], ps[7][0:16, 256:256 + 16 * UNITS].rearrange("p (a b) -> p a b", a=UNITS), ACT.Copy).then_inc(meta_copied, 1)
                        continue
                    exps(u)
                    if u >= 1:
                        hi_out(u - 1)
                    split(S("gate") + i + HI_AHEAD)
                    pt_evac(u)
                    if u == 5:
                        act.wait_ge(out_copied, UNITS * l + 4)
                        act.activation(b_t[:, :, t0:], od[:, :, t0:], ACT.Square).then_inc(od_squared, 1)
                hi_out(UNITS - 1)
                K = K0 + NDIFF
                root(K, ps[4][:, 0:12], 12, 2 * DIFF_DH)
                for half in range(2):
                    act.wait_ge(tile_free, TL("gate") + 8 * half + 8)
                    act.activation(gates[:, 8 * half:8 * half + 8, t0:], gates[:, 8 * half:8 * half + 8, t0:], ACT.Sigmoid).then_inc(sig_ready, 1)
                    split(S("oa") + half + HI_AHEAD)
                for i in range(2, 4):
                    split(S("oa") + i + HI_AHEAD)
                    for d in range(2 * i - 4, 2 * i - 2):
                        act.wait_ge(od_ready, DIFF_HEADS * l + d + 1)
                        act.activation(od_hi[:, d, t0:], od[:, d, t0:], ACT.Copy, scale=gsub[:, l:l + 1]).then_inc(od_hi_ready, 1)

                def square_tile(K, t, m):
                    if m == KC - 2:
                        act.activation(idle_act, eps, ACT.Sqrt)
                    if m < KC - 1:
                        act.wait_ge(tile_free, t + 1)
                        square(K, m, y[:, m, t0:], t0)
                    else:
                        act.wait_ge(pe_done, plan.tile_done[t])
                        square(K, m, ps[t % BANKS][:, t0:TOK], t0)

                def mix_split(m):
                    act.wait_ge(mix_ready, KC * l + m + 1)
                    act.activation(hh[:, m, t0:], gates[:, 8 + m, t0:], ACT.Copy).then_inc(mix_hi, 1)

                for i in range(4):
                    split(S("ob") + i + HI_AHEAD)
                    mix_split(2 * i)
                    mix_split(2 * i + 1)
                for m in range(KC):
                    split(S("out") + m + HI_AHEAD)
                    square_tile(K0 + POST_MIX, TL("out") + m, m)
                root(K0 + POST_MIX, ps[7][:, 0:3], 3, D_MODEL)
                boundary(2 * l + 1, K0 + PRE_FFN, G_FFNPRE, l)
                root(K0 + PRE_FFN, ps[7][:, 0:3], 3, D_MODEL)

                def pair(j, i=None, first=False):
                    s, t = S("gu") + 2 * j, TL("gu") + 2 * j
                    per = 0 if i is None else RING
                    o = 0 if i is None else per * i
                    p = 0 if i is None else 4 * i
                    J = FC * l + j
                    split(s + HI_AHEAD, i, per)
                    if not first:
                        hi_ff(j - 1, i)
                    act.wait_ge(tile_free, t + 1 + o)
                    if J >= 2:
                        act.wait_ge(ff_prod, J - 1 + p)
                    act.activation(sbuf_[:, j % 2, t0:], gbuf[:, j % 2, t0:], ACT.Silu).then_inc(silu_done, 1)
                    split(s + 1 + HI_AHEAD, i, per)

                def hi_ff(j, i=None):
                    p = 0 if i is None else 4 * i
                    act.wait_ge(ff_prod, FC * l + j + 1 + p)
                    dst = ff_hi[:, j, t0:] if i is None else ff_hi[:, bass.ds(4 * i + j, 1), t0:]
                    src = pbuf[:, j % 2, t0:] if i is None else pbuf[:, j % 2:j % 2 + 1, t0:]
                    act.activation(dst, src, ACT.Copy).then_inc(ff_hi_ready, 1)

                pair(0, first=True)
                pair(1)
                with act.Fori(0, 5) as i:
                    for j in range(2, 6):
                        pair(j, i)
                hi_ff(21)
                TD, SD = TL("down"), S("down")

                def down(m, i=None):
                    per = 0 if i is None else RING
                    for j in range(4):
                        split(SD + 4 * m + j + HI_AHEAD, i, per)
                for m in range(KC):
                    down(m)
                    square_tile(K0 + POST_FFN, TD + m, m)
                root(K0 + POST_FFN, ps[7][:, 0:3], 3, D_MODEL)
                if l < DEPTH - 1:
                    boundary(2 * l + 2, K0 + NORMS + PRE_MIX, G_MIXPRE, l + 1)

        @block.gpsimd
        def _(pool):
            def sum_squares(K, t0):
                for c in range(1, CHUNKS[K % NORMS] - 1):
                    pool.wait_ge(sq_ready, plan.sq0[K] + c + 1)
                    if c > 1:
                        pool.wait_ge(sq_added, plan.add0[K] + c - 1)
                    pool.tensor_tensor(acc[:, K % 2, t0:], acc[:, K % 2, t0:], sq[:, plan.sq_place[K, c], t0:], ALU.add).then_inc(sq_added, 1)

            def rope_add(l, i, dst, src):
                if i == 0:
                    pool.wait_ge(sq_added, plan.add0[NORMS * l + NKV] + KVC - 2)
                else:
                    pool.wait_ge(rope_done, 5 * l + i)
                pool.wait_ge(rope_in, 5 * l + i + 1)
                pool.tensor_tensor(dst, dst, src, ALU.add).then_inc(rope_done, 1)

            sum_squares(0, 0)
            for l in range(DEPTH):
                t0, K0 = T0(l), NORMS * l
                sum_squares(K0 + NQ, t0)
                sum_squares(K0 + NKV, 0)
                rope_add(l, 0, krope[64:96, :], b_t[64:96, 0, :])
                rope_add(l, 1, dqk[:, 0:4, t0:], b_t[:, 0:4, t0:])
                rope_add(l, 2, dqk[:, 4:8, :], b_t[:, 0:4, :])
                rope_add(l, 3, q_t[64:96, 0:4, t0:], b_t[64:96, 0:4, t0:])
                rope_add(l, 4, q_t[64:96, 4:8, t0:], b_t[64:96, 0:4, t0:])
                pool.wait_ge(rope_done, 5 * (l + 1))
                for m in range(KC):
                    pool.wait_ge(tile_free, plan.tile[l, "ob", m] + 1)
                    pool.tensor_tensor(gates[:, 8 + m, t0:], gates[:, 8 + m, t0:], gates[:, m, t0:], ALU.add).then_inc(mix_ready, 1)
                sum_squares(K0 + POST_MIX, t0)
                sum_squares(K0 + PRE_FFN, t0)

                def product(j, i=None):
                    o = 0 if i is None else RING * i
                    p = 0 if i is None else 4 * i
                    J = FC * l + j
                    pool.wait_ge(silu_done, J + 1 + p)
                    pool.wait_ge(tile_free, plan.tile[l, "gu", 0] + 2 * j + 2 + o)
                    if J >= 2:
                        pool.wait_ge(ff_lo_ready, J - 1 + p)
                    pool.tensor_tensor(pbuf[:, j % 2, t0:], sbuf_[:, j % 2, t0:], ubuf[:, j % 2, t0:], ALU.mult).then_inc(ff_prod, 1)

                product(0)
                product(1)
                with pool.Fori(0, 5) as i:
                    for j in range(2, 6):
                        product(j, i)
                sum_squares(K0 + POST_FFN, t0)
                if l < DEPTH - 1:
                    sum_squares(K0 + NORMS + PRE_MIX, 0)

        @block.vector
        def _(dve):
            steps = [0]

            def step(ins):
                steps[0] += 1
                ins.then_inc(dve_step, 1)
                return steps[0]

            def after(v):
                dve.wait_ge(dve_step, v)

            def split(n, i=None, per=0):
                if n >= plan.slots:
                    return
                u = 0 if i is None else per * i
                dve.wait_ge(hi_ready, n + 1 + u)
                dve.tensor_tensor(w_lo[:, n % RING, :], w_raw[:, n % RAW, :], w_hi[:, n % RING, :].bitcast(f32),
                                  ALU.subtract).then_inc(lo_ready, 1)

            def recip(K, n=3):
                dve.wait_ge(norm_std, K + 1)
                if K >= 2:
                    dve.wait_ge(norm_bc, K - 1)
                dve.reciprocal(rec[K % 2][:, 0:n], std[K % 2][:, 0:n]).then_inc(norm_rec, 1)

            def take(K, bank, dst, t0):
                dve.wait_ge(norm_bc, K + 1)
                dve.tensor_copy(dst[:, t0:], ps[bank][:, 64 + t0:64 + TOK]).then_inc(norm_ready, 1)

            def evac(t, dst, factor, rows=slice(0, P), t0=0):
                dve.wait_ge(pe_done, plan.tile_done[t])
                dve.tensor_tensor(dst, ps[t % BANKS][rows, t0:TOK], factor, ALU.mult).then_inc(tile_free, 1)

            def lo_part(b, c, g, l, t0):
                dve.wait_ge(h_hi, KC * b + c + 1)
                dve.scalar_tensor_tensor(out=hl[:, c, t0:], in0=r[:, c, t0:], scalar=gain[:, l, g + c:g + c + 1],
                                         in1=hh[:, c, t0:].bitcast(f32), op0=ALU.mult, op1=ALU.subtract).then_inc(h_lo, 1)

            def residual(b, K, gp, lp, t0):
                last = b == 2 * DEPTH
                for c in range(KC):
                    if c:
                        dve.wait_ge(r_ready, KC * (b - 1) + c)
                    ins = dve.scalar_tensor_tensor(out=tres[:, t0:], in0=y[:, c, t0:], scalar=gain[:, lp, gp + c:gp + c + 1],
                                                   in1=ps[7][:, 64 + t0:64 + TOK], op0=ALU.mult, op1=ALU.mult)
                    if c < KC - 1:
                        after(step(ins))
                    else:
                        ins.then_inc(norm_ready, 1)
                        dve.wait_ge(norm_ready, K + 1)
                    dve.tensor_tensor(r[:, c, t0:], r[:, c, t0:], tres[:, t0:], ALU.add).then_inc(r_ready, 1)
                    if not last and c:
                        lo_part(b, c - 1, *nxt(b), t0)
                if not last:
                    lo_part(b, KC - 1, *nxt(b), t0)

            def nxt(b):
                return (G_FFNPRE, b // 2) if b % 2 else (G_MIXPRE, b // 2)

            dve.memset(eps, EPS).then_inc(const_ready, 1)
            dve.memset(ones, 1.0)
            dve.wait_ge(gain_in, 16)
            for c in range(KC):
                lo_part(0, c, G_MIXPRE, 0, 0)
                if c in (1, 2):
                    split(c - 1)
            split(2)
            split(3)
            split(4)
            split(5)
            recip(PRE_MIX)
            take(PRE_MIX, 7, rstd_h, 0)
            def lambda_sums():
                dve.wait_ge(id_in, 16)
                dve.wait_ge(mask_in, 32)
                dve.tensor_copy(identb[:, :], ident)
                dve.tensor_copy(maskb[:, :], stage[:, 0, 0:P])
                dve.tensor_copy(maskmb[:, 0:128], stage[0:16, 0, 128:256])
                dve.tensor_copy(maskmb[:, 128:256], stage[0:16, 1, 0:128]).then_inc(const_ready, 1)
                for l in range(DEPTH):
                    for j in range(2):
                        o = 128 * j
                        v = step(dve.tensor_tensor(tres[:, 0:64], lam_raw[:, l, o:o + 64], lam_raw[:, l, o + 64:o + 128], ALU.mult))
                        after(v)
                        v = step(dve.reduce_sum(lamp[:, 2 * l + j:2 * l + j + 1], tres[:, 0:64], AX.X))
                        after(v)
                dve.memset(idle, 0.0).then_inc(lam_ready, 1)

            def lambdas():
                dve.wait_ge(lam_exp, 1)
                for l in range(DEPTH):
                    v = step(dve.tensor_tensor(neglam[:, l:l + 1], lam_e[:, 2 * l + 1:2 * l + 2], lam_e[:, 2 * l:2 * l + 1], ALU.subtract))
                    after(v)
                    step(dve.tensor_scalar(neglam[:, l:l + 1], neglam[:, l:l + 1], LAM_INIT[l], None, ALU.subtract))
                    step(dve.tensor_scalar(gsub[:, l:l + 1], gain[:, l, G_SUB:G_SUB + 1], 1.0 - LAM_INIT[l], None, ALU.mult))
                after(steps[0])
                dve.memset(idle, 0.0).then_inc(const_ready, 1)

            for l in range(DEPTH):
                t0, K0 = T0(l), NORMS * l
                S = lambda name, i=0: plan.slot[l, name, i]
                TL = lambda name, i=0: plan.tile[l, name, i]
                if l:
                    split(S("lat") + AHEAD)
                    recip(K0 + PRE_MIX)
                    take(K0 + PRE_MIX, 7, rstd_h, 0)
                dve.wait_ge(norm_ready, K0 + PRE_MIX + 1)

                def rotary_factors():
                    for dst, tab in ((rc_d, cos_d), (rs_d, sin_d)):
                        step(dve.tensor_tensor(dst[:, :], rstd_h[:, :], tab, ALU.mult))
                    for dst, tab in ((rc_q, cos_m), (rs_q, sin_m)):
                        v = step(dve.tensor_tensor(dst[64:96, :], rstd_h[64:96, :], tab[64:96, :], ALU.mult))
                    after(v)

                for i in range(5):
                    if i or not l:
                        split(S("lat") + i + AHEAD)
                    c0 = t0 if i < QC else 0
                    if i >= 2 or l:
                        K = K0 + NQ if i < QC else K0 + NKV
                        prev = plan.sq0[K0 + NQ] + i - 1 if i >= 2 else plan.sq0[K0 - NORMS + NKV] + 2
                        dve.wait_ge(sq_ready, prev)
                    evac(TL("lat") + i, lat[:, i % 2, c0:], rstd_h[:, c0:], t0=c0)
                    dve.wait_ge(lat_ready_hi, 5 * l + i + 1)
                    dve.scalar_tensor_tensor(out=lat_lo[:, i, c0:], in0=lat[:, i % 2, c0:], scalar=gain[:, l, G_Q + i:G_Q + i + 1],
                                             in1=lat_hi[:, i, c0:].bitcast(f32), op0=ALU.mult, op1=ALU.subtract).then_inc(lat_ready_lo, 1)
                    if i == 3 and l == 0:
                        lambda_sums()
                if l == 0:
                    dve.wait_ge(tables_in, 16)
                rotary_factors()
                split(S("lat") + 5 + AHEAD)
                t = TL("lat") + 5
                swap_m = [(i + 16) % 32 for i in range(32)]
                swap_d = [(i + 8) % 16 if i < 16 else i for i in range(32)]
                dve.wait_ge(pe_done, plan.tile_done[t])
                v = step(dve.tensor_tensor(b_t[64:96, 0, :], ps[t % BANKS][64:96, 0:TOK], rs_q[64:96, :], ALU.mult))
                evac(t, krope[64:96, :], rc_q[64:96, :], rows=slice(64, 96))
                after(v)
                dve.wait_ge(tile_free, t + 1)
                dve.stream_shuffle(b_t[64:96, 0, :], b_t[64:96, 0, :], swap_m).then_inc(rope_in, 1)
                if l == 0:
                    lambdas()
                for st, base_c, rope_i in (("dq", 0, 1), ("dk", 4, 2)):
                    c0 = t0 if st == "dq" else 0
                    dve.wait_ge(rope_done, 5 * l + rope_i)
                    for i in range(4):
                        split(S(st) + i + AHEAD)
                        t = TL(st) + i
                        dve.wait_ge(pe_done, plan.tile_done[t])
                        v = step(dve.tensor_tensor(b_t[:, i, c0:], ps[t % BANKS][:, c0:TOK], rs_d[:, c0:], ALU.mult))
                        evac(t, dqk[:, base_c + i, c0:], rc_d[:, c0:], t0=c0)
                        if st == "dq" and i == 3:
                            recip(K0 + NQ)
                            recip(K0 + NKV)
                        if st == "dk" and i == 1:
                            take(K0 + NQ, 7, rstd_q, t0)
                            take(K0 + NKV, 6, rstd_kv, 0)
                            dve.wait_ge(norm_ready, K0 + NKV + 1)
                            v = step(dve.tensor_tensor(rc_q[0:96, t0:], rstd_q[0:96, t0:], cos_m[0:96, t0:], ALU.mult))
                            v = step(dve.tensor_tensor(rs_q[64:96, t0:], rstd_q[64:96, t0:], sin_m[64:96, t0:], ALU.mult))
                    after(v)
                    dve.wait_ge(tile_free, TL(st) + 4)
                    dve.stream_shuffle(b_t[:, :, c0:], b_t[:, :, c0:], swap_d).then_inc(rope_in, 1)
                dve.wait_ge(kr_ready, l + 1)
                for st, i in TURNS:
                    split(S(st, i) + AHEAD)
                    if st == "dv":
                        evac(TL("dv", i), dv_t[:, i, :], rstd_h[:, :])
                    elif st == "ukv":
                        for h in range(4 * i, 4 * i + 4):
                            evac(TL("ukv", h), kv_t[:, h, :], rstd_kv[:, :])
                    else:
                        for h in range(3 * i, min(3 * i + 3, MLA_HEADS)):
                            if h % 4 == 0:
                                dve.wait_ge(rope_done, 5 * l + 3 + h // 4)
                            t = TL("uq", h)
                            dve.wait_ge(pe_done, plan.tile_done[t])
                            v = step(dve.tensor_tensor(b_t[64:96, h % 4, t0:], ps[t % BANKS][64:96, t0:TOK], rs_q[64:96, t0:], ALU.mult))
                            evac(t, q_t[0:96, h, t0:], rc_q[0:96, t0:], rows=slice(0, 96), t0=t0)
                            if h % 4 == 3:
                                after(v)
                                dve.wait_ge(tile_free, t + 1)
                                dve.stream_shuffle(b_t[64:96, :, t0:], b_t[64:96, :, t0:], swap_m).then_inc(rope_in, 1)

                def gate(i):
                    evac(TL("gate") + i, gates[:, i, t0:], rstd_h[:, t0:], t0=t0)

                def unit_maps(u):
                    return [(4, 0, 0), (5, 1, 2)] if u < DIFF_HEADS else [(4 + u % 2, u % 2, 0)]

                def negmax(u):
                    U = UNITS * l + u
                    dve.wait_ge(scores_ready, U + 1)
                    if U >= 2:
                        dve.wait_ge(probs_ready, U - 1)
                    scale = DIFF_SCALE if u < DIFF_HEADS else MLA_SCALE
                    for bank, e, s in unit_maps(u):
                        dve.reduce_max(mx[u % 2][:, s:s + 1], ps[bank][:, 0:144], AX.X)
                        v = step(dve.reduce_max(mx[u % 2][:, s + 1:s + 2], ps[bank][:, 144:416], AX.X))
                        after(v)
                        dve.tensor_scalar(mx[u % 2][:, s:s + 2], mx[u % 2][:, s:s + 2], -scale, None, ALU.mult).then_inc(negmax_ready, 1)

                def probs(u):
                    M = MAPS * l + first_map(u)
                    s = sm[u % 2]
                    e = unit_maps(u)[0][1]
                    dve.wait_ge(exp_ready, M + 1)
                    v = step(dve.reciprocal(s[:, 0:2], s[:, 0:2]))
                    after(v)
                    step(dve.tensor_scalar(e_t[:, e, 0:144], e_t[:, e, 0:144], s[:, 0:1], None, ALU.mult))
                    ins = dve.tensor_scalar(e_t[:, e, 144:416], e_t[:, e, 144:416], s[:, 1:2], None, ALU.mult)
                    if u >= DIFF_HEADS:
                        ins.then_inc(probs_ready, 1)
                        return
                    step(ins)
                    dve.wait_ge(exp_ready, M + 2)
                    v = step(dve.reciprocal(s[:, 2:4], s[:, 2:4]))
                    after(v)
                    v = step(dve.tensor_scalar(s[:, 2:4], s[:, 2:4], neglam[:, l:l + 1], None, ALU.mult))
                    after(v)
                    for part, (a, b) in enumerate(((0, 144), (144, 416))):
                        ins = dve.scalar_tensor_tensor(out=e_t[:, 0, a:b], in0=e_t[:, 1, a:b], scalar=s[:, 2 + part:3 + part],
                                                       in1=e_t[:, 0, a:b], op0=ALU.mult, op1=ALU.add)
                    ins.then_inc(probs_ready, 1)

                def out_part(u):
                    if u < DIFF_HEADS:
                        dve.wait_ge(pv_ready, UNITS * l + u + 1)
                        dve.tensor_copy(od[:, u, t0:], ps[7][:, t0:TOK]).then_inc(out_copied, 1)
                    else:
                        h = u - DIFF_HEADS
                        o = 64 * (h % 2)
                        dve.wait_ge(out_hi, MLA_HEADS * l + h + 1)
                        dve.tensor_tensor(am_lo[o:o + 64, h // 2, t0:], ps[7][o:o + 64, t0:TOK], am_hi[o:o + 64, h // 2, t0:].bitcast(f32),
                                          ALU.subtract).then_inc(out_copied, 1)

                for i in range(16):
                    u = i - 4
                    if u < 0:
                        split(S("gate") + i + AHEAD)
                        if i == 3 and l == 0:
                            m3 = lambda a: a.rearrange("p (a b) -> p a b", a=16)
                            dve.wait_ge(meta_scores, 1)
                            v = step(dve.reduce_max(mxm, m3(ps[7][0:16, 0:256]), AX.X))
                            after(v)
                            dve.tensor_tensor(m3(pm[:, 0, :]), m3(ps[7][0:16, 0:256]), mxm[:, :, None].to_broadcast([16, 16, 16]),
                                              ALU.subtract).then_inc(meta_shift, 1)
                            dve.wait_ge(meta_exp, 1)
                            v = step(dve.reduce_sum(mxm, m3(pm[:, 1, :]), AX.X))
                            after(v)
                            v = step(dve.reciprocal(mxm, mxm))
                            after(v)
                            v = step(dve.tensor_scalar(mxm[:, 12:16], mxm[:, 12:16], neglam[0:16, 0:1], None, ALU.mult))
                            after(v)
                            v = step(dve.tensor_tensor(m3(pm[:, 2, :]), m3(pm[:, 1, :]), mxm[:, :, None].to_broadcast([16, 16, 16]), ALU.mult))
                            after(v)
                            dve.tensor_tensor(pm[:, 2, 128:192], pm[:, 2, 128:192], pm[:, 2, 192:256], ALU.add).then_inc(meta_probs, 1)
                        gate(i)
                        continue
                    negmax(u)
                    probs(u)
                    if u >= 1:
                        out_part(u - 1)
                    split(S("gate") + i + AHEAD)
                    gate(i)
                out_part(UNITS - 1)
                K = K0 + NDIFF
                recip(K, 12)
                dve.wait_ge(sig_ready, 2 * l + 1)
                for m in range(KC):
                    if m % 2 == 0:
                        split(S("oa") + m // 2 + AHEAD)
                    evac(TL("oa") + m, gates[:, m, t0:], gates[:, m, t0:], t0=t0)
                    if m == 2:
                        dve.wait_ge(norm_bc, K + 1)
                        for d in range(DIFF_HEADS):
                            dve.tensor_tensor(od[:, d, t0:], ps[4 + d][:, 64 + t0:64 + TOK], od[:, d, t0:], ALU.mult).then_inc(od_ready, 1)
                    if m in (4, 5):
                        for d in (2 * m - 8, 2 * m - 7):
                            dve.wait_ge(od_hi_ready, DIFF_HEADS * l + d + 1)
                            dve.scalar_tensor_tensor(out=od_lo[:, d, t0:], in0=od[:, d, t0:], scalar=gsub[:, l:l + 1],
                                                     in1=od_hi[:, d, t0:].bitcast(f32), op0=ALU.mult, op1=ALU.subtract).then_inc(od_lo_ready, 1)
                dve.memset(idle, 0.0).then_inc(norm_ready, 1)

                def mix_low(m):
                    dve.wait_ge(mix_hi, KC * l + m + 1)
                    dve.tensor_tensor(hl[:, m, t0:], gates[:, 8 + m, t0:], hh[:, m, t0:].bitcast(f32), ALU.subtract).then_inc(mix_lo, 1)

                dve.wait_ge(sig_ready, 2 * l + 2)
                for m in range(KC):
                    if m % 2 == 0:
                        split(S("ob") + m // 2 + AHEAD)
                    evac(TL("ob") + m, gates[:, 8 + m, t0:], gates[:, 8 + m, t0:], t0=t0)
                    if m >= 2:
                        mix_low(m - 2)
                mix_low(KC - 2)
                mix_low(KC - 1)

                def to_y(K, t, m):
                    if m < KC - 1:
                        dve.wait_ge(pe_done, plan.tile_done[t])
                    else:
                        dve.wait_ge(sq_ready, plan.sq0[K] + KC)
                    dve.tensor_copy(y[:, m, t0:], ps[t % BANKS][:, t0:TOK]).then_inc(tile_free, 1)

                for m in range(KC):
                    split(S("out") + m + AHEAD)
                    to_y(K0 + POST_MIX, TL("out") + m, m)
                recip(K0 + POST_MIX)
                dve.wait_ge(norm_bc, K0 + POST_MIX + 1)
                residual(2 * l + 1, K0 + POST_MIX, G_MIXPOST, l, t0)
                split(S("gu") + AHEAD)
                recip(K0 + PRE_FFN)
                take(K0 + PRE_FFN, 7, rstd_h, t0)
                dve.wait_ge(norm_ready, K0 + PRE_FFN + 1)

                def pair(j, i=None, first=False):
                    s, t = S("gu") + 2 * j, TL("gu") + 2 * j
                    o = 0 if i is None else RING * i
                    p = 0 if i is None else 4 * i
                    J = FC * l + j
                    if not first:
                        split(s + AHEAD, i, RING)
                    for k, buf in ((0, gbuf), (1, ubuf)):
                        dve.wait_ge(pe_done, plan.tile_done[t + k] + o)
                        if J >= 2:
                            dve.wait_ge(ff_prod if k else silu_done, J - 1 + p)
                        dve.tensor_tensor(buf[:, j % 2, t0:], ps[(t + k) % BANKS][:, t0:TOK], rstd_h[:, t0:], ALU.mult).then_inc(tile_free, 1)
                        if k == 0:
                            split(s + 1 + AHEAD, i, RING)
                    if not first:
                        lo_ff(j - 1, i)

                def lo_ff(j, i=None):
                    p = 0 if i is None else 4 * i
                    dve.wait_ge(ff_hi_ready, FC * l + j + 1 + p)
                    at_j = slice(j, j + 1) if i is None else bass.ds(4 * i + j, 1)
                    dve.tensor_tensor(ff_lo[:, at_j, t0:], pbuf[:, j % 2:j % 2 + 1, t0:], ff_hi[:, at_j, t0:].bitcast(f32),
                                      ALU.subtract).then_inc(ff_lo_ready, 1)

                pair(0, first=True)
                pair(1)
                with dve.Fori(0, 5) as i:
                    for j in range(2, 6):
                        pair(j, i)
                lo_ff(21)
                for m in range(KC):
                    for j in range(4):
                        split(S("down") + 4 * m + j + AHEAD)
                    to_y(K0 + POST_FFN, TL("down") + m, m)
                recip(K0 + POST_FFN)
                dve.wait_ge(norm_bc, K0 + POST_FFN + 1)
                residual(2 * l + 2, K0 + POST_FFN, G_FFNPOST, l, t0)

        @block.tensor
        def _(pe):
            def slot_ready(n, i=None):
                pe.wait_ge(lo_ready, n + 1 + (0 if i is None else RING * i))

            def bank_free(t, i=None, per=0):
                if t >= BANKS:
                    pe.wait_ge(tile_free, t - BANKS + 1 + (0 if i is None else per * i))

            def block(t, n, at, width, hi, lo, t0, first, last):
                dst = ps[t % BANKS][0:width, t0:TOK]
                wh, wl = (w[:, n % RING, at:at + width] for w in (w_hi, w_lo))
                pe.matmul(dst, wh, hi, start=first, stop=False)
                pe.matmul(dst, wh, lo, start=False, stop=False)
                return pe.matmul(dst, wl, hi, start=False, stop=last)

            def tile(t, n, at, width, src, t0, wait=None, i=None, per=0):
                bank_free(t, i, per)
                for k, (a, b) in enumerate(src):
                    if wait:
                        pe.wait_ge(wait[0], wait[1] + k + 1)
                    mm = block(t, n, at + k * width, width, a, b, t0, k == 0, k == len(src) - 1)
                mm.then_inc(pe_done, 1)

            def first_tiles(tiles, wait, before_last=None):
                slot_ready(tiles[-1][1])
                bank_free(tiles[-1][0])
                for k in range(KC):
                    if before_last and k == KC - 1:
                        before_last()
                    pe.wait_ge(wait[0], wait[1] + k + 1)
                    for t, n, src, t0 in tiles:
                        mm = block(t, n, k * P, P, *src[k], t0, k == 0, k == KC - 1)
                        if k == KC - 1:
                            mm.then_inc(pe_done, 1)

            def sums(K, a, bank, col, srcs, count=True):
                for c, (t_a, t_b) in enumerate(CH):
                    if a > t_a:
                        t_a = a
                    for s, src in enumerate(srcs):
                        mm = pe.matmul(ps[bank][:, col + c:col + c + 1], src[:, t_a:t_a + P], ones, start=s == 0, stop=s == len(srcs) - 1)
                if count:
                    mm.then_inc(norm_sum, 1)

            def norm_sums(K, bank, t0):
                k = K % NORMS
                pe.wait_ge(sq_ready, plan.sq0[K] + CHUNKS[k])
                if CHUNKS[k] > 2:
                    pe.wait_ge(sq_added, plan.add0[K] + CHUNKS[k] - 2)
                before = K - 1 if k == NKV else K
                if before > 0:
                    pe.wait_ge(norm_ready, before)
                sums(K, t0, bank, 0, [acc[:, K % 2, :], sq[:, plan.sq_place[K, CHUNKS[k] - 1], :]])

            def spread(K, bank, t0, col=0, dst=None, count=True):
                for c, (a, b) in enumerate(CH):
                    if t0 > a:
                        continue
                    n = b - a
                    mm = pe.matmul(ps[bank][:, 64 + a:64 + b], rec[K % 2][0:n, col + c:col + c + 1].to_broadcast([n, P]),
                                   ident[0:n, 0:n], start=True, stop=True)
                if count:
                    mm.then_inc(norm_bc, 1)

            def norm_spread(K, bank, t0):
                pe.wait_ge(norm_rec, K + 1)
                spread(K, bank, t0)

            for l in range(DEPTH):
                t0, K0 = T0(l), NORMS * l
                S = lambda name, i=0: plan.slot[l, name, i]
                TL = lambda name, i=0: plan.tile[l, name, i]
                full = [(hh[:, k, :], hl[:, k, :]) for k in range(KC)]
                late = [(hh[:, k, t0:], hl[:, k, t0:]) for k in range(KC)]
                if l == 0:
                    first_tiles([(TL("lat") + q, S("lat") + q, late, t0) for q in range(2)], (h_lo, 0))
                    norm_sums(K0 + PRE_MIX, 7, 0)
                    slot_ready(S("lat") + 2)
                    tile(TL("lat") + 2, S("lat") + 2, 0, P, late, t0)
                    pe.wait_ge(id_in, 16)
                    norm_spread(K0 + PRE_MIX, 7, 0)
                    slot_ready(S("lat") + 3)
                    tile(TL("lat") + 3, S("lat") + 3, 0, P, full, 0)
                else:
                    first_tiles([(TL("lat") + q, S("lat") + q, *((late, t0) if q < QC else (full, 0))) for q in range(BANKS)],
                                (h_lo, KC * 2 * l), lambda: norm_sums(K0 + PRE_MIX, 7, 0))
                    norm_spread(K0 + PRE_MIX, 7, 0)
                for i in range(4, 6):
                    slot_ready(S("lat") + i)
                    tile(TL("lat") + i, S("lat") + i, 0, P if i < 5 else HW, full, 0)
                for st in ("dq", "dk"):
                    for i in range(4):
                        slot_ready(S(st) + i)
                        tile(TL(st) + i, S(st) + i, 0, P, late if st == "dq" else full, t0 if st == "dq" else 0)
                        if st == "dq" and i == 3:
                            norm_sums(K0 + NQ, 7, t0)
                            norm_sums(K0 + NKV, 6, 0)
                        if st == "dk" and i == 0:
                            norm_spread(K0 + NQ, 7, t0)
                            norm_spread(K0 + NKV, 6, 0)
                pe.wait_ge(lat_ready_lo, 5 * (l + 1))
                qsrc = [(lat_hi[:, k, t0:], lat_lo[:, k, t0:]) for k in range(QC)]
                kvsrc = [(lat_hi[:, QC + k, :], lat_lo[:, QC + k, :]) for k in range(KVC)]
                for st, i in TURNS:
                    n = S(st, i)
                    slot_ready(n)
                    if st == "dv":
                        tile(TL("dv", i), n, 0, P, full, 0)
                    elif st == "uq":
                        for h in range(3 * i, min(3 * i + 3, MLA_HEADS)):
                            tile(TL("uq", h), n, (h % 3) * QC * HW, HW, qsrc, t0)
                    else:
                        for h in range(4 * i, 4 * i + 4):
                            tile(TL("ukv", h), n, (h % 4) * KVC * P, P, kvsrc, 0)

                def v_transposes(g):
                    if g == 0:
                        pe.wait_ge(norm_ready, K0 + NKV + 1)
                        pe.wait_ge(tile_free, TL("dv", 3) + 1)
                    else:
                        pe.wait_ge(tile_free, TL("ukv", 4 * g - 1) + 1)
                        pe.wait_ge(v_copied, 9 * l + 3 * g)
                    for c, (a, b) in enumerate(CH):
                        for s in range(4):
                            src = dv_t[:, s, a:a + P] if g == 0 else kv_t[:, 4 * (g - 1) + s, a:a + P]
                            mm = pe.transpose(ps[4 + c][:, s * P:(s + 1) * P], src, ident)
                    mm.then_inc(v_ready, 1)

                def qk(u, a, b):
                    if u < DIFF_HEADS:
                        return [(dqk[o:o + 64, u, a:b], dqk[o:o + 64, 4 + u, :]) for o in (0, 64)]
                    h = u - DIFF_HEADS
                    return [(q_t[0:96, h, a:b], k_t[0:96, h, :])]

                def keys_ready():
                    pe.wait_ge(rope_done, 5 * (l + 1))
                    pe.wait_ge(kr_ready, l + 1)
                    pe.wait_ge(k_copied, MLA_HEADS * (l + 1))

                def meta_rows():
                    pe.matmul(ps[7][0:16, 0:256], identb[0:16, 0:16], maskmb[:, :], start=True, stop=False)
                    maps = [(q, k) for u_ in range(4, 12) for q, k in qk(u_, 0, 16)]
                    maps += [qk(u_, 0, 16)[s] for s in range(2) for u_ in range(4)]
                    for m, (q, k) in enumerate(maps):
                        mm = pe.matmul(ps[7][0:16, 16 * m:16 * m + 16], q, k[:, 0:16], start=False, stop=m == 15)
                        if m == 11:
                            mm.then_inc(meta_half, 1)
                            pe.wait_ge(meta_half, 1)
                    mm.then_inc(meta_scores, 1)

                def scores(u):
                    U = UNITS * l + u
                    if U:
                        pe.wait_ge(exp_ready, MAPS * l + first_map(u))
                    for m, (q_a, k) in enumerate(qk(u, 16, 144)):
                        q_b = qk(u, 144, 272)[m][0]
                        bank = ps[4 + m] if u < DIFF_HEADS else ps[4 + u % 2]
                        for q, c0, n in ((q_a, 0, 144), (q_b, 144, 272)):
                            pe.matmul(bank[:, c0:c0 + n], q, k[:, 0:n], start=True, stop=False)
                            mm = pe.matmul(bank[:, c0 + n - P:c0 + n], identb[:, :], maskb[:, :], start=False, stop=True)
                    mm.then_inc(scores_ready, 1)

                def transposes(u):
                    U = UNITS * l + u
                    pe.wait_ge(probs_ready, U + 1)
                    if U == 0:
                        pe.wait_ge(meta_copied, 1)
                    if U:
                        pe.wait_ge(out_copied, U)
                    e = e_t[:, 0 if u < DIFF_HEADS else u % 2, :]
                    for col, src in ((0, 0), (128, 144), (256, 16), (384, 160)):
                        pe.transpose(ps[6][:, col:col + P], e[:, src:src + P], ident)
                    pe.transpose(ps[7][:, 384:512], e[:, 288:416], ident).then_inc(pt_ready, 1)

                def pv(u):
                    U = UNITS * l + u
                    pe.wait_ge(pt_copied, U + 1)
                    if u < DIFF_HEADS:
                        o, n, col = 0, P, P * u
                    else:
                        h = u - DIFF_HEADS
                        o, n, col = 64 * (h % 2), 64, 512 + 64 * h
                    b = u % 2
                    pe.matmul(ps[7][o:o + n, t0:TOK], v_tok[0:16, 0, col:col + n], pt0[0:16, b, t0:], start=True, stop=False)
                    pe.matmul(ps[7][o:o + n, 16:TOK], v_tok[:, 1, col:col + n], pt1[:, b, :], start=False, stop=False)
                    pe.matmul(ps[7][o:o + n, 144:TOK], v_tok[:, 2, col:col + n], pt2[:, b, :], start=False, stop=True).then_inc(pv_ready, 1)

                for i in range(16):
                    u = i - 4
                    if u >= 0:
                        if u == 0:
                            pe.wait_ge(v_copied, 9 * (l + 1))
                        scores(u)
                        if u:
                            pv(u - 1)
                    slot_ready(S("gate") + i)
                    tile(TL("gate") + i, S("gate") + i, 0, P, late, t0)
                    if u >= 0:
                        transposes(u)
                    elif i < 3:
                        v_transposes(i)
                        if i == 2:
                            keys_ready()
                            if l == 0:
                                pe.wait_ge(const_ready, 2)
                                meta_rows()
                    elif l == 0:
                        pe.wait_ge(meta_probs, 1)
                        for u_ in range(UNITS):
                            m = 8 + u_ if u_ < DIFF_HEADS else u_ - DIFF_HEADS
                            mm = pe.matmul(ps[7][0:16, 256 + 16 * u_:272 + 16 * u_], pm[:, 2, 16 * m:16 * m + 16], ident[0:16, 0:16],
                                           start=True, stop=True)
                        mm.then_inc(meta_pt, 1)
                K = K0 + NDIFF
                pe.wait_ge(od_squared, l + 1)
                for d in range(DIFF_HEADS):
                    sums(K, t0, 4, 3 * d, [b_t[:, d, :]], d == DIFF_HEADS - 1)
                pv(UNITS - 1)
                src = [(am_hi[:, k, t0:], am_lo[:, k, t0:]) for k in range(4)]
                pe.wait_ge(out_copied, UNITS * (l + 1))
                for m in range(KC):
                    if m % 2 == 0:
                        slot_ready(S("oa") + m // 2)
                    tile(TL("oa") + m, S("oa") + m // 2, (m % 2) * 4 * P, P, src, t0)
                    if m == 2:
                        pe.wait_ge(norm_rec, K + 1)
                        for d in range(DIFF_HEADS):
                            spread(K, 4 + d, t0, 3 * d, count=d == DIFF_HEADS - 1)
                src = [(od_hi[:, k, t0:], od_lo[:, k, t0:]) for k in range(4)]
                pe.wait_ge(od_lo_ready, DIFF_HEADS * (l + 1))
                for m in range(KC):
                    if m % 2 == 0:
                        slot_ready(S("ob") + m // 2)
                    tile(TL("ob") + m, S("ob") + m // 2, (m % 2) * 4 * P, P, src, t0)
                first_tiles([(TL("out") + q, S("out") + q, late, t0) for q in range(2)], (mix_lo, KC * l))
                for m in range(2, KC):
                    slot_ready(S("out") + m)
                    tile(TL("out") + m, S("out") + m, 0, P, late, t0)
                norm_sums(K0 + POST_MIX, 7, t0)
                norm_spread(K0 + POST_MIX, 7, t0)
                g0, gt = S("gu"), TL("gu")
                first_tiles([(gt + q, g0 + q, late, t0) for q in range(BANKS)], (h_lo, KC * (2 * l + 1)),
                            lambda: norm_sums(K0 + PRE_FFN, 7, t0))
                norm_spread(K0 + PRE_FFN, 7, t0)
                with pe.Fori(0, 5) as i:
                    for j in range(4, 4 + RING):
                        slot_ready(g0 + j, i)
                        tile(gt + j, g0 + j, 0, P, late, t0, i=i, per=RING)
                d0, dt = S("down"), TL("down")
                for m in range(KC):
                    t = dt + m
                    bank_free(t)
                    k = 0
                    for j, cnt in enumerate(DOWN_SPLIT):
                        n = d0 + 4 * m + j
                        slot_ready(n)
                        for q in range(cnt):
                            if m == 0:
                                pe.wait_ge(ff_lo_ready, FC * l + k + 1)
                            mm = block(t, n, q * P, P, ff_hi[:, k, t0:], ff_lo[:, k, t0:], t0, k == 0, k == FC - 1)
                            k += 1
                        mm.then_inc(pe_done, 1)
                norm_sums(K0 + POST_FFN, 7, t0)
                norm_spread(K0 + POST_FFN, 7, t0)


def rope_table(rot, rows, period):
    half = rot // 2
    inv = (np.float32(THETA) ** (-np.arange(0, rot, 2, dtype=np.float32) / np.float32(rot))).astype(np.float32)
    ang = (np.arange(TOK, dtype=np.float32)[:, None] * inv[None, :]).astype(np.float32)
    c, s = np.cos(ang).T.astype(np.float32), np.sin(ang).T.astype(np.float32)
    cos, sin = np.ones((P, TOK), np.float32), np.zeros((P, TOK), np.float32)
    for p0 in range(rows, P, period):
        cos[p0:p0 + half], cos[p0 + half:p0 + rot] = c, c
        sin[p0:p0 + half], sin[p0 + half:p0 + rot] = s, -s
    return cos, sin


def constants():
    c = np.zeros((P, C_ALL), np.float32)
    c[:, C_ID:C_ID + P] = np.eye(P)
    c[:, C_MASK:C_MASK + P] = np.where(np.arange(P)[None, :] > np.arange(P)[:, None], MASKED, 0.0)
    m16 = np.where(np.arange(16)[None, :] > np.arange(16)[:, None], MASKED, 0.0)
    for m in range(16):
        c[0:16, C_MASKM + 16 * m:C_MASKM + 16 * m + 16] = m16
    c[:, C_COSD:C_COSD + TOK], c[:, C_SIND:C_SIND + TOK] = rope_table(DIFF_ROPE, 0, DIFF_DH)
    c[:, C_COSM:C_COSM + TOK], c[:, C_SINM:C_SINM + TOK] = rope_table(ROPE, NOPE, P)
    return c


def pack_weights(w_in, w_uq, w_ukv, w_oa, w_ob, w_out, w_gu, w_down):
    plan = Plan()
    packed = np.zeros((plan.slots, P, SLOT), np.float32)

    def blocks(w, k0, k1, c0, width):
        a = w[k0 * P:k1 * P, c0:c0 + width]
        return a.reshape(k1 - k0, P, width).transpose(1, 0, 2).reshape(P, (k1 - k0) * width)

    def put(n, parts):
        at = 0
        for a in parts:
            packed[n, :, at:at + a.shape[1]] = a
            at += a.shape[1]

    for l in range(DEPTH):
        S = lambda name, i=0: plan.slot[l, name, i]
        for i in range(5):
            put(S("lat") + i, [blocks(w_in[l], 0, KC, i * P, P)])
        put(S("lat") + 5, [blocks(w_in[l], 0, KC, Q_RANK + KV_RANK - NOPE, HW)])
        for st, o in (("dq", O_DQ), ("dk", O_DK), ("dv", O_DV)):
            for i in range(4):
                put(S(st, i), [blocks(w_in[l], 0, KC, o + i * P, P)])
        for h in range(MLA_HEADS):
            at = (h % 3) * QC * HW
            packed[S("uq", h // 3), :, at:at + QC * HW] = blocks(w_uq[l], 0, QC, h * HW, HW)
            at = (h % 4) * KVC * P
            packed[S("ukv", h // 4), :, at:at + KVC * P] = blocks(w_ukv[l], 0, KVC, h * P, P)
        for i in range(16):
            put(S("gate") + i, [blocks(w_in[l], 0, KC, O_G + i * P, P)])
        for i in range(4):
            put(S("oa") + i, [blocks(w_oa[l], 0, 4, (2 * i + q) * P, P) for q in range(2)])
            put(S("ob") + i, [blocks(w_ob[l], 0, 4, (2 * i + q) * P, P) for q in range(2)])
        for m in range(KC):
            put(S("out") + m, [blocks(w_out[l], 0, KC, m * P, P)])
        for j in range(FC):
            put(S("gu") + 2 * j, [blocks(w_gu[l], 0, KC, j * P, P)])
            put(S("gu") + 2 * j + 1, [blocks(w_gu[l], 0, KC, D_FF + j * P, P)])
        for m in range(KC):
            k = 0
            for j, cnt in enumerate(DOWN_SPLIT):
                put(S("down") + 4 * m + j, [blocks(w_down[l], k, k + cnt, m * P, P)])
                k += cnt
    return packed.reshape(plan.slots * P, SLOT)


def kernel(x, meta_tokens, norm_mix_pre, norm_mix_post, norm_ffn_pre, norm_ffn_post, w_in, mla_q_norm,
           mla_kv_norm, mla_w_uq, mla_w_ukv, w_o_mla, diff_lambda, diff_subln, w_o_diff, w_out, w_gate_up, w_down):
    import concourse.bacc as _bacc
    from concourse.bass_utils import run_bass_kernel_spmd as _run

    A = lambda a: np.asarray(a)
    tokens = np.concatenate([A(meta_tokens), A(x)[0]], axis=0)
    x_t = tokens.T.reshape(KC, P, TOK).transpose(1, 0, 2).reshape(P, KC * TOK)
    cols = [A(g).reshape(DEPTH, -1, P) for g in (norm_mix_pre, norm_mix_post, norm_ffn_pre, norm_ffn_post,
                                                 mla_q_norm, mla_kv_norm, diff_subln)]
    gains = np.concatenate(cols, axis=1).transpose(2, 0, 1).reshape(P, DEPTH * GAINS)
    lam = np.broadcast_to(A(diff_lambda).reshape(1, DEPTH * 4 * DIFF_DH), (P, DEPTH * 4 * DIFF_DH))
    packed = pack_weights(A(w_in), A(mla_w_uq), A(mla_w_ukv), A(w_o_mla), A(w_o_diff), A(w_out), A(w_gate_up), A(w_down))
    arrays = {"x_t": x_t, "weights": packed, "gains": gains, "lam": lam, "consts": constants()}
    arrays = {k: np.ascontiguousarray(v) for k, v in arrays.items()}
    f32 = mybir.dt.float32
    nc = _bacc.Bacc("TRN2", target_bir_lowering=False, num_devices=1)
    ins = [nc.dram_tensor(k, v.shape, f32, kind="ExternalInput").ap() for k, v in arrays.items()]
    out = nc.dram_tensor("out_t", (P, KC * SEQ), f32, kind="ExternalOutput").ap()
    build_trunk(nc, *ins, out)
    r = _run(nc, [arrays], core_ids=[0])
    got = r.results[0]["out_t"]
    return got.reshape(P, KC, SEQ).transpose(2, 1, 0).reshape(1, SEQ, D_MODEL)
```

```python
import concourse.bass as bass
from concourse import mybir
from contextlib import ExitStack
import math
import numpy as np

P = 128
D_MODEL, SEQ, DEPTH, N_META = 1024, 256, 2, 16
TOK = SEQ + N_META
MLA_HEADS, NOPE, ROPE, MLA_V = 8, 64, 32, 64
Q_RANK, KV_RANK = 384, 256
DIFF_HEADS, DIFF_DH = 4, 64
DIFF_ROPE = DIFF_DH // 4
D_FF = -(-(8 * D_MODEL) // (3 * 256)) * 256
THETA, EPS = 500000.0, 1e-6
MLA_SCALE = 1.0 / math.sqrt(NOPE + ROPE)
DIFF_SCALE = 1.0 / math.sqrt(DIFF_DH)
LAM_INIT = [0.8 - 0.6 * math.exp(-0.3 * l) for l in range(DEPTH)]
MASKED = -1e30

KC = D_MODEL // P
QC, KVC = Q_RANK // P, KV_RANK // P
FC = D_FF // P
HW = NOPE + ROPE
DOWN_SPLIT = (6, 6, 5, 5)
SLOT = 8 * P
RING, RAW, AHEAD, BANKS = 8, 4, 6, 4
HI_AHEAD = AHEAD + 1
CH = [(0, 16), (16, 144), (144, 272)]
KEYS = [(0, 128), (128, 256), (256, 272)]
B0, B1, A0, A1 = 0, 272, 272, 416
HEAD_SUMS = 448
UNITS = DIFF_HEADS + MLA_HEADS
MAPS = 2 * DIFF_HEADS + MLA_HEADS


def first_map(u):
    return 2 * u if u < DIFF_HEADS else u + DIFF_HEADS


def token_chunks(t0):
    return [c for c in CH if c[0] >= t0]


NORMS = 7
PRE_MIX, NQ, NKV, NDIFF, POST_MIX, PRE_FFN, POST_FFN = range(NORMS)
PE_ADDS = {PRE_MIX, POST_MIX, PRE_FFN, POST_FFN}
LAST_NORM = NORMS * DEPTH - 1
CHUNKS = {PRE_MIX: KC, NQ: QC, NKV: KVC, POST_MIX: KC, PRE_FFN: KC, POST_FFN: KC}

ENDS = {"lat": [1] * 6, "dq": [1] * 4, "dk": [1] * 4, "dv": [1] * 4, "uq": [2, 2, 2], "ukv": [4, 4],
        "gate": [1] * 16, "oa": [2] * 4, "ob": [2] * 4, "out": [1] * 8, "gu": [1] * (2 * FC),
        "down": [0, 0, 0, 1] * KC}
TURNS = [("uq", 0), ("dv", 0), ("uq", 1), ("dv", 1), ("uq", 2), ("dv", 2), ("ukv", 0), ("dv", 3), ("ukv", 1)]

O_DQ = Q_RANK + KV_RANK + ROPE
O_DK = O_DQ + DIFF_HEADS * 2 * DIFF_DH
O_DV = O_DK + DIFF_HEADS * 2 * DIFF_DH
O_G = O_DV + DIFF_HEADS * 2 * DIFF_DH
G_MIXPRE, G_MIXPOST, G_FFNPRE, G_FFNPOST, G_Q, G_KV, G_SUB = 0, 8, 16, 24, 32, 35, 37
GAINS = 38
C_ID, C_MASK, C_MASKM, C_COSD, C_SIND, C_COSM, C_SINM = 0, 128, 256, 512, 784, 1056, 1328
C_ALL = 1600


class Plan:

    def __init__(self):
        self.slot, self.tile, self.name_of = {}, {}, []
        self.slot_done, self.tile_done = [], []
        done = 0
        for l in range(DEPTH):
            order = [(n, i) for n in ("lat", "dq", "dk") for i in range(len(ENDS[n]))] + TURNS
            order += [(n, i) for n in ("gate", "oa", "ob", "out", "gu", "down") for i in range(len(ENDS[n]))]
            for name, i in order:
                self.slot[l, name, i] = len(self.slot_done)
                for _ in range(ENDS[name][i]):
                    done += 1
                    self.tile[l, name, sum(self.name_of[t] == (l, name) for t in range(len(self.name_of)))] = len(self.tile_done)
                    self.name_of.append((l, name))
                    self.tile_done.append(done)
                if ENDS[name][i] == 0:
                    done += 1
                self.slot_done.append(done)
        self.slots = len(self.slot_done)
        self.sq0, self.add0, self.sq_place, self.sq_free = {}, {}, {}, {}
        s = a = 0
        users = []
        for l in range(DEPTH):
            for k in range(NORMS):
                if k in CHUNKS:
                    K = l * NORMS + k
                    self.sq0[K], self.add0[K] = s, a
                    for c in range(1, CHUNKS[k]):
                        last = c == CHUNKS[k] - 1 and k in PE_ADDS
                        a += not last
                        self.sq_place[K, c] = len(users) % 2
                        self.sq_free[K, c] = users[-2] if len(users) >= 2 else None
                        users.append(("sum", K + 1) if last else ("add", a))
                    s += CHUNKS[k]


def build_trunk(nc: bass.Bass, xT, weights, gains, lam_in, consts, outT):
    f32, f32r, bf16 = mybir.dt.float32, mybir.dt.float32r, mybir.dt.bfloat16
    ALU, ACT, AX = mybir.AluOpType, mybir.ActivationFunctionType, mybir.AxisListType
    plan = Plan()
    ctx = ExitStack()
    with ctx:
        base = -(-nc.sbuf_base // 32) * 32

        def place(at, tensors):
            made = []
            for name, shape, dt in tensors:
                size = int(np.prod(shape[1:])) * (2 if dt == bf16 else 4)
                made.append(nc.alloc_sbuf_tensor_at(name, shape, dt, offset=at))
                at += -(-size // 32) * 32
            return made, at

        (w_raw, w_hi, w_lo, r, hh, hl, y, rstd_h, rstd_q, acc, sq, rc_d, rs_d, rc_q, rs_q,
         cst, identb, maskb, gain, small, lat, tres), at = place(base, [
            ("w_raw", [P, RAW, SLOT], f32), ("w_hi", [P, RING, SLOT], f32r), ("w_lo", [P, RING, SLOT], f32r),
            ("resid", [P, KC, TOK], f32), ("h_hi", [P, KC, TOK], f32r), ("h_lo", [P, KC, TOK], f32r),
            ("y", [P, KC, TOK], f32),
            ("rstd_h", [P, TOK], f32), ("rstd_q", [P, TOK], f32), ("acc", [P, 2, TOK], f32), ("sq", [P, 2, TOK], f32),
            ("rcos_d", [P, TOK], f32), ("rsin_d", [P, TOK], f32), ("rcos_q", [P, TOK], f32),
            ("rsin_q", [P, TOK], f32),
            ("cst", [P, C_ALL - 512 + 128], f32), ("identb", [P, P], bf16), ("maskb", [P, P], bf16),
            ("gain", [P, DEPTH, GAINS], f32), ("small", [P, 96], f32), ("lat", [P, 2, TOK], f32),
            ("tres", [P, TOK], f32)])
        lat_tmp_at = at - 4 * 3 * TOK
        rstd_kv = tres
        att0 = at
        (q_t, dqk, v_tok, gates), at = place(att0, [
            ("q_t", [P, MLA_HEADS, TOK], f32), ("dqk_t", [P, 8, TOK], f32),
            ("v_tok", [P, 3, 1024], f32), ("gates", [P, 16, TOK], f32)])
        gates_last_at = at - 4 * TOK
        k_t = nc.alloc_sbuf_tensor_at("k_t", [P, MLA_HEADS, TOK], f32, offset=base + 4 * (RAW + 2 * RING) * SLOT + 3 * 4 * KC * TOK)
        lat_at = at
        (lat_hi, lat_lo), at = place(lat_at, [("lat_hi", [P, QC + KVC, TOK], f32r), ("lat_lo", [P, QC + KVC, TOK], f32r)])
        (e_t, pt, pt_edge, ptm), _ = place(lat_at, [("e_t", [P, 2, 416], f32), ("pt", [P, 2, 384], f32), ("pt_edge", [16, 2, 32], f32),
                                                    ("ptm", [16, UNITS, 16], f32)])
        assert _ <= at
        v_at = at
        (kv_t, dv_t), at = place(v_at, [("kv_t", [P, MLA_HEADS, TOK], f32), ("dv_t", [P, DIFF_HEADS, TOK], f32)])
        (am_hi, am_lo, od), _ = place(v_at, [("am_hi", [P, 4, TOK], f32r), ("am_lo", [P, 4, TOK], f32r),
                                             ("od", [P, DIFF_HEADS, TOK], f32)])
        assert _ <= at
        (b_t,), at = place(at, [("b_t", [P, 4, TOK], f32)])
        (pm,), _ = place(lat_tmp_at, [("pm", [16, 3, 256], f32)])
        (maskmb,), _ = place(gates_last_at, [("maskmb", [16, 256], bf16)])
        rot = {"dq": b_t, "dk": gates[:, 8:12, :], "uq": gates[:, 6:8, :]}
        q_rot = gates[:, 4:6, :]
        krope = dv_t[:, 0, :]
        dqk_at = att0 + 4 * MLA_HEADS * TOK
        (od_hi, od_lo), _ = place(dqk_at, [("od_hi", [P, 4, TOK], f32r), ("od_lo", [P, 4, TOK], f32r)])
        (ff_hi, ff_lo, gbuf, ubuf, sbuf_, pbuf), _ = place(att0, [
            ("ff_hi", [P, FC, TOK], f32r), ("ff_lo", [P, FC, TOK], f32r), ("gbuf", [P, 2, TOK], f32),
            ("ubuf", [P, 2, TOK], f32), ("sbuf", [P, 2, TOK], f32), ("pbuf", [P, 2, TOK], f32)])
        assert _ <= nc.sbuf_usable_end
        ident = cst[:, 0:P]
        cos_d, sin_d, cos_m, sin_m = (cst[:, P + TOK * i:P + TOK * (i + 1)] for i in range(4))
        stage = y[:, 0:2, 0:256]
        eps = small[:, 0:1]
        ones = small[:, 1:2]
        neglam = small[:, 2:4]
        lam_e = small[:, 4:8]
        std = [small[:, 8 + 12 * i:20 + 12 * i] for i in range(2)]
        rec = [small[:, 32 + 12 * i:44 + 12 * i] for i in range(2)]
        mx = [small[:, 56 + 4 * i:60 + 4 * i] for i in range(2)]
        sm = [small[:, 64 + 4 * i:68 + 4 * i] for i in range(2)]
        mxm = small[0:16, 72:88]
        lamp = small[:, 92:96]
        idle = small[:, 90:91]
        idle_act = small[:, 91:92]
        gsub = small[:, 88:90]
        lam_raw = b_t.rearrange("p a b -> p (a b)")[:, 0:4 * DEPTH * DIFF_DH]
        ps = [ctx.enter_context(nc.psum_tensor(f"bank{i}", [P, 512], f32)) for i in range(8)]

        def sem(name):
            return ctx.enter_context(nc.semaphore(name))

        half_in = [sem(f"half_in{h}") for h in range(2)]
        quarter_hi, quarter_lo = sem("quarter_hi"), sem("quarter_lo")
        raw_in = [sem(f"raw_in{i}") for i in range(RAW)]
        x_in = [sem(f"x_in{q}") for q in range(4)]
        gain_in, id_in, tables_in, mask_in, out_done = (sem(n) for n in ("gain_in", "id_in", "tables_in", "mask_in", "out_done"))
        hi_ready, lo_ready = sem("hi_ready"), sem("lo_ready")
        pe_done, tile_free = sem("pe_done"), sem("tile_free")
        dve_step = sem("dve_step")
        warm_ready, const_ready, lam_ready, lam_exp = sem("warm_ready"), sem("const_ready"), sem("lam_ready"), sem("lam_exp")
        sq_ready, sq_added = sem("sq_ready"), sem("sq_added")
        norm_sum, norm_std, norm_rec, norm_bc, norm_ready = (sem(n) for n in ("norm_sum", "norm_std", "norm_rec", "norm_bc", "norm_ready"))
        r_ready, h_hi, h_lo = sem("r_ready"), sem("h_hi_ready"), sem("h_lo_ready")
        lat_ready_hi, lat_ready_lo = sem("lat_hi_ready"), sem("lat_lo_ready")
        rope_in, rope_done, kr_ready = sem("rope_in"), sem("rope_done"), sem("kr_ready")
        k_copied, q_placed = sem("k_copied"), sem("q_placed")
        v_ready, v_copied = sem("v_ready"), sem("v_copied")
        meta_half, meta_scores, meta_shift, meta_exp = (sem(n) for n in ("meta_half", "meta_scores", "meta_shift", "meta_exp"))
        meta_probs, meta_pt, meta_copied = sem("meta_probs"), sem("meta_pt"), sem("meta_copied")
        scores_ready, negmax_ready, exp_ready, probs_ready = (sem(n) for n in ("scores_ready", "negmax_ready", "exp_ready", "probs_ready"))
        pt_ready, pt_copied, pv_ready, out_hi, out_copied = (sem(n) for n in ("pt_ready", "pt_copied", "pv_ready", "out_hi", "out_copied"))
        od_squared, od_ready, od_hi_ready, od_lo_ready = sem("od_squared"), sem("od_ready"), sem("od_hi_ready"), sem("od_lo_ready")
        sig_ready, mix_ready, mix_hi, mix_lo = sem("sig_ready"), sem("mix_ready"), sem("mix_hi"), sem("mix_lo")
        silu_done, ff_prod, ff_hi_ready, ff_lo_ready = sem("silu_done"), sem("ff_prod"), sem("ff_hi_ready"), sem("ff_lo_ready")

        block = ctx.enter_context(nc.Block())

        def T0(l):
            return 0 if l < DEPTH - 1 else N_META

        def boundary_from(b):
            return N_META if b >= 2 * DEPTH - 1 else 0

        @block.sync
        def _(sp):
            def load(n, width, i=None, per=0):
                m = n if i is None else n + per * i
                if n >= RAW:
                    sp.wait_ge(lo_ready, m - RAW + 1)
                src = weights[bass.ds(m * P, P), 0:width] if i is not None else weights[m * P:(m + 1) * P, 0:width]
                sp.dma_start(w_raw[:, n % RAW, 0:width], src).then_inc(raw_in[n % RAW], 16)

            xc = xT.rearrange("p (k t) -> p k t", k=KC)
            sp.dma_start(gain[:, :, :], gains.rearrange("p (l g) -> p l g", l=DEPTH)).then_inc(gain_in, 16)
            two = weights[0:2 * P, :].rearrange("(s p) c -> p s c", s=2)
            for q in range(4):
                sp.dma_start(r[:, 2 * q:2 * q + 2, :], xc[:, 2 * q:2 * q + 2, :]).then_inc(x_in[q], 16)
                if q in (0, 2):
                    at = q * SLOT // 4
                    sp.dma_start(w_raw[:, 0:2, at:at + SLOT // 2], two[:, :, at:at + SLOT // 2]).then_inc(half_in[q // 2], 16)
            sp.dma_start(cst[:, 0:P], consts[:, 0:P]).then_inc(id_in, 16)
            load(2, SLOT)
            load(3, SLOT)
            load(4, SLOT)
            sp.dma_start(cst[:, P:], consts[:, 512:C_ALL]).then_inc(tables_in, 16)
            load(5, SLOT)
            sp.dma_start(stage, consts[:, P:512 + P].rearrange("p (a b) -> p a b", a=2)[:, :, 0:256]).then_inc(mask_in, 16)
            sp.dma_start(lam_raw, lam_in).then_inc(mask_in, 16)
            first = 6
            for l in range(DEPTH):
                d0 = plan.slot[l, "down", 0]
                whole = (d0 - first) // RING
                with sp.Fori(0, whole) as i:
                    for j in range(RING):
                        load(first + j, SLOT, i, RING)
                for n in range(first + whole * RING, d0):
                    load(n, SLOT)
                with sp.Fori(0, KC // 2) as i:
                    for j in range(RING):
                        load(d0 + j, DOWN_SPLIT[j % 4] * P, i, RING)
                first = d0 + 4 * KC
            out = outT.rearrange("p (k t) -> p k t", k=KC)
            for c in range(0, KC, 2):
                sp.wait_ge(r_ready, KC * (2 * DEPTH - 1) + c // 2 + 1)
                sp.dma_start(out[:, c:c + 2, :], r[:, c:c + 2, N_META:TOK]).then_inc(out_done, 16)
            sp.wait_ge(out_done, 16 * KC // 2)

        @block.scalar
        def _(act):
            def split(n, i=None, per=0):
                if n >= plan.slots:
                    return
                u, v = (0, 0) if i is None else (per * i, 4 * per * i)
                act.wait_ge(raw_in[n % RAW], 16 * (n // RAW + (n % RAW >= 2)) + v)
                if n >= RING:
                    act.wait_ge(pe_done, plan.slot_done[n - RING] + u)
                act.activation(w_hi[:, n % RING, :], w_raw[:, n % RAW, :], ACT.Copy).then_inc(hi_ready, 1)

            def square(K, c, src, t0):
                if c == 0:
                    if K >= 2:
                        act.wait_ge(norm_sum, K - 1)
                    dst = acc[:, K % 2, t0:]
                else:
                    if plan.sq_free[K, c]:
                        how, value = plan.sq_free[K, c]
                        act.wait_ge(sq_added if how == "add" else norm_sum, value)
                    dst = sq[:, plan.sq_place[K, c], t0:]
                act.activation(dst, src, ACT.Square).then_inc(sq_ready, 1)

            def root(K, bank, width, t0, heads=1, col=0):
                act.wait_ge(norm_sum, K + 1)
                if K >= 2:
                    act.wait_ge(norm_rec, K - 1)
                n = heads * len(token_chunks(t0))
                act.activation(std[K % 2][:, 0:n], ps[bank][:, col:col + n], ACT.Sqrt, bias=eps, scale=1.0 / width).then_inc(norm_std, 1)

            def boundary(b, K, g, l):
                t0 = boundary_from(b)
                for c in range(KC):
                    act.wait_ge(r_ready, KC * (b - 1) + c + 1)
                    act.activation(hh[:, c, t0:], r[:, c, t0:], ACT.Copy, scale=gain[:, l, g + c:g + c + 1]).then_inc(h_hi, 1)
                    square(K, c, r[:, c, t0:], t0)

            act.wait_ge(const_ready, 1)
            act.activation(idle_act, eps, ACT.Sqrt)
            act.wait_ge(gain_in, 16)

            def first_hi(*chunks):
                for c in chunks:
                    act.wait_ge(x_in[c // 2], 16)
                    act.activation(hh[:, c, :], r[:, c, :], ACT.Copy, scale=gain[:, 0, G_MIXPRE + c:G_MIXPRE + c + 1]).then_inc(h_hi, 1)

            def quarter_split(q):
                act.wait_ge(half_in[q // 2], 16)
                cols = slice(q * SLOT // 4, (q + 1) * SLOT // 4)
                act.activation(w_hi[:, 0:2, cols], w_raw[:, 0:2, cols], ACT.Copy).then_inc(hi_ready if q == 3 else quarter_hi, 2 if q == 3 else 1)

            def first_squares(*chunks):
                for c in chunks:
                    square(0, c, r[:, c, :], 0)

            first_hi(0, 1)
            quarter_split(0)
            quarter_split(1)
            first_hi(2, 3)
            first_squares(0, 1)
            first_hi(4, 5)
            quarter_split(2)
            quarter_split(3)
            first_hi(6, 7)
            first_squares(2)
            split(2)
            first_squares(3, 4, 5, 6, 7)
            for n in range(3, AHEAD):
                split(n)
            for l in range(DEPTH):
                t0, K0 = T0(l), NORMS * l
                S = lambda name, i=0: plan.slot[l, name, i]
                TL = lambda name, i=0: plan.tile[l, name, i]
                root(K0 + PRE_MIX, 7, D_MODEL, 0)
                if l == 0:
                    split(AHEAD)
                for i in range(6):
                    split(S("lat") + i + HI_AHEAD)
                    if i == 5:
                        continue
                    c0 = t0 if i < QC else 0
                    act.wait_ge(tile_free, TL("lat") + i + 1)
                    if l and i == 0:
                        act.wait_ge(pt_ready, UNITS * l)
                    act.activation(lat_hi[:, i, c0:], lat[:, i % 2, c0:], ACT.Copy,
                                   scale=gain[:, l, G_Q + i:G_Q + i + 1]).then_inc(lat_ready_hi, 1)
                    if i < QC:
                        square(K0 + NQ, i, lat[:, i % 2, c0:], c0)
                    else:
                        square(K0 + NKV, i - QC, lat[:, i % 2, c0:], c0)
                if l == 0:
                    act.wait_ge(lam_ready, 1)
                    act.activation(lam_e, lamp, ACT.Exp).then_inc(lam_exp, 1)
                for i in range(4):
                    split(S("dq") + i + HI_AHEAD)
                root(K0 + NQ, 7, Q_RANK, t0)
                root(K0 + NKV, 6, KV_RANK, 0)
                act.wait_ge(rope_done, 4 * l + 1)
                act.activation(k_t[64:96, :, :], krope[64:96, None, :].to_broadcast([32, MLA_HEADS, TOK]), ACT.Copy).then_inc(kr_ready, 1)
                for n in range(S("dq") + 4, S("dk") + 4):
                    split(n + HI_AHEAD)
                for st, i in TURNS:
                    split(S(st, i) + HI_AHEAD)
                    if (st, i) == ("dv", 2):
                        act.wait_ge(rope_done, 4 * (l + 1))
                        for q in range(4):
                            act.activation(q_t[64:96, q::4, t0:], q_rot[32 * q:32 * q + 32, :, t0:], ACT.Copy).then_inc(q_placed, 1)
                    if st == "ukv":
                        for h in range(4 * i, 4 * i + 4):
                            act.wait_ge(tile_free, TL("ukv", h) + 1)
                            act.activation(k_t[0:64, h, :], kv_t[0:64, h, :], ACT.Copy).then_inc(k_copied, 1)

                def v_evac(g):
                    act.wait_ge(v_ready, 3 * l + g + 1)
                    for c, (a, b) in enumerate(KEYS):
                        n = b - a
                        if g == 0:
                            act.activation(v_tok[0:n, c, 0:512], ps[4 + c][0:n, :], ACT.Copy).then_inc(v_copied, 1)
                        else:
                            act.activation(v_tok[0:n, c, 512 + 256 * (g - 1):768 + 256 * (g - 1)], ps[4 + c][0:n, 0:256], ACT.Copy).then_inc(v_copied, 1)

                def exps(u):
                    maps = [(4, 0, 0), (5, 1, 2)] if u < DIFF_HEADS else [(4 + u % 2, u % 2, 0)]
                    scale = DIFF_SCALE if u < DIFF_HEADS else MLA_SCALE
                    for m, (bank, e, s) in enumerate(maps):
                        act.wait_ge(negmax_ready, MAPS * l + first_map(u) + m + 1)
                        for part, (a, b) in enumerate(((B0, B1), (A0, A1))):
                            last = act.activation(e_t[:, e, a:b], ps[bank][:, a:b], ACT.Exp, bias=mx[u % 2][:, s + part:s + part + 1],
                                                  scale=scale, accum_out=sm[u % 2][:, s + part:s + part + 1])
                        last.then_inc(exp_ready, 1)

                def hi_out(u):
                    if u < DIFF_HEADS:
                        return
                    h = u - DIFF_HEADS
                    o = 64 * (h % 2)
                    act.wait_ge(pv_ready, UNITS * l + u + 1)
                    act.activation(am_hi[o:o + 64, h // 2, t0:], ps[7][o:o + 64, t0:TOK], ACT.Copy).then_inc(out_hi, 1)

                def pt_evac(u):
                    act.wait_ge(pt_ready, UNITS * l + u + 1)
                    b = u % 2
                    act.activation(pt_edge[:, b, :], ps[6][0:16, 384:416], ACT.Copy)
                    act.activation(pt[:, b, :], ps[6][:, 0:384], ACT.Copy).then_inc(pt_copied, 1)

                for i in range(16):
                    u = i - 4
                    if u < 0:
                        split(S("gate") + i + HI_AHEAD)
                        if i < 3:
                            v_evac(i)
                        elif l == 0:
                            act.wait_ge(meta_shift, 1)
                            act.activation(pm[:, 1, 0:128], pm[:, 0, 0:128], ACT.Exp, scale=MLA_SCALE)
                            act.activation(pm[:, 1, 128:256], pm[:, 0, 128:256], ACT.Exp, scale=DIFF_SCALE).then_inc(meta_exp, 1)
                        continue
                    exps(u)
                    if u >= 1:
                        hi_out(u - 1)
                    split(S("gate") + i + HI_AHEAD)
                    if u == 0 and l == 0:
                        act.wait_ge(meta_pt, 1)
                        act.activation(ptm[:, :, :], ps[7][0:16, 256:256 + 16 * UNITS].rearrange("p (a b) -> p a b", a=UNITS), ACT.Copy).then_inc(meta_copied, 1)
                    if u == UNITS - 1:
                        act.activation(idle_act, eps, ACT.Sqrt)
                    pt_evac(u)
                    if u == 5:
                        act.wait_ge(out_copied, UNITS * l + 4)
                        act.activation(b_t[:, :, t0:], od[:, :, t0:], ACT.Square).then_inc(od_squared, 1)
                root(K0 + NDIFF, 6, 2 * DIFF_DH, t0, DIFF_HEADS, HEAD_SUMS)
                hi_out(UNITS - 1)
                for q in range(4):
                    act.wait_ge(tile_free, TL("gate") + 4 * q + 4)
                    act.activation(gates[:, 4 * q:4 * q + 4, t0:], gates[:, 4 * q:4 * q + 4, t0:], ACT.Sigmoid).then_inc(sig_ready, 1)
                    if q % 2:
                        split(S("oa") + q // 2 + HI_AHEAD)
                for i in range(2, 4):
                    split(S("oa") + i + HI_AHEAD)
                    for d in range(2 * i - 4, 2 * i - 2):
                        act.wait_ge(od_ready, DIFF_HEADS * l + d + 1)
                        act.activation(od_hi[:, d, t0:], od[:, d, t0:], ACT.Copy, scale=gsub[:, l:l + 1]).then_inc(od_hi_ready, 1)

                def square_tile(K, t, m):
                    if m == KC - 2:
                        act.activation(idle_act, eps, ACT.Sqrt)
                    if m < KC - 1 and K != LAST_NORM:
                        act.wait_ge(tile_free, t + 1)
                        square(K, m, y[:, m, t0:], t0)
                    else:
                        act.wait_ge(pe_done, plan.tile_done[t])
                        square(K, m, ps[t % BANKS][:, t0:TOK], t0)

                def mix_split(m):
                    act.wait_ge(mix_ready, KC * l + m + 1)
                    act.activation(hh[:, m, t0:], gates[:, 8 + m, t0:], ACT.Copy).then_inc(mix_hi, 1)

                for i in range(4):
                    split(S("ob") + i + HI_AHEAD)
                    mix_split(2 * i)
                    mix_split(2 * i + 1)
                for m in range(KC):
                    split(S("out") + m + HI_AHEAD)
                    square_tile(K0 + POST_MIX, TL("out") + m, m)
                root(K0 + POST_MIX, 7, D_MODEL, t0)
                boundary(2 * l + 1, K0 + PRE_FFN, G_FFNPRE, l)
                root(K0 + PRE_FFN, 7, D_MODEL, t0)

                def pair(j, i=None, first=False):
                    s, t = S("gu") + 2 * j, TL("gu") + 2 * j
                    per = 0 if i is None else RING
                    o = 0 if i is None else per * i
                    p = 0 if i is None else 4 * i
                    J = FC * l + j
                    split(s + HI_AHEAD, i, per)
                    if not first:
                        hi_ff(j - 1, i)
                    act.wait_ge(tile_free, t + 1 + o)
                    if J >= 2:
                        act.wait_ge(ff_prod, J - 1 + p)
                    act.activation(sbuf_[:, j % 2, t0:], gbuf[:, j % 2, t0:], ACT.Silu).then_inc(silu_done, 1)
                    split(s + 1 + HI_AHEAD, i, per)

                def hi_ff(j, i=None):
                    p = 0 if i is None else 4 * i
                    act.wait_ge(ff_prod, FC * l + j + 1 + p)
                    dst = ff_hi[:, j, t0:] if i is None else ff_hi[:, bass.ds(4 * i + j, 1), t0:]
                    src = pbuf[:, j % 2, t0:] if i is None else pbuf[:, j % 2:j % 2 + 1, t0:]
                    act.activation(dst, src, ACT.Copy).then_inc(ff_hi_ready, 1)

                pair(0, first=True)
                pair(1)
                with act.Fori(0, 5) as i:
                    for j in range(2, 6):
                        pair(j, i)
                hi_ff(21)
                TD, SD = TL("down"), S("down")

                for m in range(KC):
                    for j in range(4):
                        split(SD + 4 * m + j + HI_AHEAD)
                    square_tile(K0 + POST_FFN, TD + m, m)
                root(K0 + POST_FFN, 7, D_MODEL, t0)
                if l < DEPTH - 1:
                    boundary(2 * l + 2, K0 + NORMS + PRE_MIX, G_MIXPRE, l + 1)

        @block.gpsimd
        def _(pool):
            def sum_squares(K, t0):
                for c in range(1, CHUNKS[K % NORMS] - (K % NORMS in PE_ADDS)):
                    pool.wait_ge(sq_ready, plan.sq0[K] + c + 1)
                    if c > 1:
                        pool.wait_ge(sq_added, plan.add0[K] + c - 1)
                    pool.tensor_tensor(acc[:, K % 2, t0:], acc[:, K % 2, t0:], sq[:, plan.sq_place[K, c], t0:], ALU.add).then_inc(sq_added, 1)

            def rope_add(l, i, dst, src):
                if i == 0:
                    pool.wait_ge(sq_added, plan.add0[NORMS * l + NKV] + KVC - 1)
                else:
                    pool.wait_ge(rope_done, 4 * l + i)
                pool.wait_ge(rope_in, 4 * l + i + 1)
                pool.tensor_tensor(dst, dst, src, ALU.add).then_inc(rope_done, 1)

            sum_squares(0, 0)
            for l in range(DEPTH):
                t0, K0 = T0(l), NORMS * l
                sum_squares(K0 + NQ, t0)
                sum_squares(K0 + NKV, 0)
                rope_add(l, 0, krope[64:96, :], b_t[64:96, 0, :])
                rope_add(l, 1, dqk[:, 0:4, t0:], rot["dq"][:, :, t0:])
                rope_add(l, 2, dqk[:, 4:8, :], rot["dk"])
                rope_add(l, 3, q_rot[:, :, t0:], rot["uq"][:, :, t0:])
                pool.wait_ge(rope_done, 4 * (l + 1))
                for m in range(KC):
                    pool.wait_ge(tile_free, plan.tile[l, "ob", m] + 1)
                    pool.tensor_tensor(gates[:, 8 + m, t0:], gates[:, 8 + m, t0:], gates[:, m, t0:], ALU.add).then_inc(mix_ready, 1)
                sum_squares(K0 + POST_MIX, t0)
                sum_squares(K0 + PRE_FFN, t0)

                def product(j, i=None):
                    o = 0 if i is None else RING * i
                    p = 0 if i is None else 4 * i
                    J = FC * l + j
                    pool.wait_ge(silu_done, J + 1 + p)
                    pool.wait_ge(tile_free, plan.tile[l, "gu", 0] + 2 * j + 2 + o)
                    if J >= 2:
                        pool.wait_ge(ff_lo_ready, J - 1 + p)
                    pool.tensor_tensor(pbuf[:, j % 2, t0:], sbuf_[:, j % 2, t0:], ubuf[:, j % 2, t0:], ALU.mult).then_inc(ff_prod, 1)

                product(0)
                product(1)
                with pool.Fori(0, 5) as i:
                    for j in range(2, 6):
                        product(j, i)
                sum_squares(K0 + POST_FFN, t0)
                if l < DEPTH - 1:
                    sum_squares(K0 + NORMS + PRE_MIX, 0)

        @block.vector
        def _(dve):
            steps = [0]

            def step(ins):
                steps[0] += 1
                ins.then_inc(dve_step, 1)
                return steps[0]

            def after(v):
                dve.wait_ge(dve_step, v)

            def split(n, i=None, per=0):
                if n >= plan.slots:
                    return
                u = 0 if i is None else per * i
                dve.wait_ge(hi_ready, n + 1 + u)
                dve.tensor_tensor(w_lo[:, n % RING, :], w_raw[:, n % RAW, :], w_hi[:, n % RING, :].bitcast(f32),
                                  ALU.subtract).then_inc(lo_ready, 1)

            def recip(K, t0, heads=1):
                n = heads * len(token_chunks(t0))
                dve.wait_ge(norm_std, K + 1)
                if K >= 2:
                    dve.wait_ge(norm_bc, K - 1)
                dve.reciprocal(rec[K % 2][:, 0:n], std[K % 2][:, 0:n]).then_inc(norm_rec, 1)

            def take(K, bank, dst, t0):
                dve.wait_ge(norm_bc, K + 1)
                dve.tensor_copy(dst[:, t0:], ps[bank][:, 64 + t0:64 + TOK]).then_inc(norm_ready, 1)

            def evac(t, dst, factor, rows=slice(0, P), t0=0):
                dve.wait_ge(pe_done, plan.tile_done[t])
                dve.tensor_tensor(dst, ps[t % BANKS][rows, t0:TOK], factor, ALU.mult).then_inc(tile_free, 1)

            def lo_part(b, c, g, l, t0):
                dve.wait_ge(h_hi, KC * b + c + 1)
                dve.scalar_tensor_tensor(out=hl[:, c, t0:], in0=r[:, c, t0:], scalar=gain[:, l, g + c:g + c + 1],
                                         in1=hh[:, c, t0:].bitcast(f32), op0=ALU.mult, op1=ALU.subtract).then_inc(h_lo, 1)

            def residual(b, K, gp, lp, t0):
                for c in range(KC):
                    if c:
                        dve.wait_ge(r_ready, KC * (b - 1) + c)
                    ins = dve.scalar_tensor_tensor(out=tres[:, t0:], in0=y[:, c, t0:], scalar=gain[:, lp, gp + c:gp + c + 1],
                                                   in1=ps[7][:, 64 + t0:64 + TOK], op0=ALU.mult, op1=ALU.mult)
                    if c < KC - 1:
                        after(step(ins))
                    else:
                        ins.then_inc(norm_ready, 1)
                        dve.wait_ge(norm_ready, K + 1)
                    dve.tensor_tensor(r[:, c, t0:], r[:, c, t0:], tres[:, t0:], ALU.add).then_inc(r_ready, 1)
                    if c:
                        lo_part(b, c - 1, *nxt(b), t0)
                lo_part(b, KC - 1, *nxt(b), t0)

            def nxt(b):
                return (G_FFNPRE, b // 2) if b % 2 else (G_MIXPRE, b // 2)

            dve.memset(eps, EPS).then_inc(const_ready, 1)
            dve.memset(ones, 1.0)
            dve.memset(identb[:, :], 0.0).then_inc(warm_ready, 1)
            dve.wait_ge(gain_in, 16)

            def quarter_split(q):
                dve.wait_ge(hi_ready if q == 3 else quarter_hi, 2 if q == 3 else q + 1)
                cols = slice(q * SLOT // 4, (q + 1) * SLOT // 4)
                dve.tensor_tensor(w_lo[:, 0:2, cols], w_raw[:, 0:2, cols], w_hi[:, 0:2, cols].bitcast(f32),
                                  ALU.subtract).then_inc(lo_ready if q == 3 else quarter_lo, 2 if q == 3 else 1)

            for c in range(KC):
                lo_part(0, c, G_MIXPRE, 0, 0)
                if c in (1, 5):
                    quarter_split(c // 2)
                    quarter_split(c // 2 + 1)
            split(2)
            split(3)
            split(4)
            split(5)
            recip(PRE_MIX, 0)
            take(PRE_MIX, 7, rstd_h, 0)
            def masks_and_lambda_sums():
                dve.wait_ge(id_in, 16)
                dve.wait_ge(mask_in, 32)
                dve.tensor_copy(identb[:, :], ident)
                dve.tensor_copy(maskb[:, :], stage[:, 0, 0:P])
                dve.tensor_copy(maskmb[:, 0:128], stage[0:16, 0, 128:256])
                dve.tensor_copy(maskmb[:, 128:256], stage[0:16, 1, 0:128]).then_inc(const_ready, 1)
                pairs = lam_raw.rearrange("p (a two d) -> p a two d", a=2 * DEPTH, two=2)
                prod = tres[:, 0:256].rearrange("p (a d) -> p a d", a=2 * DEPTH)
                after(step(dve.tensor_tensor(prod, pairs[:, :, 0, :], pairs[:, :, 1, :], ALU.mult)))
                dve.reduce_sum(lamp, prod, AX.X).then_inc(lam_ready, 1)

            def lambdas():
                dve.wait_ge(lam_exp, 1)
                for l in range(DEPTH):
                    v = step(dve.tensor_tensor(neglam[:, l:l + 1], lam_e[:, 2 * l + 1:2 * l + 2], lam_e[:, 2 * l:2 * l + 1], ALU.subtract))
                    after(v)
                    step(dve.tensor_scalar(neglam[:, l:l + 1], neglam[:, l:l + 1], LAM_INIT[l], None, ALU.subtract))
                    step(dve.tensor_scalar(gsub[:, l:l + 1], gain[:, l, G_SUB:G_SUB + 1], 1.0 - LAM_INIT[l], None, ALU.mult))
                after(steps[0])
                dve.memset(idle, 0.0).then_inc(const_ready, 1)

            for l in range(DEPTH):
                t0, K0 = T0(l), NORMS * l
                S = lambda name, i=0: plan.slot[l, name, i]
                TL = lambda name, i=0: plan.tile[l, name, i]
                if l:
                    split(S("lat") + AHEAD)
                    recip(K0 + PRE_MIX, 0)
                    take(K0 + PRE_MIX, 7, rstd_h, 0)
                dve.wait_ge(norm_ready, K0 + PRE_MIX + 1)

                def rotary_factors():
                    for dst, tab in ((rc_d, cos_d), (rs_d, sin_d)):
                        step(dve.tensor_tensor(dst[:, :], rstd_h[:, :], tab, ALU.mult))
                    for dst, tab in ((rc_q, cos_m), (rs_q, sin_m)):
                        v = step(dve.tensor_tensor(dst[64:96, :], rstd_h[64:96, :], tab[64:96, :], ALU.mult))
                    after(v)

                for i in range(5):
                    c0 = t0 if i < QC else 0
                    if i >= 2 or l:
                        K = K0 + NQ if i < QC else K0 + NKV
                        prev = plan.sq0[K0 + NQ] + i - 1 if i >= 2 else plan.sq0[K0 - NORMS + NKV] + 2
                        dve.wait_ge(sq_ready, prev)
                    evac(TL("lat") + i, lat[:, i % 2, c0:], rstd_h[:, c0:], t0=c0)
                    if i or not l:
                        split(S("lat") + i + AHEAD)
                    dve.wait_ge(lat_ready_hi, 5 * l + i + 1)
                    dve.scalar_tensor_tensor(out=lat_lo[:, i, c0:], in0=lat[:, i % 2, c0:], scalar=gain[:, l, G_Q + i:G_Q + i + 1],
                                             in1=lat_hi[:, i, c0:].bitcast(f32), op0=ALU.mult, op1=ALU.subtract).then_inc(lat_ready_lo, 1)
                    if i == 3 and l == 0:
                        masks_and_lambda_sums()
                if l == 0:
                    dve.wait_ge(tables_in, 16)
                rotary_factors()
                split(S("lat") + 5 + AHEAD)
                t = TL("lat") + 5
                swap_m = [(i + 16) % 32 for i in range(32)]
                swap_d = [(i + 8) % 16 if i < 16 else i for i in range(32)]
                dve.wait_ge(pe_done, plan.tile_done[t])
                v = step(dve.tensor_tensor(b_t[64:96, 0, :], ps[t % BANKS][64:96, 0:TOK], rs_q[64:96, :], ALU.mult))
                evac(t, krope[64:96, :], rc_q[64:96, :], rows=slice(64, 96))
                after(v)
                dve.wait_ge(tile_free, t + 1)
                dve.stream_shuffle(b_t[64:96, 0, :], b_t[64:96, 0, :], swap_m).then_inc(rope_in, 1)
                if l == 0:
                    lambdas()
                for st, base_c in (("dq", 0), ("dk", 4)):
                    c0 = t0 if st == "dq" else 0
                    b = rot[st]
                    if st == "dq":
                        dve.wait_ge(rope_done, 4 * l + 1)
                    for i in range(4):
                        split(S(st) + i + AHEAD)
                        t = TL(st) + i
                        dve.wait_ge(pe_done, plan.tile_done[t])
                        v = step(dve.tensor_tensor(b[:, i, c0:], ps[t % BANKS][:, c0:TOK], rs_d[:, c0:], ALU.mult))
                        evac(t, dqk[:, base_c + i, c0:], rc_d[:, c0:], t0=c0)
                        if st == "dq" and i == 3:
                            recip(K0 + NQ, t0)
                            recip(K0 + NKV, 0)
                        if st == "dk" and i == 1:
                            take(K0 + NQ, 7, rstd_q, t0)
                            take(K0 + NKV, 6, rstd_kv, 0)
                            dve.wait_ge(norm_ready, K0 + NKV + 1)
                            v = step(dve.tensor_tensor(rc_q[:, t0:], rstd_q[:, t0:], cos_m[:, t0:], ALU.mult))
                            v = step(dve.tensor_tensor(rs_q[:, t0:], rstd_q[:, t0:], sin_m[:, t0:], ALU.mult))
                    after(v)
                    dve.wait_ge(tile_free, TL(st) + 4)
                    dve.stream_shuffle(b[:, :, c0:], b[:, :, c0:], swap_d).then_inc(rope_in, 1)
                dve.wait_ge(kr_ready, l + 1)
                for st, i in TURNS:
                    if st != "ukv":
                        split(S(st, i) + AHEAD)
                    if st == "dv":
                        evac(TL("dv", i), dv_t[:, i, :], rstd_h[:, :])
                        if i == 0:
                            after(products)
                            dve.wait_ge(tile_free, TL("uq", 1) + 1)
                            dve.stream_shuffle(rot["uq"][:, :, t0:], rot["uq"][:, :, t0:], swap_m).then_inc(rope_in, 1)
                    elif st == "ukv":
                        for h in range(4 * i, 4 * i + 4):
                            evac(TL("ukv", h), kv_t[:, h, :], rstd_kv[:, :])
                            if h == 4 * i:
                                split(S(st, i) + AHEAD)
                    else:
                        for j in (2 * i, 2 * i + 1):
                            t = TL("uq", j)
                            dve.wait_ge(pe_done, plan.tile_done[t])
                            if j < 2:
                                products = step(dve.tensor_tensor(rot["uq"][:, j, t0:], ps[t % BANKS][:, t0:TOK], rs_q[:, t0:], ALU.mult))
                                evac(t, q_rot[:, j, t0:], rc_q[:, t0:], t0=t0)
                            else:
                                h = 2 * j - 4
                                dve.tensor_tensor(q_t[0:NOPE, h, t0:], ps[t % BANKS][0:NOPE, t0:TOK], rstd_q[0:NOPE, t0:], ALU.mult)
                                evac(t, q_t[0:NOPE, h + 1, t0:], rstd_q[NOPE:, t0:], rows=slice(NOPE, P), t0=t0)

                def gate(i):
                    evac(TL("gate") + i, gates[:, i, t0:], rstd_h[:, t0:], t0=t0)

                def unit_maps(u):
                    return [(4, 0, 0), (5, 1, 2)] if u < DIFF_HEADS else [(4 + u % 2, u % 2, 0)]

                def negmax(u):
                    U = UNITS * l + u
                    if U >= 2:
                        dve.wait_ge(probs_ready, U - 1)
                    scale = DIFF_SCALE if u < DIFF_HEADS else MLA_SCALE
                    for m, (bank, e, s) in enumerate(unit_maps(u)):
                        dve.wait_ge(scores_ready, MAPS * l + first_map(u) + m + 1)
                        dve.reduce_max(mx[u % 2][:, s:s + 1], ps[bank][:, B0:B1], AX.X)
                        v = step(dve.reduce_max(mx[u % 2][:, s + 1:s + 2], ps[bank][:, A0:A1], AX.X))
                        after(v)
                        dve.tensor_scalar(mx[u % 2][:, s:s + 2], mx[u % 2][:, s:s + 2], -scale, None, ALU.mult).then_inc(negmax_ready, 1)

                def probs(u):
                    M = MAPS * l + first_map(u)
                    s = sm[u % 2]
                    e = unit_maps(u)[0][1]
                    dve.wait_ge(exp_ready, M + 1)
                    v = step(dve.reciprocal(s[:, 0:2], s[:, 0:2]))
                    after(v)
                    step(dve.tensor_scalar(e_t[:, e, B0:B1], e_t[:, e, B0:B1], s[:, 0:1], None, ALU.mult))
                    ins = dve.tensor_scalar(e_t[:, e, A0:A1], e_t[:, e, A0:A1], s[:, 1:2], None, ALU.mult)
                    if u >= DIFF_HEADS:
                        ins.then_inc(probs_ready, 1)
                        return
                    step(ins)
                    dve.wait_ge(exp_ready, M + 2)
                    v = step(dve.reciprocal(s[:, 2:4], s[:, 2:4]))
                    after(v)
                    v = step(dve.tensor_scalar(s[:, 2:4], s[:, 2:4], neglam[:, l:l + 1], None, ALU.mult))
                    after(v)
                    for part, (a, b) in enumerate(((B0, B1), (A0, A1))):
                        ins = dve.scalar_tensor_tensor(out=e_t[:, 0, a:b], in0=e_t[:, 1, a:b], scalar=s[:, 2 + part:3 + part],
                                                       in1=e_t[:, 0, a:b], op0=ALU.mult, op1=ALU.add)
                    ins.then_inc(probs_ready, 1)

                def out_part(u):
                    if u < DIFF_HEADS:
                        dve.wait_ge(pv_ready, UNITS * l + u + 1)
                        dve.tensor_copy(od[:, u, t0:], ps[7][:, t0:TOK]).then_inc(out_copied, 1)
                    else:
                        h = u - DIFF_HEADS
                        o = 64 * (h % 2)
                        dve.wait_ge(out_hi, MLA_HEADS * l + h + 1)
                        dve.tensor_tensor(am_lo[o:o + 64, h // 2, t0:], ps[7][o:o + 64, t0:TOK], am_hi[o:o + 64, h // 2, t0:].bitcast(f32),
                                          ALU.subtract).then_inc(out_copied, 1)

                for i in range(16):
                    u = i - 4
                    if u < 0:
                        split(S("gate") + i + AHEAD)
                        if i == 3 and l == 0:
                            m3 = lambda a: a.rearrange("p (a b) -> p a b", a=16)
                            dve.wait_ge(meta_scores, 1)
                            v = step(dve.reduce_max(mxm, m3(ps[7][0:16, 0:256]), AX.X))
                            after(v)
                            dve.tensor_tensor(m3(pm[:, 0, :]), m3(ps[7][0:16, 0:256]), mxm[:, :, None].to_broadcast([16, 16, 16]),
                                              ALU.subtract).then_inc(meta_shift, 1)
                            dve.wait_ge(meta_exp, 1)
                            v = step(dve.reduce_sum(mxm, m3(pm[:, 1, :]), AX.X))
                            after(v)
                            v = step(dve.reciprocal(mxm, mxm))
                            after(v)
                            v = step(dve.tensor_scalar(mxm[:, 12:16], mxm[:, 12:16], neglam[0:16, 0:1], None, ALU.mult))
                            after(v)
                            v = step(dve.tensor_tensor(m3(pm[:, 2, :]), m3(pm[:, 1, :]), mxm[:, :, None].to_broadcast([16, 16, 16]), ALU.mult))
                            after(v)
                            dve.tensor_tensor(pm[:, 2, 128:192], pm[:, 2, 128:192], pm[:, 2, 192:256], ALU.add).then_inc(meta_probs, 1)
                        if i == 3:
                            negmax(0)
                        gate(i)
                        continue
                    if u:
                        negmax(u)
                    probs(u)
                    if u >= 1:
                        out_part(u - 1)
                    split(S("gate") + i + AHEAD)
                    gate(i)
                out_part(UNITS - 1)
                K = K0 + NDIFF
                recip(K, t0, DIFF_HEADS)
                for m in range(KC):
                    if m % 4 == 0:
                        dve.wait_ge(sig_ready, 4 * l + m // 4 + 1)
                    evac(TL("oa") + m, gates[:, m, t0:], gates[:, m, t0:], t0=t0)
                    if m == 2:
                        dve.wait_ge(norm_bc, K + 1)
                        for d in range(DIFF_HEADS):
                            dve.tensor_tensor(od[:, d, t0:], ps[4 + d][:, 64 + t0:64 + TOK], od[:, d, t0:], ALU.mult).then_inc(od_ready, 1)
                    if m in (4, 5):
                        for d in (2 * m - 8, 2 * m - 7):
                            dve.wait_ge(od_hi_ready, DIFF_HEADS * l + d + 1)
                            dve.scalar_tensor_tensor(out=od_lo[:, d, t0:], in0=od[:, d, t0:], scalar=gsub[:, l:l + 1],
                                                     in1=od_hi[:, d, t0:].bitcast(f32), op0=ALU.mult, op1=ALU.subtract).then_inc(od_lo_ready, 1)
                    if m % 2:
                        split(S("oa") + m // 2 + AHEAD)
                dve.memset(idle, 0.0).then_inc(norm_ready, 1)

                def mix_low(m):
                    dve.wait_ge(mix_hi, KC * l + m + 1)
                    dve.tensor_tensor(hl[:, m, t0:], gates[:, 8 + m, t0:], hh[:, m, t0:].bitcast(f32), ALU.subtract).then_inc(mix_lo, 1)

                for m in range(KC):
                    if m % 4 == 0:
                        dve.wait_ge(sig_ready, 4 * l + m // 4 + 3)
                    if m % 2 == 0:
                        split(S("ob") + m // 2 + AHEAD)
                    evac(TL("ob") + m, gates[:, 8 + m, t0:], gates[:, 8 + m, t0:], t0=t0)
                    if m >= 2:
                        mix_low(m - 2)
                mix_low(KC - 2)
                mix_low(KC - 1)

                def to_y(K, t, m):
                    if m < KC - 1 and K != LAST_NORM:
                        dve.wait_ge(pe_done, plan.tile_done[t])
                    else:
                        dve.wait_ge(sq_ready, plan.sq0[K] + m + 1)
                    if K == LAST_NORM:
                        dve.tensor_scalar(y[:, m, t0:], ps[t % BANKS][:, t0:TOK], gain[:, l, G_FFNPOST + m:G_FFNPOST + m + 1], None,
                                          ALU.mult).then_inc(tile_free, 1)
                    else:
                        dve.tensor_copy(y[:, m, t0:], ps[t % BANKS][:, t0:TOK]).then_inc(tile_free, 1)

                for m in range(KC):
                    split(S("out") + m + AHEAD)
                    to_y(K0 + POST_MIX, TL("out") + m, m)
                recip(K0 + POST_MIX, t0)
                dve.wait_ge(norm_bc, K0 + POST_MIX + 1)
                residual(2 * l + 1, K0 + POST_MIX, G_MIXPOST, l, t0)
                split(S("gu") + AHEAD)
                recip(K0 + PRE_FFN, t0)
                take(K0 + PRE_FFN, 7, rstd_h, t0)
                dve.wait_ge(norm_ready, K0 + PRE_FFN + 1)

                def pair(j, i=None, first=False):
                    s, t = S("gu") + 2 * j, TL("gu") + 2 * j
                    o = 0 if i is None else RING * i
                    p = 0 if i is None else 4 * i
                    J = FC * l + j
                    if not first:
                        split(s + AHEAD, i, RING)
                    for k, buf in ((0, gbuf), (1, ubuf)):
                        dve.wait_ge(pe_done, plan.tile_done[t + k] + o)
                        if J >= 2:
                            dve.wait_ge(ff_prod if k else silu_done, J - 1 + p)
                        dve.tensor_tensor(buf[:, j % 2, t0:], ps[(t + k) % BANKS][:, t0:TOK], rstd_h[:, t0:], ALU.mult).then_inc(tile_free, 1)
                        if k == 0:
                            split(s + 1 + AHEAD, i, RING)
                    if not first:
                        lo_ff(j - 1, i)

                def lo_ff(j, i=None):
                    p = 0 if i is None else 4 * i
                    dve.wait_ge(ff_hi_ready, FC * l + j + 1 + p)
                    at_j = slice(j, j + 1) if i is None else bass.ds(4 * i + j, 1)
                    dve.tensor_tensor(ff_lo[:, at_j, t0:], pbuf[:, j % 2:j % 2 + 1, t0:], ff_hi[:, at_j, t0:].bitcast(f32),
                                      ALU.subtract).then_inc(ff_lo_ready, 1)

                pair(0, first=True)
                pair(1)
                with dve.Fori(0, 5) as i:
                    for j in range(2, 6):
                        pair(j, i)
                lo_ff(21)
                for m in range(KC):
                    for j in range(4):
                        split(S("down") + 4 * m + j + AHEAD)
                    to_y(K0 + POST_FFN, TL("down") + m, m)
                recip(K0 + POST_FFN, t0)
                dve.wait_ge(norm_bc, K0 + POST_FFN + 1)
                if l < DEPTH - 1:
                    residual(2 * l + 2, K0 + POST_FFN, G_FFNPOST, l, t0)
            rstd2 = ps[7][:, None, 64 + N_META:64 + TOK].to_broadcast([P, 2, SEQ])
            for c in range(0, KC, 2):
                after(step(dve.tensor_tensor(y[:, c:c + 2, N_META:], y[:, c:c + 2, N_META:], rstd2, ALU.mult)))
                dve.tensor_tensor(r[:, c:c + 2, N_META:], r[:, c:c + 2, N_META:], y[:, c:c + 2, N_META:], ALU.add).then_inc(r_ready, 1)

        @block.tensor
        def _(pe):
            def slot_ready(n, i=None):
                pe.wait_ge(lo_ready, n + 1 + (0 if i is None else RING * i))

            def bank_free(t, i=None, per=0):
                if t >= BANKS:
                    pe.wait_ge(tile_free, t - BANKS + 1 + (0 if i is None else per * i))

            def block(t, n, at, width, hi, lo, t0, first, last):
                dst = ps[t % BANKS][0:width, t0:TOK]
                wh, wl = (w[:, n % RING, at:at + width] for w in (w_hi, w_lo))
                pe.matmul(dst, wh, hi, start=first, stop=False)
                pe.matmul(dst, wh, lo, start=False, stop=False)
                return pe.matmul(dst, wl, hi, start=False, stop=last)

            def tile(t, n, at, width, src, t0, i=None, per=0, inside=None):
                bank_free(t, i, per)
                for k, (a, b) in enumerate(src):
                    if inside and k in inside:
                        inside[k]()
                    mm = block(t, n, at + k * width, width, a, b, t0, k == 0, k == len(src) - 1)
                mm.then_inc(pe_done, 1)

            def first_tiles(tiles, ready, before=None, spread_factors=None):
                if tiles[0][1]:
                    slot_ready(tiles[-1][1])
                bank_free(tiles[-1][0])
                hi_sem, lo_sem, base = ready
                for k in range(KC):
                    if before and k in before:
                        before[k]()
                    pe.wait_ge(hi_sem, base + k + 1)
                    for j, (t, n, src, t0) in enumerate(tiles):
                        if spread_factors and k == KC - 1 and j == 2:
                            spread_factors()
                        for q, w in enumerate((w_hi, w_lo)):
                            pe.matmul(ps[t % BANKS][:, t0:TOK], w[:, n % RING, k * P:(k + 1) * P], src[k][0],
                                      start=k == 0 and q == 0, stop=False)
                    pe.wait_ge(lo_sem, base + k + 1)
                    for t, n, src, t0 in tiles:
                        mm = pe.matmul(ps[t % BANKS][:, t0:TOK], w_hi[:, n % RING, k * P:(k + 1) * P], src[k][1],
                                       start=False, stop=k == KC - 1)
                        if k == KC - 1:
                            mm.then_inc(pe_done, 1)

            def sums(a, bank, col, srcs, count=True, last_ready=None):
                chunks = token_chunks(a)
                for s, src in enumerate(srcs):
                    if s:
                        last_ready()
                    for c, (t_a, _) in enumerate(chunks):
                        last = s == len(srcs) - 1 and c == len(chunks) - 1
                        mm = pe.matmul(ps[bank][:, col + c:col + c + 1], src[:, t_a:t_a + P], ones, start=s == 0 and c == 0, stop=last)
                if count:
                    mm.then_inc(norm_sum, 1)

            def norm_sums(K, bank, t0):
                k = K % NORMS
                pe.wait_ge(sq_added, plan.add0[K] + CHUNKS[k] - 1 - (k in PE_ADDS))
                before = K - 1 if k == NKV else K
                if before > 0:
                    pe.wait_ge(norm_ready, before)
                parts = [acc[:, K % 2, :]] + ([sq[:, plan.sq_place[K, CHUNKS[k] - 1], :]] if k in PE_ADDS else [])
                sums(t0, bank, 0, parts, last_ready=lambda: pe.wait_ge(sq_ready, plan.sq0[K] + CHUNKS[k]))

            def spread(K, bank, t0, col=0, count=True):
                for c, (a, b) in enumerate(token_chunks(t0)):
                    n = b - a
                    mm = pe.transpose(ps[bank][:, 64 + a:64 + b], rec[K % 2][0:n, col + c:col + c + 1].to_broadcast([n, P]), ident[0:n, 0:n])
                if count:
                    mm.then_inc(norm_bc, 1)

            def keep_clock(n):
                for _ in range(n):
                    pe.matmul(ps[6][:, 0:P], identb[:, :], identb[:, :], start=True, stop=True)

            def post_norm(K):
                norm_sums(K, 7, t0)
                keep_clock(10)
                norm_spread(K, 7, t0)
                keep_clock(28)

            def norm_spread(K, bank, t0):
                pe.wait_ge(norm_rec, K + 1)
                spread(K, bank, t0)

            pe.wait_ge(warm_ready, 1)
            keep_clock(50)
            for l in range(DEPTH):
                t0, K0 = T0(l), NORMS * l
                S = lambda name, i=0: plan.slot[l, name, i]
                TL = lambda name, i=0: plan.tile[l, name, i]
                full = [(hh[:, k, :], hl[:, k, :]) for k in range(KC)]
                late = [(hh[:, k, t0:], hl[:, k, t0:]) for k in range(KC)]
                if l == 0:
                    first_tiles([(TL("lat") + q, S("lat") + q, late, t0) for q in range(2)], (h_hi, h_lo, 0),
                                {0: lambda: pe.wait_ge(quarter_lo, 1), 2: lambda: pe.wait_ge(quarter_lo, 2),
                                 4: lambda: pe.wait_ge(quarter_lo, 3), 6: lambda: slot_ready(1)})
                    slot_ready(S("lat") + 2)
                    tile(TL("lat") + 2, S("lat") + 2, 0, P, late, t0)
                    norm_sums(K0 + PRE_MIX, 7, 0)
                    pe.wait_ge(id_in, 16)
                    slot_ready(S("lat") + 3)
                    tile(TL("lat") + 3, S("lat") + 3, 0, P, full, 0, inside={6: lambda: norm_spread(K0 + PRE_MIX, 7, 0)})
                else:
                    first_tiles([(TL("lat") + q, S("lat") + q, *((late, t0) if q < QC else (full, 0))) for q in range(BANKS)],
                                (h_hi, h_lo, KC * 2 * l), {KC - 1: lambda: norm_sums(K0 + PRE_MIX, 7, 0)},
                                lambda: norm_spread(K0 + PRE_MIX, 7, 0))
                for i in range(4, 6):
                    slot_ready(S("lat") + i)
                    tile(TL("lat") + i, S("lat") + i, 0, P if i < 5 else HW, full, 0)
                def latent_spreads():
                    norm_spread(K0 + NQ, 7, t0)
                    norm_spread(K0 + NKV, 6, 0)

                for st, src, c0 in (("dq", late, t0), ("dk", full, 0)):
                    for i in range(4):
                        slot_ready(S(st) + i)
                        tile(TL(st) + i, S(st) + i, 0, P, src, c0, inside={6: latent_spreads} if (st, i) == ("dk", 1) else None)
                        if st == "dq" and i == 3:
                            norm_sums(K0 + NQ, 7, t0)
                            norm_sums(K0 + NKV, 6, 0)
                pe.wait_ge(lat_ready_lo, 5 * (l + 1))
                qsrc = [(lat_hi[:, k, t0:], lat_lo[:, k, t0:]) for k in range(QC)]
                kvsrc = [(lat_hi[:, QC + k, :], lat_lo[:, QC + k, :]) for k in range(KVC)]
                for st, i in TURNS:
                    n = S(st, i)
                    slot_ready(n)
                    if st == "dv":
                        tile(TL("dv", i), n, 0, P, full, 0)
                    elif st == "uq":
                        for j in (2 * i, 2 * i + 1):
                            tile(TL("uq", j), n, (j % 2) * QC * P, P, qsrc, t0)
                    else:
                        for h in range(4 * i, 4 * i + 4):
                            tile(TL("ukv", h), n, (h % 4) * KVC * P, P, kvsrc, 0)

                def v_transposes(g):
                    if g == 0:
                        pe.wait_ge(norm_ready, K0 + NKV + 1)
                        pe.wait_ge(tile_free, TL("dv", 3) + 1)
                    else:
                        pe.wait_ge(tile_free, TL("ukv", 4 * g - 1) + 1)
                        pe.wait_ge(v_copied, 9 * l + 3 * g)
                    for c, (a, b) in enumerate(KEYS):
                        for s in range(4):
                            if g == 0:
                                mm = pe.transpose(ps[4 + c][0:b - a, s * P:(s + 1) * P], dv_t[:, s, a:b], ident)
                            else:
                                mm = pe.transpose(ps[4 + c][0:b - a, s * MLA_V:(s + 1) * MLA_V], kv_t[NOPE:, 4 * (g - 1) + s, a:b], ident[NOPE:, NOPE:])
                    mm.then_inc(v_ready, 1)

                def qk(u, a, b):
                    if u < DIFF_HEADS:
                        return [(dqk[o:o + 64, u, a:b], dqk[o:o + 64, 4 + u, :]) for o in (0, 64)]
                    h = u - DIFF_HEADS
                    return [(q_t[0:96, h, a:b], k_t[0:96, h, :])]

                def keys_ready():
                    pe.wait_ge(rope_done, 4 * (l + 1))
                    pe.wait_ge(q_placed, 4 * (l + 1))
                    pe.wait_ge(kr_ready, l + 1)
                    pe.wait_ge(k_copied, MLA_HEADS * (l + 1))

                def meta_rows():
                    pe.matmul(ps[7][0:16, 0:256], identb[0:16, 0:16], maskmb[:, :], start=True, stop=False)
                    maps = [(q, k) for u_ in range(4, 12) for q, k in qk(u_, 0, 16)]
                    maps += [qk(u_, 0, 16)[s] for s in range(2) for u_ in range(4)]
                    for m, (q, k) in enumerate(maps):
                        mm = pe.matmul(ps[7][0:16, 16 * m:16 * m + 16], q, k[:, 0:16], start=False, stop=m == 15)
                        if m == 11:
                            mm.then_inc(meta_half, 1)
                            pe.wait_ge(meta_half, 1)
                    mm.then_inc(meta_scores, 1)

                def meta_transposes():
                    pe.wait_ge(meta_probs, 1)
                    for u in range(UNITS):
                        m = 8 + u if u < DIFF_HEADS else u - DIFF_HEADS
                        mm = pe.matmul(ps[7][0:16, 256 + 16 * u:272 + 16 * u], pm[:, 2, 16 * m:16 * m + 16], ident[0:16, 0:16],
                                       start=True, stop=True)
                    mm.then_inc(meta_pt, 1)

                def scores(u):
                    U = UNITS * l + u
                    if U:
                        pe.wait_ge(exp_ready, MAPS * l + first_map(u))
                    for m, (q_a, k) in enumerate(qk(u, 16, 144)):
                        q_b = qk(u, 144, 272)[m][0]
                        bank = ps[4 + m] if u < DIFF_HEADS else ps[4 + u % 2]
                        pe.matmul(bank[:, B0:B1], q_b, k, start=True, stop=False)
                        pe.matmul(bank[:, A0:A1], q_a, k[:, 0:144], start=False, stop=False)
                        diagonals = bank[:, 144:432].rearrange("p (a b) -> p a b", a=2)[:, :, 0:P]
                        pe.matmul(diagonals, identb[:, :], maskb[:, None, :].to_broadcast([P, 2, P]), start=False, stop=True).then_inc(scores_ready, 1)

                def head_sums(d):
                    pe.wait_ge(od_squared, l + 1)
                    sums(t0, 6, HEAD_SUMS + len(token_chunks(t0)) * d, [b_t[:, d, :]], d == DIFF_HEADS - 1)

                def first_scores():
                    pe.wait_ge(v_copied, 9 * (l + 1))
                    scores(0)

                def transposes(u):
                    pe.wait_ge(probs_ready, UNITS * l + u + 1)
                    e = e_t[:, 0 if u < DIFF_HEADS else u % 2, :]
                    for col, src in ((0, A0), (128, B0), (256, B0 + 128)):
                        pe.transpose(ps[6][:, col:col + P], e[:, src:src + P], ident)
                    for col, src in ((384, A0 + 128), (400, B0 + 256)):
                        mm = pe.matmul(ps[6][0:16, col:col + 16], e[:, src:src + 16], ident[:, P - 16:P], start=True, stop=True)
                    mm.then_inc(pt_ready, 1)

                def pv(u):
                    U = UNITS * l + u
                    pe.wait_ge(pt_copied, U + 1)
                    if U:
                        pe.wait_ge(out_copied, U)
                    if u < DIFF_HEADS:
                        o, n, col = 0, P, P * u
                    else:
                        h = u - DIFF_HEADS
                        o, n, col = 64 * (h % 2), 64, 512 + 64 * h
                    b = u % 2
                    if l == 0:
                        pe.wait_ge(meta_copied, 1)
                        pe.matmul(ps[7][o:o + n, 0:16], v_tok[0:16, 0, col:col + n], ptm[:, u, :], start=True, stop=True)
                    pe.matmul(ps[7][o:o + n, 16:TOK], v_tok[:, 0, col:col + n], pt[:, b, 0:256], start=True, stop=False)
                    pe.matmul(ps[7][o:o + n, 144:TOK], v_tok[:, 1, col:col + n], pt[:, b, 256:384], start=False, stop=False)
                    pe.matmul(ps[7][o:o + n, 128:144], v_tok[0:16, 1, col:col + n], pt_edge[:, b, 0:16], start=False, stop=False)
                    pe.matmul(ps[7][o:o + n, 256:TOK], v_tok[0:16, 2, col:col + n], pt_edge[:, b, 16:32], start=False, stop=True).then_inc(pv_ready, 1)

                for i in range(16):
                    u = i - 4
                    inside = None
                    if u == -1:
                        inside = {4: first_scores}
                    elif u == 0 and l == 0:
                        inside = {2: meta_transposes}
                    elif u > 0:
                        scores(u)
                        inside = {2: lambda: pv(u - 1)}
                        if u >= UNITS - DIFF_HEADS:
                            inside[5] = lambda: head_sums(u - (UNITS - DIFF_HEADS))
                    slot_ready(S("gate") + i)
                    tile(TL("gate") + i, S("gate") + i, 0, P, late, t0, inside=inside)
                    if u >= 0:
                        transposes(u)
                    elif i < 3:
                        v_transposes(i)
                        if i == 2:
                            keys_ready()
                            if l == 0:
                                pe.wait_ge(const_ready, 2)
                                meta_rows()
                K = K0 + NDIFF
                def two_half_tiles(st, src, chunk_ready):
                    slot_ready(S(st))
                    bank_free(TL(st) + 1)
                    for k in range(4):
                        chunk_ready(k)
                        for m in range(2):
                            mm = block(TL(st) + m, S(st), (m * 4 + k) * P, P, *src[k], t0, k == 0, k == 3)
                            if k == 3:
                                mm.then_inc(pe_done, 1)

                src = [(am_hi[:, k, t0:], am_lo[:, k, t0:]) for k in range(4)]
                def heads_ready(k):
                    if k == 1:
                        pv(UNITS - 1)
                    pe.wait_ge(out_copied, UNITS * l + DIFF_HEADS + 2 * (k + 1))

                two_half_tiles("oa", src, heads_ready)
                for m in range(2, KC):
                    if m % 2 == 0:
                        slot_ready(S("oa") + m // 2)
                    tile(TL("oa") + m, S("oa") + m // 2, (m % 2) * 4 * P, P, src, t0)
                    if m == 2:
                        pe.wait_ge(norm_rec, K + 1)
                        for d in range(DIFF_HEADS):
                            spread(K, 4 + d, t0, len(token_chunks(t0)) * d, count=d == DIFF_HEADS - 1)
                src = [(od_hi[:, k, t0:], od_lo[:, k, t0:]) for k in range(4)]
                two_half_tiles("ob", src, lambda k: pe.wait_ge(od_lo_ready, DIFF_HEADS * l + k + 1))
                for m in range(2, KC):
                    if m % 2 == 0:
                        slot_ready(S("ob") + m // 2)
                    tile(TL("ob") + m, S("ob") + m // 2, (m % 2) * 4 * P, P, src, t0)
                first_tiles([(TL("out") + q, S("out") + q, late, t0) for q in range(2)], (mix_hi, mix_lo, KC * l))
                for m in range(2, KC):
                    slot_ready(S("out") + m)
                    tile(TL("out") + m, S("out") + m, 0, P, late, t0)
                post_norm(K0 + POST_MIX)
                g0, gt = S("gu"), TL("gu")
                first_tiles([(gt + q, g0 + q, late, t0) for q in range(BANKS)], (h_hi, h_lo, KC * (2 * l + 1)),
                            {KC - 1: lambda: norm_sums(K0 + PRE_FFN, 7, t0)}, lambda: norm_spread(K0 + PRE_FFN, 7, t0))
                with pe.Fori(0, 5) as i:
                    for j in range(4, 4 + RING):
                        slot_ready(g0 + j, i)
                        tile(gt + j, g0 + j, 0, P, late, t0, i=i, per=RING)
                d0, dt = S("down"), TL("down")
                for m in range(KC):
                    t = dt + m
                    bank_free(t)
                    k = 0
                    for j, cnt in enumerate(DOWN_SPLIT):
                        n = d0 + 4 * m + j
                        slot_ready(n)
                        for q in range(cnt):
                            if m == 0:
                                pe.wait_ge(ff_lo_ready, FC * l + k + 1)
                            mm = block(t, n, q * P, P, ff_hi[:, k, t0:], ff_lo[:, k, t0:], t0, k == 0, k == FC - 1)
                            k += 1
                        mm.then_inc(pe_done, 1)
                if l < DEPTH - 1:
                    post_norm(K0 + POST_FFN)
                else:
                    norm_sums(K0 + POST_FFN, 7, t0)
                    norm_spread(K0 + POST_FFN, 7, t0)


def rope_table(rot, rows, period):
    half = rot // 2
    inv = (np.float32(THETA) ** (-np.arange(0, rot, 2, dtype=np.float32) / np.float32(rot))).astype(np.float32)
    ang = (np.arange(TOK, dtype=np.float32)[:, None] * inv[None, :]).astype(np.float32)
    c, s = np.cos(ang).T.astype(np.float32), np.sin(ang).T.astype(np.float32)
    cos, sin = np.ones((P, TOK), np.float32), np.zeros((P, TOK), np.float32)
    for p0 in range(rows, P, period):
        cos[p0:p0 + half], cos[p0 + half:p0 + rot] = c, c
        sin[p0:p0 + half], sin[p0 + half:p0 + rot] = s, -s
    return cos, sin


def constants():
    c = np.zeros((P, C_ALL), np.float32)
    c[:, C_ID:C_ID + P] = np.eye(P)
    c[:, C_MASK:C_MASK + P] = np.where(np.arange(P)[None, :] > np.arange(P)[:, None], MASKED, 0.0)
    m16 = np.where(np.arange(16)[None, :] > np.arange(16)[:, None], MASKED, 0.0)
    for m in range(16):
        c[0:16, C_MASKM + 16 * m:C_MASKM + 16 * m + 16] = m16
    c[:, C_COSD:C_COSD + TOK], c[:, C_SIND:C_SIND + TOK] = rope_table(DIFF_ROPE, 0, DIFF_DH)
    c[:, C_COSM:C_COSM + TOK], c[:, C_SINM:C_SINM + TOK] = rope_table(ROPE, 0, ROPE)
    return c


def pack_weights(w_in, w_uq, w_ukv, w_oa, w_ob, w_out, w_gu, w_down):
    plan = Plan()
    packed = np.zeros((plan.slots, P, SLOT), np.float32)

    def blocks(w, k0, k1, c0, width):
        a = w[k0 * P:k1 * P, c0:c0 + width]
        return a.reshape(k1 - k0, P, width).transpose(1, 0, 2).reshape(P, (k1 - k0) * width)

    def put(n, parts):
        at = 0
        for a in parts:
            packed[n, :, at:at + a.shape[1]] = a
            at += a.shape[1]

    for l in range(DEPTH):
        S = lambda name, i=0: plan.slot[l, name, i]
        for i in range(5):
            put(S("lat") + i, [blocks(w_in[l], 0, KC, i * P, P)])
        put(S("lat") + 5, [blocks(w_in[l], 0, KC, Q_RANK + KV_RANK - NOPE, HW)])
        for st, o in (("dq", O_DQ), ("dk", O_DK), ("dv", O_DV)):
            for i in range(4):
                put(S(st, i), [blocks(w_in[l], 0, KC, o + i * P, P)])
        heads = w_uq[l].reshape(Q_RANK, MLA_HEADS, HW)
        cols = np.concatenate([heads[:, :, NOPE:].reshape(Q_RANK, -1), heads[:, :, :NOPE].reshape(Q_RANK, -1)], axis=1)
        for i in range(3):
            put(S("uq", i), [blocks(cols, 0, QC, j * P, P) for j in (2 * i, 2 * i + 1)])
        for h in range(MLA_HEADS):
            at = (h % 4) * KVC * P
            packed[S("ukv", h // 4), :, at:at + KVC * P] = blocks(w_ukv[l], 0, KVC, h * P, P)
        for i in range(16):
            put(S("gate") + i, [blocks(w_in[l], 0, KC, O_G + i * P, P)])
        for i in range(4):
            put(S("oa") + i, [blocks(w_oa[l], 0, 4, (2 * i + q) * P, P) for q in range(2)])
            put(S("ob") + i, [blocks(w_ob[l], 0, 4, (2 * i + q) * P, P) for q in range(2)])
        for m in range(KC):
            put(S("out") + m, [blocks(w_out[l], 0, KC, m * P, P)])
        for j in range(FC):
            put(S("gu") + 2 * j, [blocks(w_gu[l], 0, KC, j * P, P)])
            put(S("gu") + 2 * j + 1, [blocks(w_gu[l], 0, KC, D_FF + j * P, P)])
        for m in range(KC):
            k = 0
            for j, cnt in enumerate(DOWN_SPLIT):
                put(S("down") + 4 * m + j, [blocks(w_down[l], k, k + cnt, m * P, P)])
                k += cnt
    return packed.reshape(plan.slots * P, SLOT)


def kernel(x, meta_tokens, norm_mix_pre, norm_mix_post, norm_ffn_pre, norm_ffn_post, w_in, mla_q_norm,
           mla_kv_norm, mla_w_uq, mla_w_ukv, w_o_mla, diff_lambda, diff_subln, w_o_diff, w_out, w_gate_up, w_down):
    import concourse.bacc as _bacc
    from concourse.bass_utils import run_bass_kernel_spmd as _run

    A = lambda a: np.asarray(a)
    tokens = np.concatenate([A(meta_tokens), A(x)[0]], axis=0)
    x_t = tokens.T.reshape(KC, P, TOK).transpose(1, 0, 2).reshape(P, KC * TOK)
    cols = [A(g).reshape(DEPTH, -1, P) for g in (norm_mix_pre, norm_mix_post, norm_ffn_pre, norm_ffn_post,
                                                 mla_q_norm, mla_kv_norm, diff_subln)]
    gains = np.concatenate(cols, axis=1).transpose(2, 0, 1).reshape(P, DEPTH * GAINS)
    lam = np.broadcast_to(A(diff_lambda).reshape(1, DEPTH * 4 * DIFF_DH), (P, DEPTH * 4 * DIFF_DH))
    packed = pack_weights(A(w_in), A(mla_w_uq), A(mla_w_ukv), A(w_o_mla), A(w_o_diff), A(w_out), A(w_gate_up), A(w_down))
    arrays = {"x_t": x_t, "weights": packed, "gains": gains, "lam": lam, "consts": constants()}
    arrays = {k: np.ascontiguousarray(v) for k, v in arrays.items()}
    f32 = mybir.dt.float32
    nc = _bacc.Bacc("TRN2", target_bir_lowering=False, num_devices=1)
    ins = [nc.dram_tensor(k, v.shape, f32, kind="ExternalInput").ap() for k, v in arrays.items()]
    out = nc.dram_tensor("out_t", (P, KC * SEQ), f32, kind="ExternalOutput").ap()
    build_trunk(nc, *ins, out)
    r = _run(nc, [arrays], core_ids=[0])
    got = r.results[0]["out_t"]
    return got.reshape(P, KC, SEQ).transpose(2, 1, 0).reshape(1, SEQ, D_MODEL)
```
